# Optimizing a Trainium2 kernel written in Bass

```python
import jax, jax.numpy as jnp
from jax import lax
import numpy as np

D_MODEL = 1024
BATCH = 1
SEQ = 512
DEPTH = 2
DEC_BATCH = 8
DEC_SEQ = 4
PAST_LEN = 1024
PAGE_SIZE = 128

HEAD_DIM = 64
SCALE = HEAD_DIM ** -0.5
ROPE_THETA = 10000.0
EPS = 1e-6
TINY = 1e-30
N_MIXERS = 2
N_A_LAYERS = (DEPTH + 1) // 2
N_B_LAYERS = DEPTH // 2
DIL_PATTERNS = ((128, 1), (512, 4), (2048, 16))
N_GROUPS_A = len(DIL_PATTERNS)
HEADS_A = 8
WIDTH_A = HEADS_A * HEAD_DIM
QKV_A = 3 * N_GROUPS_A * WIDTH_A
IN_A = QKV_A + WIDTH_A
HEADS_B = D_MODEL // HEAD_DIM
KV_HEADS_B = 4
GQA_B = HEADS_B // KV_HEADS_B
WIDTH_B = HEADS_B * HEAD_DIM
KVW_B = KV_HEADS_B * HEAD_DIM
N_KV_B = 6
CMP_LEN = 32
CMP_STRIDE = 16
CMP_RATIO = CMP_LEN // CMP_STRIDE
CMP_HIDDEN = 128
SEL_BLOCK = 64
SEL_TOPN = 16
WIN_B = 512
IN_B = WIDTH_B + N_KV_B * KVW_B + 3 * HEADS_B + WIDTH_B
BAND_QB = 128
SEL_QB = 32

kernel_name = 'hybrid_dilated_nsa_decoder_step'

def rms_norm(x, g):
    xf = x.astype(jnp.float32)
    y = xf * lax.rsqrt(jnp.mean(xf * xf, axis=-1, keepdims=True) + EPS)
    return (y * g.astype(jnp.float32)).astype(x.dtype)

def rope(x, pos):
    half = HEAD_DIM // 2
    inv_freq = ROPE_THETA ** (-jnp.arange(half, dtype=jnp.float32) / half)
    ang = pos.astype(jnp.float32)[:, None] * inv_freq[None, :]
    shape = (pos.shape[0],) + (1,) * (x.ndim - 3) + (half,)
    cos = jnp.cos(ang).reshape(shape)
    sin = jnp.sin(ang).reshape(shape)
    xf = x.astype(jnp.float32)
    x1, x2 = xf[..., :half], xf[..., half:]
    return jnp.concatenate([x1 * cos - x2 * sin, x2 * cos + x1 * sin], axis=-1).astype(x.dtype)

def masked_attend(s, mask, v, eqn):
    s = jnp.where(mask, s, -jnp.inf)
    m = jnp.max(s, axis=-1, keepdims=True)
    m = jnp.where(jnp.isfinite(m), m, 0.0)
    e = jnp.exp(s - m)
    den = jnp.sum(e, axis=-1, keepdims=True)
    p = e / jnp.maximum(den, TINY)
    out = jnp.einsum(eqn, p.astype(v.dtype), v)
    lse = (m + jnp.log(den))[..., 0]
    return out, lse, p

def band_attention(q, k, v, kw):
    N, n, H, Dh = q.shape
    KH = k.shape[2]
    G = H // KH
    qb = min(BAND_QB, n)
    nb = -(-n // qb)
    pad_end = nb * qb - n
    qp = jnp.pad(q, ((0, 0), (0, pad_end), (0, 0), (0, 0))).reshape(N, nb, qb, KH, G, Dh)
    kp = jnp.pad(k, ((0, 0), (kw, pad_end), (0, 0), (0, 0)))
    vp = jnp.pad(v, ((0, 0), (kw, pad_end), (0, 0), (0, 0)))
    qi = jnp.arange(qb)[:, None]
    kj = jnp.arange(qb + kw)[None, :]
    dist = qi + kw - kj
    band = (dist >= 0) & (dist <= kw)

    def one_block(b):
        qblk = lax.dynamic_index_in_dim(qp, b, axis=1, keepdims=False)
        kb = lax.dynamic_slice_in_dim(kp, b * qb, qb + kw, axis=1)
        vb = lax.dynamic_slice_in_dim(vp, b * qb, qb + kw, axis=1)
        s = jnp.einsum('nqkgd,nskd->nkgqs', qblk, kb, preferred_element_type=jnp.float32) * SCALE
        valid = band & (b * qb + kj - kw >= 0)
        o, lse, _ = masked_attend(s, valid, vb, 'nkgqs,nskd->nqkgd')
        return o, lse

    o, lse = lax.map(one_block, jnp.arange(nb))
    o = jnp.moveaxis(o, 0, 1).reshape(N, nb * qb, H, Dh)[:, :n]
    lse = jnp.transpose(lse, (1, 0, 4, 2, 3)).reshape(N, nb * qb, H)[:, :n]
    return o, lse

def fold_residues(t, d):
    B, S, H, Dh = t.shape
    return t.reshape(B, S // d, d, H, Dh).transpose(0, 2, 1, 3, 4).reshape(B * d, S // d, H, Dh)

def unfold_residues(t, B, d):
    n = t.shape[1]
    rest = t.shape[2:]
    t = jnp.moveaxis(t.reshape((B, d, n) + rest), 1, 2)
    return t.reshape((B, n * d) + rest)

def project_a(h, w_in, q_gain, k_gain, pos):
    N, T, _ = h.shape
    u = jnp.einsum('ntd,de->nte', h, w_in)
    qkv = u[..., :QKV_A].reshape(N, T, 3, N_GROUPS_A, HEADS_A, HEAD_DIM)
    z = u[..., QKV_A:]
    q = rope(rms_norm(qkv[:, :, 0], q_gain), pos)
    k = rope(rms_norm(qkv[:, :, 1], k_gain), pos)
    return q, k, qkv[:, :, 2], z

def dilated_output(outs, lses, z, w_out):
    wts = jax.nn.softmax(jnp.stack(lses, 0), axis=0)
    o = jnp.einsum('gnth,gnthd->nthd', wts.astype(outs[0].dtype), jnp.stack(outs, 0))
    N, T = o.shape[:2]
    return jnp.einsum('nte,ed->ntd', o.reshape(N, T, WIDTH_A) * jax.nn.silu(z), w_out)

def layer_a_prompt(x, norm_g, w_in, q_gain, k_gain, w_out):
    B, S, _ = x.shape
    q, k, v, z = project_a(rms_norm(x, norm_g), w_in, q_gain, k_gain, jnp.arange(S))
    outs, lses, states = [], [], []
    for g, (win, dil) in enumerate(DIL_PATTERNS):
        o, lse = band_attention(fold_residues(q[:, :, g], dil), fold_residues(k[:, :, g], dil),
                                fold_residues(v[:, :, g], dil), win // dil)
        outs.append(unfold_residues(o, B, dil))
        lses.append(unfold_residues(lse, B, dil))
        states.append(jnp.stack([k[:, :, g], v[:, :, g]], axis=2)[:, -min(win, S):])
    return x + dilated_output(outs, lses, z, w_out), states

def layer_a_sample(x, bufs, past_len, norm_g, w_in, q_gain, k_gain, w_out):
    N, T, _ = x.shape
    q, k, v, z = project_a(rms_norm(x, norm_g), w_in, q_gain, k_gain, past_len + jnp.arange(T))
    outs, lses, states = [], [], []
    for g, (win, dil) in enumerate(DIL_PATTERNS):
        L = bufs[g].shape[1]
        cat = jnp.concatenate([bufs[g], jnp.stack([k[:, :, g], v[:, :, g]], axis=2)], axis=1)
        idx = L + jnp.arange(T)[:, None] - dil * jnp.arange(win // dil + 1)[None, :]
        idc = jnp.maximum(idx, 0)
        kg = cat[:, :, 0][:, idc]
        vg = cat[:, :, 1][:, idc]
        s = jnp.einsum('nthd,ntkhd->nhtk', q[:, :, g], kg, preferred_element_type=jnp.float32) * SCALE
        o, lse, _ = masked_attend(s, (idx >= 0)[None, None], vg, 'nhtk,ntkhd->nthd')
        outs.append(o)
        lses.append(jnp.transpose(lse, (0, 2, 1)))
        states.append(cat[:, -min(win, L + T):])
    return x + dilated_output(outs, lses, z, w_out), states

def project_b(h, w_in, q_gain, k_gain, pos):
    N, T, _ = h.shape
    u = jnp.einsum('ntd,de->nte', h, w_in)
    q = rms_norm(u[..., :WIDTH_B].reshape(N, T, HEADS_B, HEAD_DIM), q_gain)
    o1 = WIDTH_B + N_KV_B * KVW_B
    kv = u[..., WIDTH_B:o1].reshape(N, T, N_KV_B, KV_HEADS_B, HEAD_DIM)
    gates = jax.nn.sigmoid(u[..., o1:o1 + 3 * HEADS_B].reshape(N, T, 3, HEADS_B))
    z = u[..., o1 + 3 * HEADS_B:]
    q_rot = rope(q, pos)
    k_cmp = rms_norm(kv[:, :, 0], k_gain)
    k_sel = rope(rms_norm(kv[:, :, 2], k_gain), pos)
    k_win = rope(rms_norm(kv[:, :, 4], k_gain), pos)
    rows = jnp.stack([k_cmp, kv[:, :, 1], k_sel, kv[:, :, 3]], axis=2)
    win_rows = jnp.stack([k_win, kv[:, :, 5]], axis=2)
    return q, q_rot, rows, win_rows, gates, z

def compress_rows(x, pe, w1, w2):
    N, Tk = x.shape[:2]
    n_cmp = (Tk - CMP_LEN) // CMP_STRIDE + 1
    n_chunk = n_cmp + CMP_RATIO - 1
    chunks = x[:, :n_chunk * CMP_STRIDE].reshape(N, n_chunk, CMP_STRIDE, KV_HEADS_B, HEAD_DIM)
    w1r = w1.reshape(CMP_RATIO, CMP_STRIDE, HEAD_DIM, CMP_HIDDEN)
    proj = jnp.einsum('ncjkd,rjde->rncke', chunks, w1r)
    hid = jnp.einsum('jd,jde->e', pe, w1)
    for r in range(CMP_RATIO):
        hid = hid + proj[r, :, r:r + n_cmp]
    return jnp.einsum('ncke,ed->nckd', jax.nn.silu(hid), w2)

def nsa_cmp_sel(q_c, q_s, rows, q_pos, k_gain, pe, w1, w2):
    N, Tq = q_c.shape[:2]
    Tk = rows.shape[1]
    k_cmp = rms_norm(compress_rows(rows[:, :, 0], pe[0], w1[0], w2[0]), k_gain)
    v_cmp = compress_rows(rows[:, :, 1], pe[1], w1[1], w2[1])
    n_cmp = k_cmp.shape[1]
    cmp_start = jnp.arange(n_cmp) * CMP_STRIDE
    cmp_end = cmp_start + CMP_LEN - 1
    n_sel = -(-Tk // SEL_BLOCK)
    sel_start = jnp.arange(n_sel) * SEL_BLOCK
    cover = ((cmp_start[:, None] <= sel_start[None, :] + SEL_BLOCK - 1)
             & (cmp_end[:, None] >= sel_start[None, :])).astype(jnp.float32)
    pad_k = n_sel * SEL_BLOCK - Tk

    def blocks_of(t):
        t = jnp.pad(t, ((0, 0), (0, pad_k), (0, 0), (0, 0)))
        return t.reshape(N, n_sel, SEL_BLOCK, KV_HEADS_B, HEAD_DIM).transpose(0, 3, 1, 2, 4)

    k_blk = blocks_of(rows[:, :, 2])
    v_blk = blocks_of(rows[:, :, 3])
    top_n = min(SEL_TOPN, n_sel)
    qch = min(SEL_QB, Tq)
    nq = -(-Tq // qch)
    pad_q = nq * qch - Tq

    def chunks(t):
        t = jnp.pad(t, ((0, 0), (0, pad_q), (0, 0), (0, 0)))
        return t.reshape(N, nq, qch, KV_HEADS_B, GQA_B, HEAD_DIM)

    qc_all = chunks(q_c)
    qs_all = chunks(q_s)
    pos_all = jnp.pad(q_pos, (0, pad_q), mode='edge')
    n_ix = jnp.arange(N)[:, None, None, None]
    h_ix = jnp.arange(KV_HEADS_B)[None, :, None, None]
    blk_ids = jnp.arange(n_sel)
    in_blk = jnp.arange(SEL_BLOCK)

    def one_chunk(i):
        qc = lax.dynamic_index_in_dim(qc_all, i, axis=1, keepdims=False)
        qs = lax.dynamic_index_in_dim(qs_all, i, axis=1, keepdims=False)
        pos = lax.dynamic_slice_in_dim(pos_all, i * qch, qch)
        s = jnp.einsum('nqkgd,nckd->nkgqc', qc, k_cmp, preferred_element_type=jnp.float32) * SCALE
        o_c, _, p_c = masked_attend(s, cmp_end[None, :] <= pos[:, None], v_cmp, 'nkgqc,nckd->nqkgd')
        imp = jnp.einsum('nkgqc,cj->nkqj', p_c, cover)
        cur = (pos // SEL_BLOCK)[:, None]
        forced = (blk_ids == 0) | (blk_ids == cur) | (blk_ids == cur - 1)
        imp = jnp.where(forced, jnp.inf, jnp.where(blk_ids <= cur, imp, -jnp.inf))
        _, sel = lax.top_k(imp, top_n)
        kg = k_blk[n_ix, h_ix, sel]
        vg = v_blk[n_ix, h_ix, sel]
        kpos = sel[..., None] * SEL_BLOCK + in_blk
        s2 = jnp.einsum('nqkgd,nkqtbd->nkgqtb', qs, kg, preferred_element_type=jnp.float32) * SCALE
        s2 = s2.reshape(N, KV_HEADS_B, GQA_B, qch, top_n * SEL_BLOCK)
        m2 = (kpos <= pos[:, None, None]).reshape(N, KV_HEADS_B, 1, qch, top_n * SEL_BLOCK)
        vg = vg.reshape(N, KV_HEADS_B, qch, top_n * SEL_BLOCK, HEAD_DIM)
        o_s, _, _ = masked_attend(s2, m2, vg, 'nkgqs,nkqsd->nqkgd')
        return o_c, o_s

    o_c, o_s = lax.map(one_chunk, jnp.arange(nq))
    o_c = jnp.moveaxis(o_c, 0, 1).reshape(N, nq * qch, HEADS_B, HEAD_DIM)[:, :Tq]
    o_s = jnp.moveaxis(o_s, 0, 1).reshape(N, nq * qch, HEADS_B, HEAD_DIM)[:, :Tq]
    return o_c, o_s

def window_sample(q, rows, buf, win):
    N, T = q.shape[:2]
    L = buf.shape[1]
    cat = jnp.concatenate([buf, rows], axis=1)
    dist = (L + jnp.arange(T))[:, None] - jnp.arange(L + T)[None, :]
    qg = q.reshape(N, T, KV_HEADS_B, GQA_B, HEAD_DIM)
    s = jnp.einsum('ntkgd,nskd->nkgts', qg, cat[:, :, 0], preferred_element_type=jnp.float32) * SCALE
    o, _, _ = masked_attend(s, (dist >= 0) & (dist <= win), cat[:, :, 1], 'nkgts,nskd->ntkgd')
    return o.reshape(N, T, HEADS_B, HEAD_DIM), cat[:, -min(win, L + T):]

def nsa_output(o_c, o_s, o_w, gates, z, w_out):
    o = (gates[:, :, 0, :, None] * o_c + gates[:, :, 1, :, None] * o_s
         + gates[:, :, 2, :, None] * o_w)
    N, T = o.shape[:2]
    return jnp.einsum('nte,ed->ntd', o.reshape(N, T, WIDTH_B) * jax.nn.silu(z), w_out)

def layer_b_prompt(x, norm_g, w_in, q_gain, k_gain, pe, w1, w2, w_out):
    B, S, _ = x.shape
    pos = jnp.arange(S)
    q_c, q_r, rows, wrows, gates, z = project_b(rms_norm(x, norm_g), w_in, q_gain, k_gain, pos)
    o_c, o_s = nsa_cmp_sel(q_c, q_r, rows, pos, k_gain, pe, w1, w2)
    o_w, _ = band_attention(q_r, wrows[:, :, 0], wrows[:, :, 1], WIN_B)
    y = x + nsa_output(o_c, o_s, o_w, gates, z, w_out)
    return y, rows, wrows[:, -min(WIN_B, S):]

def layer_b_sample(x, pool, page_table, buf, norm_g, w_in, q_gain, k_gain, pe, w1, w2, w_out):
    N, T, _ = x.shape
    past_len = page_table.shape[1] * PAGE_SIZE
    pos = past_len + jnp.arange(T)
    q_c, q_r, rows, wrows, gates, z = project_b(rms_norm(x, norm_g), w_in, q_gain, k_gain, pos)
    past = pool[page_table].reshape((N, past_len) + pool.shape[2:])
    full = jnp.concatenate([past, rows], axis=1)
    o_c, o_s = nsa_cmp_sel(q_c, q_r, full, pos, k_gain, pe, w1, w2)
    o_w, new_buf = window_sample(q_r, wrows, buf, WIN_B)
    y = x + nsa_output(o_c, o_s, o_w, gates, z, w_out)
    return y, rows, new_buf

def setup_inputs(seed: int = 0) -> dict:
    key = jax.random.key(seed)
    ks = jax.random.split(key, 24)
    f32 = jnp.float32
    n_pages = PAST_LEN // PAGE_SIZE
    n_used = DEC_BATCH * n_pages
    n_pool = n_used + max(1, n_used // 4)

    def nrm(k, shape, scale=1.0):
        return jax.random.normal(k, shape, f32) * scale

    inp = {}
    inp['x_prompt'] = nrm(ks[0], (BATCH, SEQ, D_MODEL))
    inp['x_sample'] = nrm(ks[1], (DEC_BATCH, DEC_SEQ, D_MODEL))
    for g, (win, _) in enumerate(DIL_PATTERNS):
        inp['cache_dil_' + str(g)] = nrm(ks[2 + g], (N_A_LAYERS, DEC_BATCH, min(win, PAST_LEN), 2, HEADS_A, HEAD_DIM))
    inp['cache_nsa_paged'] = nrm(ks[5], (N_B_LAYERS, n_pool, PAGE_SIZE, 4, KV_HEADS_B, HEAD_DIM))
    inp['cache_nsa_win'] = nrm(ks[6], (N_B_LAYERS, DEC_BATCH, min(WIN_B, PAST_LEN), 2, KV_HEADS_B, HEAD_DIM))
    inp['page_table'] = jax.random.permutation(ks[7], n_pool)[:n_used].reshape(DEC_BATCH, n_pages).astype(jnp.int32)
    inp['a_norm'] = 1.0 + nrm(ks[8], (N_A_LAYERS, D_MODEL), 0.02)
    inp['a_w_in'] = nrm(ks[9], (N_A_LAYERS, D_MODEL, IN_A), D_MODEL ** -0.5)
    inp['a_q_norm'] = 1.0 + nrm(ks[10], (N_A_LAYERS, HEAD_DIM), 0.02)
    inp['a_k_norm'] = 1.0 + nrm(ks[11], (N_A_LAYERS, HEAD_DIM), 0.02)
    inp['a_w_out'] = nrm(ks[12], (N_A_LAYERS, WIDTH_A, D_MODEL), WIDTH_A ** -0.5)
    inp['b_norm'] = 1.0 + nrm(ks[13], (N_B_LAYERS, D_MODEL), 0.02)
    inp['b_w_in'] = nrm(ks[14], (N_B_LAYERS, D_MODEL, IN_B), D_MODEL ** -0.5)
    inp['b_q_norm'] = 1.0 + nrm(ks[15], (N_B_LAYERS, HEAD_DIM), 0.02)
    inp['b_k_norm'] = 1.0 + nrm(ks[16], (N_B_LAYERS, HEAD_DIM), 0.02)
    inp['b_cmp_pe'] = nrm(ks[17], (N_B_LAYERS, 2, CMP_LEN, HEAD_DIM), 0.1)
    inp['b_cmp_w1'] = nrm(ks[18], (N_B_LAYERS, 2, CMP_LEN, HEAD_DIM, CMP_HIDDEN), (CMP_LEN * HEAD_DIM) ** -0.5)
    inp['b_cmp_w2'] = nrm(ks[19], (N_B_LAYERS, 2, CMP_HIDDEN, HEAD_DIM), CMP_HIDDEN ** -0.5)
    inp['b_w_out'] = nrm(ks[20], (N_B_LAYERS, WIDTH_B, D_MODEL), WIDTH_B ** -0.5)
    return inp

def reference(x_prompt, x_sample, cache_dil_0, cache_dil_1, cache_dil_2, cache_nsa_paged, cache_nsa_win,
              page_table, a_norm, a_w_in, a_q_norm, a_k_norm, a_w_out, b_norm, b_w_in, b_q_norm,
              b_k_norm, b_cmp_pe, b_cmp_w1, b_cmp_w2, b_w_out):
    dil_caches = (cache_dil_0, cache_dil_1, cache_dil_2)
    past_len = page_table.shape[1] * PAGE_SIZE
    xp, xs = x_prompt, x_sample
    dil_p = [[] for _ in DIL_PATTERNS]
    dil_s = [[] for _ in DIL_PATTERNS]
    rows_p, rows_s, win_p, win_s = [], [], [], []
    for layer in range(DEPTH):
        j = layer // N_MIXERS
        if layer % N_MIXERS == 0:
            xp, st_p = layer_a_prompt(xp, a_norm[j], a_w_in[j], a_q_norm[j], a_k_norm[j], a_w_out[j])
            xs, st_s = layer_a_sample(xs, [c[j] for c in dil_caches], past_len, a_norm[j], a_w_in[j],
                                      a_q_norm[j], a_k_norm[j], a_w_out[j])
            for g in range(N_GROUPS_A):
                dil_p[g].append(st_p[g])
                dil_s[g].append(st_s[g])
        else:
            xp, rp, wp = layer_b_prompt(xp, b_norm[j], b_w_in[j], b_q_norm[j], b_k_norm[j], b_cmp_pe[j],
                                        b_cmp_w1[j], b_cmp_w2[j], b_w_out[j])
            xs, rs, ws = layer_b_sample(xs, cache_nsa_paged[j], page_table, cache_nsa_win[j], b_norm[j],
                                        b_w_in[j], b_q_norm[j], b_k_norm[j], b_cmp_pe[j], b_cmp_w1[j],
                                        b_cmp_w2[j], b_w_out[j])
            rows_p.append(rp)
            win_p.append(wp)
            rows_s.append(rs)
            win_s.append(ws)
    return (xp, xs,
            jnp.stack(dil_p[0]), jnp.stack(dil_p[1]), jnp.stack(dil_p[2]),
            jnp.stack(rows_p), jnp.stack(win_p),
            jnp.stack(dil_s[0]), jnp.stack(dil_s[1]), jnp.stack(dil_s[2]),
            jnp.stack(rows_s), jnp.stack(win_s))


_drawn_inputs = setup_inputs


def setup_inputs(seed=0):
    import zlib

    import numpy as np

    out = dict(_drawn_inputs(seed))
    spreads = {}
    factors = {'a_norm': 2.979,
     'a_q_norm': 8.0,
     'a_k_norm': 3.877,
     'b_norm': 2.732,
     'b_q_norm': 8.0,
     'b_k_norm': 3.318,
     'b_cmp_pe': 3.858}
    for name, (base, spread) in spreads.items():
        noise = np.random.default_rng([zlib.crc32(name.encode()), seed]).standard_normal(out[name].shape)
        drawn = base * np.exp(spread * noise) if base else spread * noise
        out[name] = __import__('jax').numpy.asarray(drawn.astype(out[name].dtype))
    for name, factor in factors.items():
        out[name] = (out[name] * factor).astype(out[name].dtype)
    return out
```

```python
from contextlib import ExitStack, contextmanager

import numpy as np

import concourse.bass as bass
from concourse import mybir

ALU = mybir.AluOpType
ACT = mybir.ActivationFunctionType
F32 = mybir.dt.float32
I32 = mybir.dt.int32
AX = mybir.AxisListType.X

P = 128
D = 1024
SEQ = 512
NB = 8
NT = 4
NS = NB * NT
TOK = SEQ + NS
TILES = SEQ // P
DH = 64
HALF = DH // 2
SCALE = DH ** -0.5
EPS = 1e-6
KC = D // P
PATTERNS = ((128, 1), (512, 4), (2048, 16))
HA = 8
WA = HA * DH
HB = 16
KVH = 4
GQA = HB // KVH
KVW = KVH * DH
PAST = 1024
PAGE = 128
NPAGES = PAST // PAGE
WIN = 512
CSTRIDE = 16
CLEN = 32
NCMP_P = (SEQ - CLEN) // CSTRIDE + 1
NCMP_S = (PAST + NT - CLEN) // CSTRIDE + 1
SELB = 64
NSEL_S = -(-(PAST + NT) // SELB)
HID = 128
NEG = -1e30
ROPE_SETS = 2 * TILES + 1


def rows_of(t):
    return P if t < TILES else NS


def token_of(g, t, p):
    return TILES * p + t if g else t * P + p


def constants():
    f = np.float32
    parts = {}
    parts["ident"] = np.eye(P, dtype=f)
    inv = (f(10000.0) ** (-np.arange(HALF, dtype=f) / f(HALF))).astype(f)
    pos = np.zeros((P, ROPE_SETS), f)
    for g in range(2):
        for t in range(TILES):
            pos[:, g * TILES + t] = [token_of(g, t, p) for p in range(P)]
    pos[:NS, ROPE_SETS - 1] = [PAST + r % NT for r in range(NS)]
    ang = pos[:, :, None] * inv[None, None, :]
    c, s = np.cos(ang).astype(f), np.sin(ang).astype(f)
    parts["cos"] = np.concatenate([c, c], -1)
    parts["sin"] = np.concatenate([-s, s], -1)
    q, k = np.arange(P)[:, None], np.arange(P)[None, :]
    causal = np.where(k <= q, 0, NEG).astype(f)
    parts["band"] = np.concatenate([np.where(k >= q, 0, NEG).astype(f), causal], 1)
    parts["every4"] = np.where((k <= q) & ((q - k) % 4 == 0), 0, NEG).astype(f)
    parts["causal"] = np.concatenate([np.zeros((P, 3 * P), f), causal], 1)
    end = np.arange(NCMP_P) * CSTRIDE + CLEN - 1
    tok = np.arange(TILES)[None, :] * P + np.arange(P)[:, None]
    parts["cmp_mask"] = np.where(end[None, None, :] <= tok[:, :, None], 0, NEG).astype(f)
    parts["cmp_any"] = (tok >= CLEN - 1).astype(f)
    t = (np.arange(P) % NT)[:, None]
    n2 = (np.arange(P) // 64)[:, None]
    s = (np.arange(WIN) % P * 4 + np.arange(WIN) // P)[None, :]
    parts["win_mask"] = np.where(s >= t, 0, NEG).astype(f)
    new = np.arange(NS)[None, None, :]
    pair = np.arange(NB // 2)[None, :, None]
    parts["new_mask"] = np.where((new // NT == 2 * pair + n2[:, :, None]) & (new % NT <= t[:, :, None]), 0, NEG).astype(f)
    grp = np.arange(P) // 16 * 4 + np.arange(P) % 4
    parts["group_sum"] = (grp[:, None] == grp[None, :]).astype(f)
    c0 = np.arange(NCMP_S)[:, None] * CSTRIDE
    b0 = np.arange(NSEL_S)[None, :] * SELB
    cover = np.zeros((P, NSEL_S), f)
    cover[:NCMP_S] = (c0 <= b0 + SELB - 1) & (c0 + CLEN - 1 >= b0)
    parts["cover"] = cover
    parts["block_id"] = np.broadcast_to(np.arange(1, NSEL_S - 2, dtype=f), (P, NSEL_S - 3))
    parts["half_power"] = np.full((P, 16), -0.5, f)
    t = (np.arange(P) % NT)[:, None]
    n4 = (np.arange(P) // 32)[:, None]
    new = np.arange(NS)[None, :]
    a_mask = np.zeros((P, 2, 3 * P + 3 * NS), f)
    a_mask[:, :, 0:P] = np.where(k >= t, 0, NEG)[:, None]
    a_mask[:, :, 2 * P:3 * P] = np.where(k // 64 == t // 2, 0, NEG)[:, None]
    for b in range(2):
        own = new // NT == 4 * b + n4
        for g in range(3):
            seen = own & ((new % NT == t) if g else (new % NT <= t))
            a_mask[:, b, 3 * P + g * NS:3 * P + (g + 1) * NS] = np.where(seen, 0, NEG)
    parts["a_mask"] = a_mask
    where, at = {}, 0
    flat = []
    for name, a in parts.items():
        a = np.asarray(a, f).reshape(P, -1)
        where[name] = (at, at + a.shape[1])
        at += a.shape[1]
        flat.append(a)
    return np.ascontiguousarray(np.concatenate(flat, 1)), where


LASTING = (["s_const", "s_copy", "s_page_table", "pa_vout", "pb_rows_out", "pb_win_out", "oa_stored", "ob_stored", "s_og"]
           + [f"s_x{t}" for t in range(TILES + 1)] + [f"pa_kout{i}" for i in range(3)])


class Stage:

    def __init__(self, nc, dram, where, ctx):
        self.nc, self.dram, self.where, self.ctx = nc, dram, where, ctx
        self.lasting = {n: ctx.enter_context(nc.semaphore(n)) for n in LASTING}
        self.stage_sems = []
        self.n_vout = 0
        self.outs = []

    def const(self, name):
        a, b = self.where[name]
        return self.consts[:, a:b]

    def lasting_sem(self, name):
        return self.lasting[name]

    def sem(self, name):
        handle = self.nc.alloc_semaphore(name=name)
        self.stage_sems.append(handle)
        return handle

    @contextmanager
    def block(self):
        with self.nc.Block() as block:
            yield block
        self.nc.clear_and_free_semaphores(self.stage_sems)
        self.stage_sems = []
        self.nc.all_engine_barrier()


def permuted(ap, g, t):
    if t == TILES:
        return ap[:, SEQ:TOK]
    return ap[:, t:SEQ:TILES] if g else ap[:, t * P:(t + 1) * P]


def dram_rows(ap, g, t):
    return ap[t:SEQ:TILES] if g else ap[t * P:(t + 1) * P]


def linker(engine, sem):
    count = [0]

    def link(ins):
        count[0] += 1
        ins.then_inc(sem, 1)
        engine.wait_ge(sem, count[0])
    return link



def load_stage(S):
    nc, A = S.nc, S.dram
    S.s_const, S.s_x, S.s_copy = S.lasting_sem("s_const"), [S.lasting_sem(f"s_x{t}") for t in range(TILES + 1)], S.lasting_sem("s_copy")
    S.s_pages = S.lasting_sem("s_page_table")
    S.n_copy = 0
    with nc.Block() as block:
        @block.sync
        def _(sp):
            xp, xs = A["x_prompt"][0], A["x_sample"].rearrange("n t d -> (n t) d")
            for t in range(TILES):
                sp.dma_start(S.x[:, t, :], xp[t * P:(t + 1) * P, :]).then_inc(S.s_x[t], 16)
            sp.dma_start(S.x[0:NS, TILES, :], xs).then_inc(S.s_x[TILES], 16)
            sp.dma_start(S.consts[:, :], A["consts"][:, 0:S.where["a_mask"][0]]).then_inc(S.s_const, 16)
            sp.dma_start(S.page_table[:, :], A["page_table"].rearrange("(o n) p -> o (n p)", o=1)).then_inc(S.s_pages, 16)
            sp.wait_ge(S.s_pages, 16)


def copy_kept(S, engine, which, sequences):
    A = S.dram
    for n in sequences:
        if which == 3:
            cache, out, first, kept = A["cache_nsa_win"], A["new_win_s"], NT, WIN - NT
        else:
            win = PATTERNS[which][0]
            L = min(win, PAST)
            first = max(L + NT - win, 0)
            cache, out, kept = A[f"cache_dil_{which}"], A[f"new_dil_{which}_s"], L - first
        src = cache[0, n, first:first + kept].rearrange("r v h d -> (r v h d)")
        dst = out[0, n, 0:kept].rearrange("r v h d -> (r v h d)")
        engine.dma_start(dst.rearrange("(a b) -> a b", a=64), src.rearrange("(a b) -> a b", a=64)).then_inc(S.s_copy, 16)
        S.n_copy += 16


def norm_stage(S, pfx, x_ready, gain, hT):
    nc = S.nc
    with ExitStack() as ctx:
        def sb(name, shape):
            return ctx.enter_context(nc.sbuf_tensor(pfx + name, shape, F32))
        sq = sb("squares", [P, D])
        ss = sb("square_sum", [P, TILES + 1])
        ms = sb("mean_square", [P, TILES + 1])
        rstd = sb("rstd", [P, TILES + 1])
        xn = sb("x_normed", [P, 2, D])
        gain_rows = sb("gain_rows", [KC, P])
        gain_cols = sb("gain_cols", [P, KC])
        s_gain, s_gt, s_gc = S.sem(pfx + "gain"), S.sem(pfx + "gain_turned"), S.sem(pfx + "gain_cols")
        s_ss, s_ms, s_rstd = S.sem(pfx + "ss"), S.sem(pfx + "ms"), S.sem(pfx + "rstd")
        s_xn, s_tr, s_h = S.sem(pfx + "xn"), S.sem(pfx + "turned"), S.sem(pfx + "h")
        with S.block() as block:
            @block.sync
            def _(sp):
                sp.dma_start(gain_rows[:, :], gain.rearrange("o (k p) -> (o k) p", p=P)).then_inc(s_gain, 16)

            @block.scalar
            def _(act):
                for t in range(TILES + 1):
                    R = rows_of(t)
                    x_ready(act, t)
                    if t:
                        act.wait_ge(s_ss, t)
                    nc.scalar.activation(sq[0:R, :], S.x[0:R, t, :], ACT.Square,
                                         accum_out=ss[0:R, t:t + 1]).then_inc(s_ss, 1)
                for t in range(TILES + 1):
                    R = rows_of(t)
                    if t == 0:
                        act.wait_ge(s_gc, 1)
                    for k in range(KC):
                        if k % 4 == 0:
                            act.wait_ge(s_tr, 2 * t + k // 4 + 1)
                        ins = nc.scalar.activation(hT[:, k, t * P:t * P + R], S.banks[k // 4][:, (k % 4) * P:(k % 4) * P + R],
                                                   ACT.Copy, scale=gain_cols[:, k:k + 1])
                        if k % 4 == 3:
                            ins.then_inc(s_h, 1)

            @block.gpsimd
            def _(pool):
                pool.wait_ge(S.s_const, 16)
                for t in range(TILES + 1):
                    R = rows_of(t)
                    pool.wait_ge(s_ss, t + 1)
                    nc.gpsimd.tensor_scalar(ms[0:R, t:t + 1], ss[0:R, t:t + 1], 1.0 / D, EPS, ALU.mult, ALU.add).then_inc(s_ms, 1)
                    pool.wait_ge(s_ms, t + 1)
                    nc.gpsimd.tensor_tensor(rstd[0:R, t:t + 1], ms[0:R, t:t + 1], S.const("half_power")[0:R, 0:1],
                                            ALU.pow).then_inc(s_rstd, 1)

            @block.vector
            def _(dve):
                dve.wait_ge(s_gt, 1)
                nc.vector.tensor_copy(gain_cols[:, :], S.banks[2][:, 0:KC]).then_inc(s_gc, 1)
                for t in range(TILES + 1):
                    R = rows_of(t)
                    dve.wait_ge(s_rstd, t + 1)
                    x_ready(dve, t)
                    if t >= 2:
                        dve.wait_ge(s_tr, 2 * (t - 1))
                    nc.vector.tensor_scalar(xn[0:R, t % 2, :], S.x[0:R, t, :], rstd[0:R, t:t + 1], None, ALU.mult).then_inc(s_xn, 1)

            @block.tensor
            def _(pe):
                ident = S.const("ident")
                pe.wait_ge(S.s_const, 16)
                pe.wait_ge(s_gain, 16)
                nc.tensor.transpose(S.banks[2][:, 0:KC], gain_rows[:, :], ident[0:KC, 0:KC]).then_inc(s_gt, 1)
                for t in range(TILES + 1):
                    R = rows_of(t)
                    pe.wait_ge(s_xn, t + 1)
                    for k in range(KC):
                        if t and k % 4 == 0:
                            pe.wait_ge(s_h, 2 * (t - 1) + k // 4 + 1)
                        ins = nc.tensor.transpose(S.banks[k // 4][:, (k % 4) * P:(k % 4) * P + R],
                                                  xn[0:R, t % 2, k * P:(k + 1) * P], ident[0:R, 0:R])
                        if k % 4 == 3:
                            ins.then_inc(s_tr, 1)


def rope_tables(S, dve, sem, gains, tabs, spans):
    nc = S.nc
    for i in range(gains.shape[1]):
        for which, name in ((0, "cos"), (1, "sin")):
            src = S.const(name).rearrange("p (s d) -> p s d", d=DH)
            for lo in (0, HALF):
                glo = lo if which == 0 else HALF - lo
                for at, n, to in spans:
                    g = gains[:, i, glo:glo + HALF].unsqueeze(1).broadcast_to((P, n, HALF))
                    nc.vector.tensor_tensor(tabs[:, i, which, to:to + n, lo:lo + HALF], src[:, at:at + n, lo:lo + HALF], g,
                                            ALU.mult).then_inc(sem, 1)


class Unit:
    pass


def project_a_stage(S, hT, QK, V, Z):
    nc, A = S.nc, S.dram
    w = A["a_w_in"][0].rearrange("(k p) e -> p k e", p=P)
    units = []
    n_qk = n_lin = 0
    for c in range(10):
        for t in range(TILES + 1):
            u = Unit()
            u.c, u.t, u.g, u.R, u.v = c, t, (c % 3 if c < 9 else 0), rows_of(t), len(units)
            u.qk = c < 6
            u.i = n_qk if u.qk else n_lin
            if u.qk:
                n_qk += 1
            else:
                n_lin += 1
            units.append(u)
    qk_units = [u for u in units if u.qk]
    with ExitStack() as ctx:
        def sb(name, shape):
            return ctx.enter_context(nc.sbuf_tensor("pa_" + name, shape, F32))
        W = sb("w", [P, 2, KC, WA])
        gains = sb("gains", [P, 2, DH])
        tabs = sb("tables", [P, 2, 2, ROPE_SETS, DH])
        sq = sb("squares", [P, WA])
        ss = sb("square_sum", [P, 2, HA])
        ms = sb("mean_square", [P, HA])
        rstd = sb("rstd", [P, 2, HA])
        normed = sb("normed", [P, 2, WA])
        straight = sb("straight", [P, WA])
        swapped = sb("swapped", [P, 2, WA])
        rot = sb("rotated", [P, 3, WA])
        s_w = [S.sem(f"pa_w{i}") for i in range(2)]
        s_gains, s_tabs = S.sem("pa_gains"), S.sem("pa_tabs")
        s_u, s_lin, s_sq, s_ss, s_ms, s_rstd = (S.sem("pa_" + n) for n in ("u", "lin", "sq", "ss", "ms", "rstd"))
        s_n, s_st, s_sw, s_rot, s_tr, s_ev = (S.sem("pa_" + n) for n in ("n", "st", "sw", "rot", "tr", "ev"))
        s_kout = [S.lasting_sem(f"pa_kout{i}") for i in range(3)]
        S.s_vout = S.lasting_sem("pa_vout")
        n_kout, kout_at = [0, 0, 0], {}
        for u in qk_units:
            if u.c >= 3:
                stored = u.t == TILES or u.g or u.t == TILES - 1
                if stored:
                    n_kout[u.i % 3] += 16
                    kout_at[u.i] = n_kout[u.i % 3]
        U = S.banks[0:3]
        T = S.banks[3:5]

        def dest(u, kv):
            win = PATTERNS[u.g][0]
            if u.t == TILES:
                new = A[f"new_dil_{u.g}_s"]
                return new[0, :, new.shape[2] - NT:, kv].rearrange("n t h d -> n t (h d)")
            out = A[f"new_dil_{u.g}_p"][0, 0, :, kv].rearrange("r h d -> r (h d)")
            return dram_rows(out, u.g, u.t) if u.g else out

        S.n_tabs = 8
        with S.block() as block:
            @block.sync
            def _(sp):
                for i, name in enumerate(("a_q_norm", "a_k_norm")):
                    sp.dma_start(gains[:, i, :], A[name].broadcast_to((P, DH))).then_inc(s_gains, 16)
                for c in range(2):
                    sp.dma_start(W[:, c, :, :], w[:, :, c * WA:(c + 1) * WA]).then_inc(s_w[c], 16)
                for c in range(10):
                    if c + 2 < 10:
                        sp.wait_ge(s_u, 5 * (c + 1))
                        sp.dma_start(W[:, c % 2, :, :], w[:, :, (c + 2) * WA:(c + 3) * WA]).then_inc(s_w[c % 2], 16)
                        copy_kept(S, sp, 1, [c])
                    for u in units[5 * c:5 * c + 5]:
                        if u.i in kout_at and u.qk:
                            sp.wait_ge(s_rot, u.i + 1)
                            sp.dma_start(dest(u, 0), rot[0:u.R, u.i % 3, :]).then_inc(s_kout[u.i % 3], 16)
                        if 6 <= c < 9 and (u.t == TILES or u.g or u.t == TILES - 1):
                            sp.wait_ge(s_lin, u.i + 1)
                            sp.dma_start(dest(u, 1), V[0:u.R, u.g, u.t, :]).then_inc(S.s_vout, 16)
                            S.n_vout += 16
                S.outs += [(s_kout[i], n_kout[i]) for i in range(3)] + [(S.s_vout, S.n_vout)]

            @block.tensor
            def _(pe):
                ident = S.const("ident")

                def turn(u):
                    pe.wait_ge(s_rot, u.i + 1)
                    if u.i >= 2:
                        pe.wait_ge(s_ev, u.i - 1)
                    for j in range(4):
                        ins = nc.tensor.transpose(T[u.i % 2][:, j * P:j * P + u.R], rot[0:u.R, u.i % 3, j * P:(j + 1) * P],
                                                  ident[0:u.R, 0:u.R])
                    ins.then_inc(s_tr, 1)
                for u in units:
                    if u.t == 0:
                        pe.wait_ge(s_w[u.c % 2], 16 * (u.c // 2 + 1))
                    if u.v >= 3:
                        old = units[u.v - 3]
                        pe.wait_ge(s_n if old.qk else s_lin, old.i + 1)
                    for k in range(KC):
                        ins = nc.tensor.matmul(U[u.v % 3][0:u.R, :], permuted(hT[:, k, :], u.g, u.t), W[:, u.c % 2, k, :],
                                               start=(k == 0), stop=(k == KC - 1))
                    ins.then_inc(s_u, 1)
                    if u.v >= 2 and units[u.v - 2].qk:
                        turn(units[u.v - 2])

            @block.scalar
            def _(act):
                def evacuate(u):
                    act.wait_ge(s_tr, u.i + 1)
                    nc.scalar.activation(QK[:, u.c, :, u.t * P:u.t * P + u.R],
                                         T[u.i % 2][:, :].rearrange("p (j r) -> p j r", j=4)[:, :, 0:u.R], ACT.Copy).then_inc(s_ev, 1)
                for u in units:
                    act.wait_ge(s_u, u.v + 1)
                    src = U[u.v % 3][0:u.R, :]
                    if u.qk:
                        if u.i:
                            act.wait_ge(s_ss, u.i)
                        nc.scalar.activation(sq[0:u.R, :], src, ACT.Square).then_inc(s_sq, 1)
                    elif u.c < 9:
                        nc.scalar.activation(V[0:u.R, u.g, u.t, :], src, ACT.Copy).then_inc(s_lin, 1)
                    else:
                        nc.scalar.activation(Z[0:u.R, u.t, :], src, ACT.Silu).then_inc(s_lin, 1)
                    if u.v >= 2 and units[u.v - 2].qk:
                        evacuate(units[u.v - 2])

            @block.gpsimd
            def _(pool):
                for u in qk_units:
                    R, i = u.R, u.i
                    pool.wait_ge(s_ss, i + 1)
                    nc.gpsimd.tensor_scalar(ms[0:R, :], ss[0:R, i % 2, :], 1.0 / DH, EPS, ALU.mult, ALU.add).then_inc(s_ms, 1)
                    pool.wait_ge(s_ms, i + 1)
                    nc.gpsimd.tensor_tensor(rstd[0:R, i % 2, :], ms[0:R, :], S.const("half_power")[0:R, 0:HA], ALU.pow).then_inc(s_rstd, 1)
                    pool.wait_ge(s_n, i + 1)
                    if i == 0:
                        pool.wait_ge(s_tabs, S.n_tabs)
                    if i >= 2:
                        pool.wait_ge(s_rot, i - 1)
                    n3 = normed[0:R, i % 2, :].rearrange("p (h d) -> p h d", d=DH)
                    o3 = swapped[0:R, i % 2, :].rearrange("p (h d) -> p h d", d=DH)
                    for lo in (0, HALF):
                        tab = rope_tab(tabs, u.c // 3, 1, u)[0:R, lo:lo + HALF].unsqueeze(1).broadcast_to((R, HA, HALF))
                        nc.gpsimd.tensor_tensor(o3[:, :, lo:lo + HALF], n3[:, :, HALF - lo:DH - lo], tab, ALU.mult).then_inc(s_sw, 1)

            @block.vector
            def _(dve):
                dve.wait_ge(S.s_const, 16)
                dve.wait_ge(s_gains, 32)
                rope_tables(S, dve, s_tabs, gains, tabs, [(0, ROPE_SETS, 0)])

                def first(u):
                    R, i = u.R, u.i
                    dve.wait_ge(s_sq, i + 1)
                    nc.vector.tensor_reduce(ss[0:R, i % 2, :], sq[0:R, :].rearrange("p (h d) -> p h d", d=DH), AX,
                                            ALU.add).then_inc(s_ss, 1)

                def second(u):
                    R, i = u.R, u.i
                    dve.wait_ge(s_rstd, i + 1)
                    n3 = normed[0:R, i % 2, :].rearrange("p (h d) -> p h d", d=DH)
                    dve.wait_ge(s_u, u.v + 1)
                    nc.vector.tensor_tensor(n3, U[u.v % 3][0:R, :].rearrange("p (h d) -> p h d", d=DH),
                                            rstd[0:R, i % 2, :].unsqueeze(2).broadcast_to((R, HA, DH)), ALU.mult).then_inc(s_n, 1)
                    dve.wait_ge(s_n, i + 1)
                    tab = rope_tab(tabs, u.c // 3, 0, u)[0:R, :].unsqueeze(1).broadcast_to((R, HA, DH))
                    nc.vector.tensor_tensor(straight[0:R, :].rearrange("p (h d) -> p h d", d=DH), n3, tab, ALU.mult).then_inc(s_st, 1)
                    dve.wait_ge(s_st, i + 1)
                    dve.wait_ge(s_sw, 2 * (i + 1))
                    if i >= 3:
                        dve.wait_ge(s_tr, i - 2)
                        if i - 3 in kout_at:
                            dve.wait_ge(s_kout[i % 3], kout_at[i - 3])
                    nc.vector.tensor_tensor(rot[0:R, i % 3, :], straight[0:R, :], swapped[0:R, i % 2, :], ALU.add).then_inc(s_rot, 1)
                dve.wait_ge(s_tabs, S.n_tabs)
                for i, u in enumerate(qk_units):
                    first(u)
                    if i:
                        second(qk_units[i - 1])
                second(qk_units[-1])


def rope_tab(tabs, which, part, u):
    s = ROPE_SETS - 1 if u.t == TILES else (TILES if u.g else 0) + u.t
    return tabs[:, which, part, s, :]


def attend_stage(S, pfx, groups, finish, sync_program=None, loaded=None):
    nc = S.nc
    units = [u for gr in groups for u in gr.units]
    for v, u in enumerate(units):
        u.v = v
        u.gi = v // 8
    N = len(units)
    with ExitStack() as ctx:
        def sb(name, shape):
            return ctx.enter_context(nc.sbuf_tensor(pfx + name, shape, F32))
        masked = sb("masked", [P, 2, SEQ])
        probs = sb("probs", [P, 2, SEQ])
        pT = sb("probs_turned", [P, 2, 4, P])
        s_sc, s_m, s_e, s_tr, s_pv = (S.sem(pfx + n) for n in ("scores", "masked", "exp", "turned", "pv"))
        s_ev = [S.sem(pfx + "copied_by_vector"), S.sem(pfx + "copied_by_scalar")]
        s_fin, s_link = S.sem(pfx + "finished"), S.sem(pfx + "link")
        SC, TR, OB = S.banks[0:3], S.banks[3:5], S.banks[5:7]

        def copied(engine, v):
            engine.wait_ge(s_ev[v % 2], v // 2 + 1)

        def copy_out(engine, v):
            u = units[v]
            engine.wait_ge(s_tr, v + 1)
            if v >= 2:
                engine.wait_ge(s_pv, v - 1)
            n = len(u.vs)
            rows = u.vs[0].shape[0]
            src = TR[v % 2][0:rows, 0:n * P].rearrange("p (c q) -> p c q", q=P)
            if v % 2 == 0:
                nc.vector.tensor_copy(pT[0:rows, v % 2, 0:n, :], src).then_inc(s_ev[0], 1)
            else:
                nc.scalar.activation(pT[0:rows, v % 2, 0:n, :], src, ACT.Copy).then_inc(s_ev[1], 1)

        with S.block() as block:
            if sync_program:
                @block.sync
                def _(sp):
                    sync_program(sp, s_fin)

            @block.tensor
            def _(pe):
                ident = S.const("ident")
                if loaded:
                    loaded(pe)

                def scores(v):
                    u = units[v]
                    if v >= 3:
                        pe.wait_ge(s_m, v - 2)
                    nc.tensor.matmul(SC[v % 3][:, 0:u.N], u.q, u.k, start=True, stop=True).then_inc(s_sc, 1)

                def turn(v):
                    u = units[v]
                    pe.wait_ge(s_e, v + 1)
                    if v >= 2:
                        copied(pe, v - 2)
                    for c, val in enumerate(u.vs):
                        rows = val.shape[0]
                        ins = nc.tensor.transpose(TR[v % 2][0:rows, c * P:(c + 1) * P], probs[:, v % 2, c * P:c * P + rows], ident)
                    ins.then_inc(s_tr, 1)

                def values(v):
                    u = units[v]
                    copied(pe, v)
                    if v % 8 == 0 and u.gi >= 2:
                        pe.wait_ge(s_fin, u.gi - 1)
                    h = v % 8
                    for c, val in enumerate(u.vs):
                        rows = val.shape[0]
                        ins = nc.tensor.matmul(OB[u.gi % 2][:, h * DH:(h + 1) * DH], pT[0:rows, v % 2, c, :], val,
                                               start=(c == 0), stop=(c == len(u.vs) - 1))
                    ins.then_inc(s_pv, 1)
                for v in range(N + 3):
                    if v < N:
                        scores(v)
                    if 2 <= v < N + 2:
                        turn(v - 2)
                    if v >= 3:
                        values(v - 3)

            @block.scalar
            def _(act):
                for v in range(N + 2):
                    if v < N:
                        u = units[v]
                        act.wait_ge(s_m, v + 1)
                        if v >= 2:
                            act.wait_ge(s_tr, v - 1)
                        nc.scalar.activation(probs[:, v % 2, 0:u.N], masked[:, v % 2, 0:u.N], ACT.Exp, bias=u.low,
                                             scale=-1.0, accum_out=u.den).then_inc(s_e, 1)
                    if v >= 2 and (v - 2) % 2 == 1:
                        copy_out(act, v - 2)

            @block.vector
            def _(dve):
                link = linker(dve, s_link)
                for v in range(N + 12):
                    if v < N:
                        u = units[v]
                        dve.wait_ge(s_sc, v + 1)
                        if v >= 2:
                            dve.wait_ge(s_e, v - 1)
                        nc.vector.tensor_tensor_reduce(masked[:, v % 2, 0:u.N], SC[v % 3][:, 0:u.N], u.mask, -SCALE, 3e38,
                                                       ALU.add, ALU.min, u.low).then_inc(s_m, 1)
                    if 2 <= v < N + 2 and (v - 2) % 2 == 0:
                        copy_out(dve, v - 2)
                    if v >= 11 and (v - 11) % 8 == 0:
                        gi = (v - 11) // 8
                        if gi < len(groups):
                            if gi:
                                dve.wait_ge(s_fin, gi)
                            dve.wait_ge(s_pv, 8 * gi + 8)
                            finish(dve, gi, groups[gi], OB[gi % 2], link).then_inc(s_fin, 1)


def attend_a_stage(S, QK, V, OG):
    nc = S.nc
    groups = []
    with ExitStack() as ctx:
        stats = ctx.enter_context(nc.sbuf_tensor("aa_stats", [P, 3 * TILES, 2, HA], F32))
        out = ctx.enter_context(nc.sbuf_tensor("aa_out", [P, 2, WA + 2 * HA], F32))
        for g in (1, 2, 0):
            for t in range(TILES):
                gr = Unit()
                gr.g, gr.t, gr.units = g, t, []
                for h in range(HA):
                    u = Unit()
                    half, j = h % 2, h // 2
                    part = slice(half * DH, half * DH + DH)
                    keys = (max(t - 1, 0), t + 1) if g == 0 else (t, t + 1)
                    u.q = QK[part, g, j, t * P:(t + 1) * P]
                    u.k = QK[part, 3 + g, j, keys[0] * P:keys[1] * P]
                    u.N = (keys[1] - keys[0]) * P
                    band = S.const("band")
                    u.mask = {0: band if t else band[:, P:], 1: band[:, P:], 2: S.const("every4")}[g]
                    u.vs = [V[:, g, kt, h * DH:(h + 1) * DH] for kt in range(*keys)]
                    u.low = stats[:, len(groups), 0, h:h + 1]
                    u.den = stats[:, len(groups), 1, h:h + 1]
                    gr.units.append(u)
                groups.append(gr)
        s_out = [S.sem("aa_out0"), S.sem("aa_out1")]
        s_back = S.s_og
        scratch = S.dram["scratch_a"]

        def finish(dve, gi, gr, bank, link):
            if gr.g:
                if gi >= 2:
                    dve.wait_ge(s_out[gi % 2], 16 * (gi // 2))
                dst = out[:, gi % 2, :]
            else:
                dst = OG[:, gr.t, 0, :]
            nc.vector.tensor_copy(dst[:, 0:WA], bank[:, :])
            return nc.vector.tensor_copy(dst[:, WA:].rearrange("p (s h) -> p s h", s=2), stats[:, gi, :, :])

        def moves(sp, s_fin):
            for gi, gr in enumerate(groups[:8]):
                sp.wait_ge(s_fin, gi + 1)
                sp.dma_start(dram_rows(scratch[gr.g - 1], gr.g, gr.t), out[:, gi % 2, :]).then_inc(s_out[gi % 2], 16)
            sp.wait_ge(s_out[0], 64)
            sp.wait_ge(s_out[1], 64)
            for t in range(TILES):
                sp.dma_start(OG[:, t, 1:3, :], scratch[:, t * P:(t + 1) * P, :].rearrange("g p c -> p g c")).then_inc(s_back, 16)

        attend_stage(S, "aa_", groups, finish, moves)


def merge_a_stage(S, OG, QK, V, Z, T, oT):
    nc = S.nc
    with ExitStack() as ctx:
        def sb(name, shape):
            return ctx.enter_context(nc.sbuf_tensor("ma_" + name, shape, F32))
        low = sb("low", [P, TILES, HA])
        diff = sb("diff", [P, TILES, 3, HA])
        wt = sb("weight", [P, TILES, 3, HA])
        wd = sb("weighted", [P, TILES, 3, HA])
        den = sb("den", [P, TILES, HA])
        rec = sb("rec", [P, TILES, HA])
        norm = sb("norm", [P, TILES, 3, HA])
        part = sb("part", [P, 3, WA])
        o = sb("o", [P, 2, WA])
        s_diff, s_wt, s_o, s_tr, s_ev, s_link = (S.sem("ma_" + n) for n in ("diff", "wt", "o", "tr", "ev", "link"))
        s_kept = S.sem("ma_kept")
        with S.block() as block:
            @block.gpsimd
            def _(pool):
                nc.gpsimd.tensor_copy(T.q[:, :, :, :], QK[:, 0:3, :, SEQ:TOK]).then_inc(s_kept, 1)
                nc.gpsimd.tensor_copy(T.k[:, :, :, :], QK[:, 3:6, :, SEQ:TOK]).then_inc(s_kept, 1)
                nc.gpsimd.tensor_copy(T.v[:, :, :], V[0:NS, :, TILES, :]).then_inc(s_kept, 1)
                nc.gpsimd.tensor_copy(T.z[:, :], Z[0:NS, TILES, :]).then_inc(s_kept, 1)
                pool.wait_ge(s_kept, 4)

            @block.vector
            def _(dve):
                link = linker(dve, s_link)
                dve.wait_ge(S.s_og, 16 * TILES)
                stat = OG[:, :, :, WA:]
                lows = [stat[:, :, g, 0:HA] for g in range(3)]
                link(nc.vector.tensor_tensor(low[:, :, :], lows[0], lows[1], ALU.min))
                link(nc.vector.tensor_tensor(low[:, :, :], low[:, :, :], lows[2], ALU.min))
                for g in range(3):
                    nc.vector.tensor_tensor(diff[:, :, g, :], low[:, :, :], lows[g], ALU.subtract).then_inc(s_diff, 1)
                dve.wait_ge(s_wt, 1)
                for g in range(3):
                    link(nc.vector.tensor_tensor(wd[:, :, g, :], wt[:, :, g, :], stat[:, :, g, HA:], ALU.mult))
                link(nc.vector.tensor_tensor(den[:, :, :], wd[:, :, 0, :], wd[:, :, 1, :], ALU.add))
                link(nc.vector.tensor_tensor(den[:, :, :], den[:, :, :], wd[:, :, 2, :], ALU.add))
                link(nc.vector.reciprocal(rec[:, :, :], den[:, :, :]))
                for g in range(3):
                    link(nc.vector.tensor_tensor(norm[:, :, g, :], wt[:, :, g, :], rec[:, :, :], ALU.mult))
                for t in range(TILES):
                    if t:
                        dve.wait_ge(s_o, t)
                    for g in range(3):
                        link(nc.vector.tensor_tensor(part[:, g, :].rearrange("p (h d) -> p h d", d=DH),
                                                     OG[:, t, g, 0:WA].rearrange("p (h d) -> p h d", d=DH),
                                                     norm[:, t, g, :].unsqueeze(2).broadcast_to((P, HA, DH)), ALU.mult))
                    link(nc.vector.tensor_tensor(part[:, 0, :], part[:, 0, :], part[:, 1, :], ALU.add))
                    link(nc.vector.tensor_tensor(part[:, 0, :], part[:, 0, :], part[:, 2, :], ALU.add))
                    if t >= 2:
                        dve.wait_ge(s_tr, t - 1)
                    nc.vector.tensor_tensor(o[:, t % 2, :], part[:, 0, :], Z[:, t, :], ALU.mult).then_inc(s_o, 1)

            @block.scalar
            def _(act):
                act.wait_ge(s_diff, 3)
                nc.scalar.activation(wt[:, :, :, :], diff[:, :, :, :], ACT.Exp).then_inc(s_wt, 1)
                for t in range(TILES):
                    act.wait_ge(s_tr, t + 1)
                    nc.scalar.activation(oT[:, 0:4, t * P:(t + 1) * P], S.banks[t % 2][:, :].rearrange("p (j r) -> p j r", j=4),
                                         ACT.Copy).then_inc(s_ev, 1)

            @block.tensor
            def _(pe):
                for t in range(TILES):
                    pe.wait_ge(s_o, t + 1)
                    if t >= 2:
                        pe.wait_ge(s_ev, t - 1)
                    for j in range(4):
                        ins = nc.tensor.transpose(S.banks[t % 2][:, j * P:(j + 1) * P], o[:, t % 2, j * P:(j + 1) * P], S.const("ident"))
                    ins.then_inc(s_tr, 1)


KTILES_A = 7


def sample_a_stage(S, T, oT):
    nc, A = S.nc, S.dram
    NK = KTILES_A * NB
    SLOTS = 3
    BLOCK = 4 * NB * 32
    COLS = 3 * P + 3 * NS
    with ExitStack() as ctx:
        def sb(name, shape):
            return ctx.enter_context(nc.sbuf_tensor("sa_" + name, shape, F32))
        ring = sb("cache", [P, SLOTS, KTILES_A, WA])
        qz = sb("q_padded", [P, 9 * BLOCK + 32])
        kT = sb("keys_turned", [P, 2, 4, P])
        masked = sb("masked", [P, COLS])
        probs = sb("probs", [P, 2, COLS])
        low, den, rec = (sb(n, [P, 2]) for n in ("low", "den", "rec"))
        pz = sb("p_padded", [P, 2, 7, P])
        pTn = sb("p_new_turned", [NS, 2, 3, P])
        out = sb("out", [P, WA])
        mask = sb("mask", [P, 2, COLS])
        zT = sb("z_t", [P, 4, NS])
        s_ring = [[S.sem(f"sa_ring{i}_{m}") for m in range(3)] for i in range(SLOTS)]
        s_mask = S.sem("sa_mask")
        s_zero, s_pzero, s_q, s_turn, s_mul, s_sc = (S.sem("sa_" + n) for n in ("zero", "pzero", "q", "turn", "mul", "scores_done"))
        s_ev = [S.sem("sa_ev0"), S.sem("sa_ev1")]
        s_low, s_exp, s_pt, s_ptc = (S.sem("sa_" + n) for n in ("low", "exp", "pt", "ptc"))
        s_pv, s_out, s_ot, s_o, s_zt, s_ztc = (S.sem("sa_" + n) for n in ("pv", "out", "out_turned", "o", "zt", "ztc"))
        B = S.banks

        def load(sp, m):
            kv, n = divmod(m, NB)
            slot = ring[:, m % SLOTS, :, :]
            sems = s_ring[m % SLOTS]
            c0, c1, c2 = (A[f"cache_dil_{g}"][0, n, :, kv].rearrange("r h d -> r (h d)") for g in range(3))
            sp.dma_start(slot[:, 0, :], c0).then_inc(sems[0], 16)
            sp.dma_start(slot[:, 1:1 + NT, :], c1.rearrange("(p t) e -> p t e", t=NT)).then_inc(sems[1], 16)
            c2 = c2.rearrange("(p c) e -> p c e", c=16)
            for half in range(2):
                sp.dma_start(slot[64 * half:64 * half + 64, 1 + NT:, :], c2[:, 2 * half:2 * half + 2, :]).then_inc(sems[2], 16)

        def landed(engine, m):
            for i, k in enumerate((1, 1, 2)):
                engine.wait_ge(s_ring[m % SLOTS][i], 16 * k * (m // SLOTS + 1))

        def variant(kk):
            return (0, 0) if kk == 0 else (2 + kk, 1) if kk <= NT else (2 + kk, 2)

        def queries(block, j, n):
            at = block * BLOCK + j * NB * 32 + n * 32
            return qz[:, at:at + 32]

        def pad_view(block, e):
            step = NB * 32 + 8
            v = qz[e * DH:(e + 1) * DH, block * BLOCK:block * BLOCK + 4 * step].rearrange("p (j s) -> p j s", s=step)
            return v[:, :, 0:NB * 32].rearrange("p j (n c) -> p j n c", c=32)[:, :, :, e * NT:(e + 1) * NT]

        def quad(n):
            return slice(32 * (n % 4), 32 * (n % 4) + 32)

        with S.block() as block:
            @block.sync
            def _(sp):
                for m in range(2 * NB):
                    if m >= SLOTS:
                        old = m - SLOTS
                        if old < NB:
                            sp.wait_ge(s_turn, KTILES_A * (old + 1))
                        else:
                            sp.wait_ge(s_pv, KTILES_A * (old + 1 - NB))
                    load(sp, m)
                    if m == 0:
                        a, b = S.where["a_mask"]
                        sp.dma_start(mask[:, :, :].rearrange("p b c -> p (b c)"), A["consts"][:, a:b]).then_inc(s_mask, 16)

            @block.gpsimd
            def _(pool):
                half = 9 * BLOCK // 2
                nc.gpsimd.memset(qz[:, 0:half], 0.0).then_inc(s_zero, 1)
                nc.gpsimd.memset(pz[:, :, :, :], 0.0).then_inc(s_pzero, 1)

            @block.tensor
            def _(pe):
                ident = S.const("ident")
                for j in range(4):
                    ins = nc.tensor.transpose(B[5][:, j * NS:(j + 1) * NS], T.z[:, j * P:(j + 1) * P], ident[0:NS, 0:NS])
                ins.then_inc(s_zt, 1)

                def turn(i):
                    n, kk = divmod(i, KTILES_A)
                    if kk == 0:
                        landed(pe, n)
                    if i >= 2:
                        pe.wait_ge(s_ev[i % 2], i // 2)
                    for j in range(4):
                        ins = nc.tensor.transpose(B[2 + i % 2][:, j * P:(j + 1) * P], ring[:, n % SLOTS, kk, j * P:(j + 1) * P], ident)
                    ins.then_inc(s_turn, 1)

                def multiply(i):
                    n, kk = divmod(i, KTILES_A)
                    q_block, g = variant(kk)
                    pe.wait_ge(s_ev[i % 2], i // 2 + 1)
                    for j in range(4):
                        ins = nc.tensor.matmul(B[n // 4][quad(n), g * P:(g + 1) * P], queries(q_block, j, n), kT[:, i % 2, j, :],
                                               start=(kk in (0, 1, 1 + NT) and j == 0), stop=(kk in (0, NT, NT + 2) and j == 3),
                                               skip_group_check=True)
                    ins.then_inc(s_mul, 1)

                def new_scores(b):
                    for n in range(4 * b, 4 * b + 4):
                        for g in range(3):
                            for j in range(4):
                                ins = nc.tensor.matmul(B[b][quad(n), 3 * P + g * NS:3 * P + (g + 1) * NS], queries(g, j, n),
                                                       T.k[:, g, j, :], start=(j == 0), stop=(j == 3), skip_group_check=True)
                    ins.then_inc(s_sc, 1)

                def turn_probs(b):
                    pe.wait_ge(s_exp, b + 1)
                    if b:
                        pe.wait_ge(s_ptc, 8)
                    for g in range(3):
                        nc.tensor.transpose(B[4][:, g * P:(g + 1) * P], probs[:, b, g * P:(g + 1) * P], ident)
                    if b == 0:
                        pe.wait_ge(s_ztc, 1)
                    for g in range(3):
                        ins = nc.tensor.transpose(B[5][0:NS, g * P:(g + 1) * P], probs[:, b, 3 * P + g * NS:3 * P + (g + 1) * NS], ident)
                    ins.then_inc(s_pt, 1)

                def values(n):
                    b = n // 4
                    landed(pe, n + NB)
                    for g in range(3):
                        nc.tensor.matmul(B[6 + b][quad(n), :], pTn[:, b, g, quad(n)], T.v[:, g, :], start=(g == 0), stop=False,
                                         skip_group_check=True)
                    for kk in range(KTILES_A):
                        nc.tensor.matmul(B[6 + b][quad(n), :], pz[:, b, kk, quad(n)], ring[:, (n + NB) % SLOTS, kk, :],
                                         start=False, stop=(kk == KTILES_A - 1), skip_group_check=True).then_inc(s_pv, 1)

                def turn_out(b):
                    pe.wait_ge(s_out, b + 1)
                    if b == 0:
                        pe.wait_ge(s_ptc, 16)
                    else:
                        pe.wait_ge(s_o, 8)
                    for j in range(4):
                        ins = nc.tensor.transpose(B[4][:, j * P:(j + 1) * P], out[:, j * P:(j + 1) * P], ident)
                    ins.then_inc(s_ot, 1)
                pe.wait_ge(s_q, 18)
                for i in range(NK + 1):
                    if i < NK:
                        turn(i)
                    if i:
                        multiply(i - 1)
                    if i == NK // 2:
                        new_scores(0)
                    if i == NK // 2 + 6:
                        turn_probs(0)
                new_scores(1)
                pe.wait_ge(s_ptc, 8)
                for n in range(2):
                    values(n)
                turn_probs(1)
                for n in range(2, 4):
                    values(n)
                pe.wait_ge(s_ptc, 16)
                values(4)
                turn_out(0)
                for n in range(5, 8):
                    values(n)
                turn_out(1)

            def evacuate(engine, i):
                engine.wait_ge(s_turn, i + 1)
                if i >= 2:
                    engine.wait_ge(s_mul, i - 1)
                src = B[2 + i % 2][:, :].rearrange("p (j r) -> p j r", j=4)
                if i % 2 == 0:
                    nc.vector.tensor_copy(kT[:, 0, :, :], src).then_inc(s_ev[0], 1)
                else:
                    nc.scalar.activation(kT[:, 1, :, :], src, ACT.Copy).then_inc(s_ev[1], 1)

            @block.scalar
            def _(act):
                act.wait_ge(s_zt, 1)
                nc.scalar.activation(zT[:, :, :], B[5][:, 0:4 * NS].rearrange("p (j r) -> p j r", j=4), ACT.Copy).then_inc(s_ztc, 1)

                def exp(b):
                    act.wait_ge(s_low, b + 1)
                    nc.scalar.activation(probs[:, b, :], masked[:, :], ACT.Exp, bias=low[:, b:b + 1], scale=-1.0,
                                         accum_out=den[:, b:b + 1]).then_inc(s_exp, 1)
                for i in range(1, NK, 2):
                    evacuate(act, i)
                    if i == NK // 2 + 3:
                        exp(0)
                exp(1)

            @block.vector
            def _(dve):
                nc.vector.memset(qz[:, 9 * BLOCK // 2:], 0.0).then_inc(s_zero, 1)
                dve.wait_ge(s_zero, 2)
                for e in range(2):
                    part = slice(e * DH, (e + 1) * DH)
                    src = [T.q[part, g, :, :].rearrange("p j (n t) -> p j n t", t=NT) for g in range(3)]
                    for g in range(3):
                        nc.vector.tensor_copy(pad_view(g, e), src[g]).then_inc(s_q, 1)
                    for t in range(NT):
                        nc.vector.tensor_copy(pad_view(3 + t, e)[:, :, :, t], src[1][:, :, :, t]).then_inc(s_q, 1)
                    for i in range(2):
                        nc.vector.tensor_copy(pad_view(7 + i, e)[:, :, :, i::2], src[2][:, :, :, i::2]).then_inc(s_q, 1)

                def soft(b):
                    dve.wait_ge(s_sc, b + 1)
                    dve.wait_ge(s_mask, 16)
                    if b:
                        dve.wait_ge(s_exp, b)
                    nc.vector.tensor_tensor_reduce(masked[:, :], B[b][:, 0:COLS], mask[:, b, :], -SCALE,
                                                   3e38, ALU.add, ALU.min, low[:, b:b + 1]).then_inc(s_low, 1)

                def copy_probs(b):
                    dve.wait_ge(s_pt, b + 1)
                    if b == 0:
                        dve.wait_ge(s_pzero, 1)
                    src = [B[4][:, g * P:(g + 1) * P].rearrange("p (n t) -> p n t", t=NT) for g in range(3)]
                    dst = [pz[:, b, kk, :].rearrange("p (n t) -> p n t", t=NT) for kk in range(KTILES_A)]
                    nc.vector.tensor_copy(pz[:, b, 0, :], B[4][:, 0:P]).then_inc(s_ptc, 1)
                    for t in range(NT):
                        nc.vector.tensor_copy(dst[1 + t][:, :, t], src[1][:, :, t]).then_inc(s_ptc, 1)
                    for i in range(2):
                        nc.vector.tensor_copy(dst[1 + NT + i][:, :, i::2], src[2][:, :, i::2]).then_inc(s_ptc, 1)
                    nc.vector.tensor_copy(pTn[:, b, :, :], B[5][0:NS, 0:3 * P].rearrange("p (g r) -> p g r", g=3)).then_inc(s_ptc, 1)
                    nc.vector.reciprocal(rec[:, b:b + 1], den[:, b:b + 1])
                for i in range(0, NK, 2):
                    evacuate(dve, i)
                    if i == NK // 2 + 2:
                        soft(0)
                    if i == NK // 2 + 8:
                        copy_probs(0)
                soft(1)
                copy_probs(1)
                for b in range(2):
                    dve.wait_ge(s_pv, KTILES_A * 4 * (b + 1))
                    if b:
                        dve.wait_ge(s_ot, b)
                    dve.wait_ge(s_ptc, 16)
                    nc.vector.tensor_scalar(out[:, :], B[6 + b][:, :], rec[:, b:b + 1], None, ALU.mult).then_inc(s_out, 1)
                    dve.wait_ge(s_ot, b + 1)
                    dve.wait_ge(s_ztc, 1)
                    for j in range(4):
                        for e in range(2):
                            part = slice(e * DH, (e + 1) * DH)
                            h = 2 * j + e
                            src = B[4][part, j * P:(j + 1) * P].rearrange("p (n c) -> p n c", n=4)[:, :, h * NT:(h + 1) * NT]
                            dst = oT[part, j, SEQ + 16 * b:SEQ + 16 * (b + 1)].rearrange("p (n t) -> p n t", t=NT)
                            z = zT[part, j, 16 * b:16 * (b + 1)].rearrange("p (n t) -> p n t", t=NT)
                            nc.vector.tensor_tensor(dst, src, z, ALU.mult).then_inc(s_o, 1)


def output_stage(S, pfx, oT, w_dram, nk, take):
    nc = S.nc
    with ExitStack() as ctx:
        W = ctx.enter_context(nc.sbuf_tensor(pfx + "w_out", [P, nk, D], F32))
        s_w, s_mm, s_y = S.sem(pfx + "w"), S.sem(pfx + "mm"), S.sem(pfx + "y")
        s_st = S.lasting_sem(pfx + "stored")
        with S.block() as block:
            @block.sync
            def _(sp):
                for dst, src in w_dram(W):
                    sp.dma_start(dst, src).then_inc(s_w, 16)
                if S.store_y:
                    for t in range(TILES + 1):
                        sp.wait_ge(s_y, 2 * t + 2)
                        sp.dma_start(S.store_y(t), S.x[0:rows_of(t), t, :]).then_inc(s_st, 16)
                    S.outs.append((s_st, 16 * (TILES + 1)))

            n_w = len(w_dram(W))

            @block.tensor
            def _(pe):
                pe.wait_ge(s_w, 16 * n_w)
                for v in range(2 * (TILES + 1)):
                    t, half = divmod(v, 2)
                    if v >= 4:
                        pe.wait_ge(s_y, v - 3)
                    for k in range(nk):
                        ins = nc.tensor.matmul(S.banks[v % 4][0:rows_of(t), :], oT[:, k, t * P:t * P + rows_of(t)],
                                               W[:, k, half * 512:half * 512 + 512], start=(k == 0), stop=(k == nk - 1))
                    ins.then_inc(s_mm, 1)

            @block.vector
            def _(dve):
                for v in range(2 * (TILES + 1)):
                    t, half = divmod(v, 2)
                    R = rows_of(t)
                    dve.wait_ge(s_mm, v + 1)
                    xs = S.x[0:R, t, half * 512:half * 512 + 512]
                    nc.vector.tensor_tensor(xs, S.banks[v % 4][0:R, :], xs, ALU.add).then_inc(s_y, 1)


def layer_a(S):
    nc, A = S.nc, S.dram
    with ExitStack() as ctx:
        def sb(name, shape, c=ctx):
            return c.enter_context(nc.sbuf_tensor("la_" + name, shape, F32))
        T = Unit()
        T.q = sb("s_q", [P, 3, 4, NS])
        T.z = sb("s_z", [NS, WA])
        hT = sb("hT", [P, KC, TOK])
        oT = hT[:, 0:4, :]
        rest = hT[:, 4:8, :].rearrange("p k r -> p (k r)")
        T.k = rest[:, 0:12 * NS].rearrange("p (g j r) -> p g j r", g=3, j=4)
        T.v = rest[0:NS, 12 * NS:12 * NS + 3 * WA].rearrange("p (g e) -> p g e", g=3)
        with ExitStack() as inner:
            QK = sb("qk", [P, 6, 4, TOK], inner)
            V = sb("v", [P, 3, TILES + 1, WA], inner)
            Z = sb("z", [P, TILES + 1, WA], inner)
            norm_stage(S, "na_", lambda e, t: e.wait_ge(S.s_x[t], 16), A["a_norm"], hT)
            project_a_stage(S, hT, QK, V, Z)
            S.s_og = S.lasting_sem("s_og")
            with nc.sbuf_tensor("la_og", [P, TILES, 3, WA + 2 * HA], F32) as OG:
                attend_a_stage(S, QK, V, OG)
                merge_a_stage(S, OG, QK, V, Z, T, oT)
        sample_a_stage(S, T, oT)
        S.store_y = None
        w = A["a_w_out"][0].rearrange("(k p) e -> p k e", p=P)
        output_stage(S, "oa_", oT, lambda W: [(W[:, :, :], w)], 4, None)


def project_b_stage(S, hT, QP, KT, ROWS, WINR, Z, GATES):
    nc, A = S.nc, S.dram
    w = A["b_w_in"][0].rearrange("(k p) e -> p k e", p=P)
    NG = 3 * HB
    cols = [(0, 512), (512, 512), (1024, 512), (1536, 512), (2048, 512), (2560, NG), (2560 + NG, 512), (3072 + NG, 512)]
    NC = len(cols)
    units = []
    for c in range(NC):
        for t in range(TILES + 1):
            u = Unit()
            u.c, u.t, u.g, u.R, u.v = c, t, 0, rows_of(t), len(units)
            u.q, u.kv = c < 2, 2 <= c < 5
            u.qk = u.q or u.kv
            u.i = u.v if u.qk else u.v - 25
            u.heads = 8 if u.q else 4
            u.ri = u.i if c < 2 else u.i - 5
            units.append(u)
    qk_units = units[:25]
    with ExitStack() as ctx:
        def sb(name, shape):
            return ctx.enter_context(nc.sbuf_tensor("pb_" + name, shape, F32))
        W = sb("w", [P, 2, KC, 512])
        gains = sb("gains", [P, 2, DH])
        tabs = sb("tables", [P, 2, 2, TILES + 1, DH])
        sq = sb("squares", [P, 512])
        ss, rstd = sb("square_sum", [P, 2, 8]), sb("rstd", [P, 2, 8])
        ms = sb("mean_square", [P, 8])
        normed = sb("normed", [P, 2, 512])
        straight = sb("straight", [P, 512])
        swapped = sb("swapped", [P, 512])
        plain = sb("plain", [P, 2, 512])
        rot = sb("rotated", [P, 2, 512])
        s_w = [S.sem(f"pb_w{i}") for i in range(2)]
        s_gains, s_tabs = S.sem("pb_gains"), S.sem("pb_tabs")
        s_u, s_lin, s_sq, s_ss, s_ms, s_rstd = (S.sem("pb_" + n) for n in ("u", "lin", "sq", "ss", "ms", "rstd"))
        s_n, s_st, s_sw, s_pl, s_rot, s_tr, s_ev, s_v = (S.sem("pb_" + n) for n in ("n", "st", "sw", "pl", "rot", "tr", "ev", "v"))
        S.s_rows_out = S.lasting_sem("pb_rows_out")
        s_win_out = S.lasting_sem("pb_win_out")
        U = S.banks[0:3]
        TP, TR = S.banks[3:5], S.banks[5:7]
        with S.block() as block:
            @block.sync
            def _(sp):
                for i, name in enumerate(("b_q_norm", "b_k_norm")):
                    sp.dma_start(gains[:, i, :], A[name].broadcast_to((P, DH))).then_inc(s_gains, 16)
                for c in range(2):
                    sp.dma_start(W[:, c, :, :], w[:, :, cols[c][0]:sum(cols[c])]).then_inc(s_w[c], 16)
                for c in range(NC):
                    if c + 2 < NC:
                        lo, n = cols[c + 2]
                        sp.wait_ge(s_u, 5 * (c + 1))
                        sp.dma_start(W[:, c % 2, :, 0:n], w[:, :, lo:lo + n]).then_inc(s_w[c % 2], 16)
                        copy_kept(S, sp, 3, [c])
                    if c in (3, 4):
                        for t in range(TILES + 1):
                            u = units[5 * c + t]
                            sp.wait_ge(s_rot, u.i + 1)
                            sp.wait_ge(s_v, u.i - 9)
                            if c == 3 and t < TILES:
                                sp.dma_start(A["new_rows_p"][0, 0, t * P:(t + 1) * P].rearrange("r s h d -> r (s h d)"),
                                             ROWS[:, t, :]).then_inc(S.s_rows_out, 16)
                            elif c == 3:
                                sp.dma_start(A["new_rows_s"][0].rearrange("n t s h d -> (n t) (s h d)"),
                                             ROWS[0:NS, t, :]).then_inc(S.s_rows_out, 16)
                            elif t < TILES:
                                sp.dma_start(A["new_win_p"][0, 0, t * P:(t + 1) * P].rearrange("r s h d -> r (s h d)"),
                                             WINR[:, t, :]).then_inc(s_win_out, 16)
                            else:
                                sp.dma_start(A["new_win_s"][0, :, WIN - NT:].rearrange("n t s h d -> n t (s h d)"),
                                             WINR[0:NS, t, :]).then_inc(s_win_out, 16)
                S.outs += [(S.s_rows_out, 80), (s_win_out, 80)]

            @block.tensor
            def _(pe):
                ident = S.const("ident")

                def turn(u):
                    pe.wait_ge(s_rot, u.i + 1)
                    if u.ri >= 2:
                        pe.wait_ge(s_ev, u.ri - 1)
                    if u.q:
                        pe.wait_ge(s_pl, 2 * (u.i + 1))
                        for bank, src in ((TP[u.ri % 2], plain), (TR[u.ri % 2], rot)):
                            for j in range(4):
                                ins = nc.tensor.transpose(bank[:, j * P:j * P + u.R], src[0:u.R, u.i % 2, j * P:(j + 1) * P],
                                                          ident[0:u.R, 0:u.R])
                    else:
                        src = ROWS[0:u.R, u.t, 512:768] if u.c == 3 else WINR[0:u.R, u.t, 0:256]
                        for j in range(2):
                            ins = nc.tensor.transpose(TR[u.ri % 2][:, j * P:j * P + u.R], src[:, j * P:(j + 1) * P],
                                                      ident[0:u.R, 0:u.R])
                    ins.then_inc(s_tr, 1)
                for u in units:
                    n = cols[u.c][1]
                    if u.t == 0:
                        pe.wait_ge(s_w[u.c % 2], 16 * (u.c // 2 + 1))
                    if u.v >= 3:
                        old = units[u.v - 3]
                        pe.wait_ge(s_n if old.qk else s_lin, old.i + 1)
                        if old.kv:
                            pe.wait_ge(s_v, old.i - 9)
                    for k in range(KC):
                        ins = nc.tensor.matmul(U[u.v % 3][0:u.R, 0:n], hT[:, k, u.t * P:u.t * P + u.R], W[:, u.c % 2, k, 0:n],
                                               start=(k == 0), stop=(k == KC - 1))
                    ins.then_inc(s_u, 1)
                    if u.v >= 2 and (units[u.v - 2].q or units[u.v - 2].c in (3, 4)):
                        turn(units[u.v - 2])

            @block.scalar
            def _(act):
                def evacuate(u):
                    act.wait_ge(s_tr, u.ri + 1)
                    tok = slice(u.t * P, u.t * P + u.R)
                    if u.q:
                        for var, bank in enumerate((TP, TR)):
                            ins = nc.scalar.activation(QP[:, var, 4 * u.c:4 * u.c + 4, tok],
                                                       bank[u.ri % 2][:, :].rearrange("p (j r) -> p j r", j=4)[:, :, 0:u.R], ACT.Copy)
                    else:
                        ins = nc.scalar.activation(KT[:, u.c - 3, :, tok],
                                                   TR[u.ri % 2][:, 0:2 * P].rearrange("p (j r) -> p j r", j=2)[:, :, 0:u.R], ACT.Copy)
                    ins.then_inc(s_ev, 1)
                for u in units:
                    act.wait_ge(s_u, u.v + 1)
                    src = U[u.v % 3]
                    n = cols[u.c][1]
                    if u.qk:
                        if u.i:
                            act.wait_ge(s_ss, u.i)
                        w_ = DH * u.heads
                        sq_ins = nc.scalar.activation(sq[0:u.R, 0:w_], src[0:u.R, 0:w_], ACT.Square)
                        if u.kv:
                            dst = {2: ROWS[0:u.R, u.t, 256:512], 3: ROWS[0:u.R, u.t, 768:1024], 4: WINR[0:u.R, u.t, 256:512]}[u.c]
                            nc.scalar.activation(dst, src[0:u.R, 256:512], ACT.Copy).then_inc(s_v, 1)
                        sq_ins.then_inc(s_sq, 1)
                    elif u.c == 5:
                        nc.scalar.activation(GATES[0:u.R, u.t, :], src[0:u.R, 0:n], ACT.Sigmoid).then_inc(s_lin, 1)
                    else:
                        nc.scalar.activation(Z[0:u.R, u.t, (u.c - 6) * 512:(u.c - 5) * 512], src[0:u.R, :], ACT.Silu).then_inc(s_lin, 1)
                    if u.v >= 2 and (units[u.v - 2].q or units[u.v - 2].c in (3, 4)):
                        evacuate(units[u.v - 2])

            @block.gpsimd
            def _(pool):
                for u in qk_units:
                    R, i, H = u.R, u.i, u.heads
                    pool.wait_ge(s_ss, i + 1)
                    if i:
                        pool.wait_ge(s_rstd, i)
                    nc.gpsimd.tensor_scalar(ms[0:R, 0:H], ss[0:R, i % 2, 0:H], 1.0 / DH, EPS, ALU.mult, ALU.add).then_inc(s_ms, 1)
                    pool.wait_ge(s_ms, i + 1)
                    nc.gpsimd.tensor_tensor(rstd[0:R, i % 2, 0:H], ms[0:R, 0:H], S.const("half_power")[0:R, 0:H], ALU.pow).then_inc(s_rstd, 1)
                    if u.c == 2:
                        continue
                    pool.wait_ge(s_n, i + 1)
                    if i == 0:
                        pool.wait_ge(s_tabs, 16)
                    if i:
                        pool.wait_ge(s_rot, i)
                    n3 = normed[0:R, i % 2, 0:DH * H].rearrange("p (h d) -> p h d", d=DH)
                    o3 = swapped[0:R, 0:DH * H].rearrange("p (h d) -> p h d", d=DH)
                    for lo in (0, HALF):
                        tab = tabs[0:R, 1 if u.kv else 0, 1, u.t, lo:lo + HALF].unsqueeze(1).broadcast_to((R, H, HALF))
                        nc.gpsimd.tensor_tensor(o3[:, :, lo:lo + HALF], n3[:, :, HALF - lo:DH - lo], tab, ALU.mult).then_inc(s_sw, 1)
                    if u.q:
                        if i >= 2:
                            pool.wait_ge(s_tr, i - 1)
                        gain = gains[0:R, 0, :].unsqueeze(1).broadcast_to((R, GQA, DH))
                        for k2 in range(2):
                            nc.gpsimd.tensor_tensor(plain[0:R, i % 2, :].rearrange("p (g k d) -> p k g d", g=GQA, d=DH)[:, k2],
                                                    n3[:, 4 * k2:4 * k2 + 4, :], gain, ALU.mult).then_inc(s_pl, 1)

            @block.vector
            def _(dve):
                dve.wait_ge(s_gains, 32)
                rope_tables(S, dve, s_tabs, gains, tabs, [(0, TILES, 0), (ROPE_SETS - 1, 1, TILES)])

                def first(u):
                    R, i, w_ = u.R, u.i, DH * u.heads
                    dve.wait_ge(s_sq, i + 1)
                    nc.vector.tensor_reduce(ss[0:R, i % 2, 0:u.heads], sq[0:R, 0:w_].rearrange("p (h d) -> p h d", d=DH), AX,
                                            ALU.add).then_inc(s_ss, 1)

                def second(u):
                    R, i, H = u.R, u.i, u.heads
                    w_ = DH * H
                    dve.wait_ge(s_rstd, i + 1)
                    n3 = normed[0:R, i % 2, 0:w_].rearrange("p (h d) -> p h d", d=DH)
                    dve.wait_ge(s_u, u.v + 1)
                    if u.kv:
                        dve.wait_ge(s_v, i - 9)
                    nc.vector.tensor_tensor(n3, U[u.v % 3][0:R, 0:w_].rearrange("p (h d) -> p h d", d=DH),
                                            rstd[0:R, i % 2, 0:H].unsqueeze(2).broadcast_to((R, H, DH)), ALU.mult).then_inc(s_n, 1)
                    dve.wait_ge(s_n, i + 1)
                    if u.c == 2:
                        gain = gains[0:R, 1, :].unsqueeze(1).broadcast_to((R, H, DH))
                        nc.vector.tensor_tensor(ROWS[0:R, u.t, 0:256].rearrange("p (h d) -> p h d", d=DH), n3, gain,
                                                ALU.mult).then_inc(s_rot, 1)
                        return
                    tab = tabs[0:R, 1 if u.kv else 0, 0, u.t, :].unsqueeze(1).broadcast_to((R, H, DH))
                    nc.vector.tensor_tensor(straight[0:R, 0:w_].rearrange("p (h d) -> p h d", d=DH), n3, tab, ALU.mult).then_inc(s_st, 1)
                    dve.wait_ge(s_st, u.ri + 1)
                    dve.wait_ge(s_sw, 2 * (u.ri + 1))
                    if u.q:
                        if i >= 2:
                            dve.wait_ge(s_tr, i - 1)
                        out = rot[0:R, i % 2, :].rearrange("p (g k d) -> p k g d", g=GQA, d=DH)
                        a = straight[0:R, :].rearrange("p (k g d) -> p k g d", g=GQA, d=DH)
                        b = swapped[0:R, :].rearrange("p (k g d) -> p k g d", g=GQA, d=DH)
                    else:
                        out = ROWS[0:R, u.t, 512:768] if u.c == 3 else WINR[0:R, u.t, 0:256]
                        a, b = straight[0:R, 0:256], swapped[0:R, 0:256]
                    nc.vector.tensor_tensor(out, a, b, ALU.add).then_inc(s_rot, 1)
                dve.wait_ge(s_tabs, 16)
                for i, u in enumerate(qk_units):
                    first(u)
                    if i:
                        second(qk_units[i - 1])
                second(qk_units[-1])


def compress_stage(S, pfx, items, load, pages_of, KC_T, VC):
    nc, A = S.nc, S.dram
    nI = len(items)
    CH = 16 * max(items)
    with ExitStack() as ctx:
        def sb(name, shape):
            return ctx.enter_context(nc.sbuf_tensor(pfx + name, shape, F32))
        w1 = sb("w1", [P, 2, 2, 8, HID])
        w2 = sb("w2", [HID, 2, DH])
        pe_rows = sb("pe_rows", [2 * CSTRIDE, P])
        peT = sb("peT", [P, 2 * CSTRIDE])
        pe_hid = sb("pe_hidden", [HID, 2])
        gains = sb("gains", [P, 2, DH])
        gain = sb("gain", [P, 1])
        pages = sb("pages", [P, min(2, nI), max(items), 2, 512])
        chunksT = sb("chunks_turned", [P, 2, KVH, 8, CH])
        hid = sb("hidden", [HID, 2, KVH, CH])
        sq = sb("squares", [64, 256])
        ss, ms, rstd = (sb(n, [64, KVH]) for n in ("ss", "ms", "rstd"))
        kn = sb("keys", [64, 256])
        s_w, s_pg = S.sem(pfx + "w"), [S.sem(pfx + "pages0"), S.sem(pfx + "pages1")]
        names = ("tr", "hm", "hid", "w2", "sq", "ss", "ms", "rstd", "kn", "knt", "kc", "vc", "pre", "pe0", "pe1", "pe2", "g")
        m = {n: S.sem(pfx + n) for n in names}
        s_ev = [S.sem(pfx + "copied_by_vector"), S.sem(pfx + "copied_by_scalar")]
        B = S.banks
        tus = [(it, kv, j, a) for it in range(nI) for kv in range(2) for j in range(2) for a in range(2)]
        with S.block() as block:
            @block.sync
            def _(sp):
                for kv in range(2):
                    for a in range(2):
                        src = A["b_cmp_w1"][0, kv].rearrange("(m a) d e -> a d m e", a=2)[a]
                        sp.dma_start(w1[a * DH:(a + 1) * DH, kv, :, :, :].rearrange("p r m e -> p (r m) e"), src).then_inc(s_w, 16)
                sp.dma_start(w2[:, :, :], A["b_cmp_w2"][0].rearrange("v e d -> e v d")).then_inc(s_w, 16)
                sp.dma_start(pe_rows[:, :], A["b_cmp_pe"][0].rearrange("v (m a) d -> (v m) (a d)", a=2)).then_inc(s_w, 16)
                for i in range(2):
                    sp.dma_start(gains[:, i, :], A["b_k_norm"].broadcast_to((P, DH))).then_inc(s_w, 16)
                load(sp, pages, s_pg, m["tr"])

            @block.tensor
            def _(pe):
                ident = S.const("ident")
                pe.wait_ge(s_w, 16 * 8)
                nc.tensor.transpose(B[7][:, 0:32], pe_rows[:, :], ident[0:32, 0:32])
                nc.tensor.transpose(B[7][:, 128:256], gains[:, :, :].rearrange("p a d -> p (a d)"), ident).then_inc(m["pe0"], 1)
                pe.wait_ge(m["pe1"], 2)
                for kv in range(2):
                    for rm in range(16):
                        ins = nc.tensor.matmul(B[7][:, 256 + kv:257 + kv], w1[:, kv, rm // 8, rm % 8, :],
                                               peT[:, 16 * kv + rm:16 * kv + rm + 1], start=(rm == 0), stop=(rm == 15))
                ins.then_inc(m["pe2"], 1)

                def turn(x):
                    it, kv, j, a = tus[x]
                    if kv == 0 and j == 0 and a == 0:
                        pages_of(pe, it, s_pg)
                    if x >= 2:
                        pe.wait_ge(s_ev[x % 2], 2 * (x // 2))
                    for pp in range(items[it]):
                        ins = nc.tensor.transpose(B[x % 2][:, pp * P:(pp + 1) * P], pages[:, it % 2, pp, a, kv * 256 + j * P:kv * 256 + (j + 1) * P],
                                                  ident)
                    ins.then_inc(m["tr"], 1)

                def hidden(y):
                    it, kv = divmod(y, 2)
                    nc_ = 16 * items[it] - 1
                    for e in range(2):
                        pe.wait_ge(s_ev[e], 4 * (y + 1))
                    if y >= 2:
                        pe.wait_ge(m["hid"], y - 1)
                    for rm in range(16):
                        r, mm = divmod(rm, 8)
                        ins = nc.tensor.matmul(B[2 + y % 2][:, 0:KVH * nc_], w1[:, kv, r, mm, :], chunksT[:, y % 2, :, mm, r:r + nc_],
                                               start=(rm == 0), stop=(rm == 15))
                    ins.then_inc(m["hm"], 1)

                def tokens(y):
                    it, kv = divmod(y, 2)
                    nc_ = 16 * items[it] - 1
                    pe.wait_ge(m["hid"], y + 1)
                    if it:
                        pe.wait_ge(m["kn"] if kv == 0 else m["vc"], it)
                    for k in range(KVH):
                        ins = nc.tensor.matmul(B[4 + kv][0:nc_, k * DH:(k + 1) * DH], hid[:, y % 2, k, 0:nc_], w2[:, kv, :],
                                               start=True, stop=True)
                    ins.then_inc(m["w2"], 1)

                def turn_keys(it):
                    nc_ = 16 * items[it] - 1
                    pe.wait_ge(m["kn"], it + 1)
                    if it:
                        pe.wait_ge(m["kc"], it)
                    for j in range(2):
                        ins = nc.tensor.transpose(B[6][:, j * 64:j * 64 + nc_], kn[0:nc_, j * P:(j + 1) * P], ident[0:nc_, 0:nc_])
                    ins.then_inc(m["knt"], 1)
                for y in range(2 * nI + 2):
                    if y < 2 * nI:
                        for x in range(4 * y, 4 * y + 4):
                            turn(x)
                    if 1 <= y < 2 * nI + 1:
                        hidden(y - 1)
                    if y >= 2:
                        tokens(y - 2)
                        if (y - 2) % 2 == 1:
                            turn_keys((y - 2) // 2)

            def copy_out(engine, x):
                it, kv, j, a = tus[x]
                y = 2 * it + kv
                engine.wait_ge(m["tr"], x + 1)
                if y >= 2:
                    engine.wait_ge(m["hm"], y - 1)
                n = 16 * items[it]
                for k2 in range(2):
                    src = B[x % 2][k2 * DH:(k2 + 1) * DH, 0:8 * n].rearrange("p (c m) -> p m c", m=8)
                    dst = chunksT[a * DH:(a + 1) * DH, y % 2, 2 * j + k2, :, 0:n]
                    if x % 2 == 0:
                        nc.vector.tensor_copy(dst, src).then_inc(s_ev[0], 1)
                    else:
                        nc.scalar.activation(dst, src, ACT.Copy).then_inc(s_ev[1], 1)

            @block.scalar
            def _(act):
                act.wait_ge(m["pe0"], 1)

                def silu(y):
                    it, kv = divmod(y, 2)
                    nc_ = 16 * items[it] - 1
                    act.wait_ge(m["hm"], y + 1)
                    if y == 0:
                        act.wait_ge(m["pre"], 1)
                    if y >= 2:
                        act.wait_ge(m["w2"], y - 1)
                    nc.scalar.activation(hid[:, y % 2, :, 0:nc_], B[2 + y % 2][:, 0:KVH * nc_].rearrange("p (k c) -> p k c", k=KVH),
                                         ACT.Silu, bias=pe_hid[:, kv:kv + 1]).then_inc(m["hid"], 1)

                def finish(y):
                    it, kv = divmod(y, 2)
                    nc_ = 16 * items[it] - 1
                    act.wait_ge(m["w2"], y + 1)
                    if kv == 0:
                        if it:
                            act.wait_ge(m["ss"], it)
                        nc.scalar.activation(sq[0:nc_, :], B[4][0:nc_, 0:256], ACT.Square).then_inc(m["sq"], 1)
                    else:
                        nc.scalar.activation(VC[0:nc_, it, :], B[5][0:nc_, 0:256], ACT.Copy).then_inc(m["vc"], 1)
                for y in range(2 * nI + 2):
                    if y < 2 * nI:
                        copy_out(act, 4 * y + 1)
                        copy_out(act, 4 * y + 3)
                    if 1 <= y < 2 * nI + 1:
                        silu(y - 1)
                    if y >= 2:
                        finish(y - 2)

            @block.gpsimd
            def _(pool):
                for it in range(nI):
                    nc_ = 16 * items[it] - 1
                    pool.wait_ge(m["ss"], it + 1)
                    if it:
                        pool.wait_ge(m["kn"], it)
                    nc.gpsimd.tensor_scalar(ms[0:nc_, :], ss[0:nc_, :], 1.0 / DH, EPS, ALU.mult, ALU.add).then_inc(m["ms"], 1)
                    pool.wait_ge(m["ms"], it + 1)
                    nc.gpsimd.tensor_tensor(rstd[0:nc_, :], ms[0:nc_, :], S.const("half_power")[0:nc_, 0:KVH], ALU.pow).then_inc(m["rstd"], 1)

            @block.vector
            def _(dve):
                dve.wait_ge(m["pe0"], 1)
                nc.vector.tensor_copy(peT[:, :], B[7][:, 0:32]).then_inc(m["pe1"], 1)
                nc.vector.tensor_copy(gain[:, :], B[7][:, 128:129]).then_inc(m["pe1"], 1)
                dve.wait_ge(m["pe2"], 1)
                nc.vector.tensor_copy(pe_hid[:, :], B[7][:, 256:258]).then_inc(m["pre"], 1)

                def keys(it):
                    nc_ = 16 * items[it] - 1
                    dve.wait_ge(m["sq"], it + 1)
                    if it:
                        dve.wait_ge(m["rstd"], it)
                    nc.vector.tensor_reduce(ss[0:nc_, :], sq[0:nc_, :].rearrange("p (k d) -> p k d", d=DH), AX, ALU.add).then_inc(m["ss"], 1)
                    dve.wait_ge(m["rstd"], it + 1)
                    if it:
                        dve.wait_ge(m["knt"], it)
                    nc.vector.tensor_tensor(kn[0:nc_, :].rearrange("p (k d) -> p k d", d=DH),
                                            B[4][0:nc_, 0:256].rearrange("p (k d) -> p k d", d=DH),
                                            rstd[0:nc_, :].unsqueeze(2).broadcast_to((nc_, KVH, DH)), ALU.mult).then_inc(m["kn"], 1)

                def keep(it):
                    nc_ = 16 * items[it] - 1
                    dve.wait_ge(m["knt"], it + 1)
                    nc.vector.tensor_scalar(KC_T[:, it, :, 0:nc_], B[6][:, 0:P].rearrange("p (j c) -> p j c", j=2)[:, :, 0:nc_],
                                            gain[:, 0:1], None, ALU.mult).then_inc(m["kc"], 1)
                for y in range(2 * nI + 3):
                    if y < 2 * nI:
                        copy_out(dve, 4 * y)
                        copy_out(dve, 4 * y + 2)
                    if y >= 2 and y % 2 == 0 and (y - 2) // 2 < nI:
                        keys((y - 2) // 2)
                    if y >= 4 and y % 2 == 0:
                        keep((y - 4) // 2)


def attend_b_stage(S, QP, KT, ROWS, WINR, KC_P, VC_P, GATES, OA):
    nc = S.nc
    assert SEQ // SELB <= 16 and SEQ <= WIN
    groups = []
    with ExitStack() as ctx:
        stats = ctx.enter_context(nc.sbuf_tensor("ab_stats", [P, 6 * TILES, 2, 8], F32))
        tmp = ctx.enter_context(nc.sbuf_tensor("ab_tmp", [P, 512], F32))
        rec = ctx.enter_context(nc.sbuf_tensor("ab_rec", [P, 8], F32))
        for t in range(TILES):
            for j in range(2):
                for br in range(3):
                    gr = Unit()
                    gr.t, gr.j, gr.br, gr.units = t, j, br, []
                    for h in range(8):
                        k2, g = divmod(h, GQA)
                        part = slice(k2 * DH, (k2 + 1) * DH)
                        k = 2 * j + k2
                        u = Unit()
                        u.q = QP[part, 1 if br else 0, 4 * j + g, t * P:(t + 1) * P]
                        if br == 0:
                            u.k, u.N = KC_P[part, 0, j, 0:NCMP_P], NCMP_P
                            u.mask = S.const("cmp_mask").rearrange("p (t c) -> p t c", t=TILES)[:, t, :]
                            u.vs = [VC_P[0:NCMP_P, 0, k * DH:(k + 1) * DH]]
                        else:
                            u.N = (t + 1) * P
                            u.k = KT[part, br - 1, j, 0:u.N]
                            u.mask = S.const("causal")[:, (TILES - 1 - t) * P:]
                            src, at = (ROWS, 768) if br == 1 else (WINR, 256)
                            u.vs = [src[:, kt, at + k * DH:at + (k + 1) * DH] for kt in range(t + 1)]
                        u.low = stats[:, len(groups), 0, h:h + 1]
                        u.den = stats[:, len(groups), 1, h:h + 1]
                        gr.units.append(u)
                    groups.append(gr)

        def finish(dve, gi, gr, bank, link):
            link(nc.vector.reciprocal(rec[:, :], stats[:, gi, 1, :]))
            gate = GATES[:, gr.t, gr.br * HB + 8 * gr.j:gr.br * HB + 8 * gr.j + 8]
            if gr.br == 0:
                link(nc.vector.scalar_tensor_tensor(out=rec[:, :], in0=rec[:, :], scalar=S.const("cmp_any")[:, gr.t:gr.t + 1],
                                                    in1=gate, op0=ALU.mult, op1=ALU.mult))
            else:
                link(nc.vector.tensor_tensor(rec[:, :], rec[:, :], gate, ALU.mult))
            src = bank[:, :].rearrange("p (h d) -> p h d", d=DH)
            wt = rec[:, :].unsqueeze(2).broadcast_to((P, 8, DH))
            out = OA[:, gr.t, gr.j * 512:(gr.j + 1) * 512]
            if gr.br == 0:
                return nc.vector.tensor_tensor(out.rearrange("p (h d) -> p h d", d=DH), src, wt, ALU.mult)
            link(nc.vector.tensor_tensor(tmp[:, :].rearrange("p (h d) -> p h d", d=DH), src, wt, ALU.mult))
            return nc.vector.tensor_tensor(out, out, tmp[:, :], ALU.add)

        def copies(sp, s_fin):
            copy_kept(S, sp, 3, [NB - 2, NB - 1])
            copy_kept(S, sp, 0, range(NB))
            for n in range(NB):
                if n:
                    sp.wait_ge(s_fin, 2 * n)
                copy_kept(S, sp, 2, [n])

        attend_stage(S, "ab_", groups, finish, copies)


def merge_b_stage(S, OA, Z, oT):
    nc = S.nc
    with ExitStack() as ctx:
        o = ctx.enter_context(nc.sbuf_tensor("mb_o", [P, 2, D], F32))
        s_o, s_tr, s_ev = S.sem("mb_o"), S.sem("mb_tr"), S.sem("mb_ev")
        with S.block() as block:
            @block.vector
            def _(dve):
                for t in range(TILES):
                    if t >= 2:
                        dve.wait_ge(s_tr, 2 * (t - 1))
                    for j in range(2):
                        sl = slice(512 * j, 512 * j + 512)
                        perm = o[:, t % 2, sl].rearrange("p (g k d) -> p k g d", g=GQA, d=DH)
                        nc.vector.tensor_tensor(perm, OA[:, t, sl].rearrange("p (k g d) -> p k g d", g=GQA, d=DH),
                                                Z[:, t, sl].rearrange("p (k g d) -> p k g d", g=GQA, d=DH), ALU.mult).then_inc(s_o, 1)

            @block.scalar
            def _(act):
                for v in range(2 * TILES):
                    t, j = divmod(v, 2)
                    act.wait_ge(s_tr, v + 1)
                    nc.scalar.activation(oT[:, 4 * j:4 * j + 4, t * P:(t + 1) * P],
                                         S.banks[v % 2][:, :].rearrange("p (g r) -> p g r", g=4), ACT.Copy).then_inc(s_ev, 1)

            @block.tensor
            def _(pe):
                for v in range(2 * TILES):
                    t, j = divmod(v, 2)
                    pe.wait_ge(s_o, v + 1)
                    if v >= 2:
                        pe.wait_ge(s_ev, v - 1)
                    for g in range(4):
                        ins = nc.tensor.transpose(S.banks[v % 2][:, g * P:(g + 1) * P],
                                                  o[:, t % 2, 512 * j + g * P:512 * j + (g + 1) * P], S.const("ident"))
                    ins.then_inc(s_tr, 1)


def prepare_sample_b_stage(S, QP, KT, ROWS, WINR, Z, GATES, T):
    nc, A = S.nc, S.dram
    sem = {n: S.sem("pp_" + n) for n in ("zero", "q", "zt", "ztc", "rest", "gs", "gl")}
    z_rows = Z[0:NS, TILES, :]
    with S.block() as block:
        @block.gpsimd
        def _(pool):
            nc.gpsimd.memset(T.q[:, :, :, :, :, :, :], 0.0).then_inc(sem["zero"], 1)

        @block.sync
        def _(sp):
            sp.dma_start(A["scratch_gates"], GATES[0:NS, TILES, :]).then_inc(sem["gs"], 16)
            sp.wait_ge(sem["gs"], 16)
            for pair in range(NB // 2):
                for n2 in range(2):
                    r = (2 * pair + n2) * NT
                    sp.dma_start(T.gates[64 * n2:64 * n2 + 64, pair, :],
                                 A["scratch_gates"][r:r + NT].rearrange("t (b h) -> h t b", b=3),
                                 allow_slow_non_contiguous=True).then_inc(sem["gl"], 16)
            sp.wait_ge(sem["gl"], 16 * NB)

        @block.tensor
        def _(pe):
            for h in range(HB):
                ins = nc.tensor.transpose(S.banks[0][0:DH, h * NS:(h + 1) * NS], z_rows[:, h * DH:(h + 1) * DH],
                                          S.const("ident")[0:NS, 0:NS])
            ins.then_inc(sem["zt"], 1)

        @block.scalar
        def _(act):
            nc.scalar.activation(T.kT[:, :, :, :], KT[:, :, :, SEQ:TOK], ACT.Copy)
            nc.scalar.activation(T.v[:, 0, :], ROWS[0:NS, TILES, 768:1024], ACT.Copy)
            nc.scalar.activation(T.v[:, 1, :], WINR[0:NS, TILES, 256:512], ACT.Copy).then_inc(sem["rest"], 1)
            act.wait_ge(sem["zt"], 1)
            for k2 in range(2):
                src = S.banks[0][0:DH, :].rearrange("p (j k c) -> p j k c", j=2, k=2)[:, :, k2, :]
                nc.scalar.activation(T.zT[k2 * DH:(k2 + 1) * DH, :].rearrange("p (j c) -> p j c", j=2), src,
                                     ACT.Copy).then_inc(sem["ztc"], 1)
            act.wait_ge(sem["ztc"], 2)
            act.wait_ge(sem["rest"], 1)

        @block.vector
        def _(dve):
            dve.wait_ge(sem["zero"], 1)
            n = 0
            for var in range(2):
                for j in range(2):
                    for k2 in range(2):
                        part = slice(k2 * DH, (k2 + 1) * DH)
                        for s in range(NB):
                            nc.vector.tensor_copy(T.q[part, var, s, j, k2, :, :],
                                                  QP[part, var, 4 * j:4 * j + 4, SEQ + s * NT:SEQ + (s + 1) * NT]).then_inc(sem["q"], 1)
                            n += 1
            dve.wait_ge(sem["q"], n)


def sample_b_stage(S, T, KC_S, VC_S, oT):
    nc, A = S.nc, S.dram
    NPAIR = NB // 2
    SELW = PAST + NS
    WINW = WIN + NS
    NU = 12
    order = [u for n2 in range(2) for u in [(n2, 0, j, half) for j in range(2) for half in range(2)] + [(n2, 1, j, 0) for j in range(2)]]
    n_imp = NSEL_S - 3
    with ExitStack() as ctx:
        def sb(name, shape, dt=F32):
            return ctx.enter_context(nc.sbuf_tensor("sb_" + name, shape, dt))
        sel = sb("sel_pages", [P, 2, NPAGES, 512])
        win = sb("win_rows", [P, 2, 4, 512])
        kT = sb("keys_turned", [P, 2, 512])
        pc = sb("p_cmp", [P, 64])
        pcn = sb("p_cmp_plain", [P, 64])
        psel = sb("p_sel", [P, SELW])
        pwin = sb("p_win", [P, WINW])
        mx, low, den, rec, wt = (sb(n, [P, 3]) for n in ("max", "low", "den", "rec", "wt"))
        pcT = sb("p_cmp_turned", [64, 2, P])
        cov = sb("covered", [P, NSEL_S])
        small = sb("small", [P, 4, n_imp])
        least = sb("least", [P, 2])
        bmask = sb("block_mask", [P, 16])
        pT = sb("p_turned", [P, 12, P])
        pTn = sb("p_new_turned", [NS, 2, P])
        s_sel, s_win = [S.sem("sb_sel0"), S.sem("sb_sel1")], [S.sem("sb_win0"), S.sem("sb_win1")]
        m = {n: S.sem("sb_" + n) for n in ("tr", "mul", "small", "cmpT", "cmpTc", "cov", "covc", "imp", "impc", "ecmp", "esel",
                                           "ewin", "lcmp", "lsel", "lwin", "ptr", "ptc", "pv", "o", "link", "pcmp", "psel", "pwin", "msk", "zero")}
        s_ev = [S.sem("sb_copied_by_vector"), S.sem("sb_copied_by_scalar")]
        B = S.banks
        ident = S.const("ident")
        new_mask = S.const("new_mask").rearrange("p (a c) -> p a c", a=NPAIR)

        with S.block() as block:
            @block.sync
            def _(sp):
                for n in range(NB):
                    if n >= 2:
                        sp.wait_ge(m["pv"], n // 2)
                    for pg in range(NPAGES):
                        page = sp.value_load(S.page_table[0:1, n * NPAGES + pg:n * NPAGES + pg + 1], min_val=0, max_val=S.n_pool - 1)
                        src = A["cache_nsa_paged"][0, bass.DynSlice(page, 1)].rearrange("o r s h d -> (o r) (s h d)")
                        sp.dma_start(sel[:, n % 2, pg, :], src[:, 512:1024]).then_inc(s_sel[n % 2], 16)
                    sp.dma_start(win[:, n % 2, :, :], A["cache_nsa_win"][0, n].rearrange("(p a) s h d -> p a (s h d)", a=4)).then_inc(s_win[n % 2], 16)

            @block.tensor
            def _(pe):
                def turn(x):
                    pair, u = divmod(x, NU)
                    n2, which, j, half = order[u]
                    if u == 0:
                        pe.wait_ge(s_sel[0], 128 * (pair + 1))
                    if u == 6:
                        pe.wait_ge(s_sel[1], 128 * (pair + 1))
                    if u in (4, 10):
                        pe.wait_ge(s_win[u // 6], 16 * (pair + 1))
                    if x >= 2:
                        pe.wait_ge(s_ev[x % 2], x // 2)
                    for c in range(4):
                        src = win[:, n2, c, :] if which else sel[:, n2, 4 * half + c, :]
                        ins = nc.tensor.transpose(B[4 + x % 2][:, c * P:(c + 1) * P], src[:, j * P:(j + 1) * P], ident)
                    ins.then_inc(m["tr"], 1)

                def multiply(x):
                    pair, u = divmod(x, NU)
                    n2, which, j, half = order[u]
                    n = 2 * pair + n2
                    if u == 0 and pair:
                        pe.wait_ge(m["msk"], pair)
                    pe.wait_ge(s_ev[x % 2], x // 2 + 1)
                    rows = slice(64 * n2 + 32 * j, 64 * n2 + 32 * j + 32)
                    q = T.q[:, 1, n, j, :, :, :].rearrange("p k g t -> p (k g t)")
                    bank = B[2] if which else B[half]
                    nc.tensor.matmul(bank[rows, :], q, kT[:, x % 2, :], start=True, stop=True, skip_group_check=True).then_inc(m["mul"], 1)

                def small_scores(pair):
                    for n2 in range(2):
                        for j in range(2):
                            n = 2 * pair + n2
                            rows = slice(64 * n2 + 32 * j, 64 * n2 + 32 * j + 32)
                            q = T.q[:, 1, n, j, :, :, :].rearrange("p k g t -> p (k g t)")
                            qc = T.q[:, 0, n, j, :, :, :].rearrange("p k g t -> p (k g t)")
                            for which in range(2):
                                nc.tensor.matmul(B[3][rows, which * NS:(which + 1) * NS], q, T.kT[:, which, j, :], start=True,
                                                 stop=True, skip_group_check=True)
                            ins = nc.tensor.matmul(B[3][rows, 64:64 + NCMP_S], qc, KC_S[:, n, j, 0:NCMP_S], start=True, stop=True,
                                                   skip_group_check=True)
                    ins.then_inc(m["small"], 1)
                x = 0
                for pair in range(NPAIR):
                    if pair:
                        pe.wait_ge(m["msk"], pair)
                    small_scores(pair)
                    for u in range(NU + 1):
                        if u < NU:
                            turn(x + u)
                        if u:
                            multiply(x + u - 1)
                    x += NU
                    pe.wait_ge(m["pcmp"], 2 * pair + 2)
                    nc.tensor.transpose(B[7][0:NCMP_S, 0:P], pcn[:, 0:NCMP_S], ident)
                    nc.tensor.transpose(B[7][0:NCMP_S, P:2 * P], pc[:, 0:NCMP_S], ident).then_inc(m["cmpT"], 1)
                    pe.wait_ge(m["cmpTc"], pair + 1)
                    nc.tensor.matmul(B[7][:, 256:256 + NSEL_S], pcT[0:NCMP_S, 0, :], S.const("cover")[0:NCMP_S, :], start=True,
                                     stop=True).then_inc(m["cov"], 1)
                    pe.wait_ge(m["covc"], pair + 1)
                    nc.tensor.matmul(B[7][:, 288:288 + NSEL_S], S.const("group_sum"), cov[:, :], start=True, stop=True).then_inc(m["imp"], 1)
                    pe.wait_ge(m["psel"], pair + 1)
                    pe.wait_ge(s_ev[0], x // 2)
                    pe.wait_ge(s_ev[1], x // 2)
                    for c in range(8):
                        nc.tensor.transpose(B[4 + c // 4][:, (c % 4) * P:(c % 4 + 1) * P], psel[:, c * P:(c + 1) * P], ident)
                    pe.wait_ge(m["pwin"], pair + 1)
                    nc.tensor.transpose(B[3][0:NS, 128:256], psel[:, PAST:], ident)
                    nc.tensor.transpose(B[3][0:NS, 256:384], pwin[:, WIN:], ident)
                    for c in range(4):
                        ins = nc.tensor.transpose(B[7][:, c * P:(c + 1) * P], pwin[:, c * P:(c + 1) * P], ident)
                    ins.then_inc(m["ptr"], 1)
                    pe.wait_ge(m["ptc"], 4 * (pair + 1))
                    if pair:
                        pe.wait_ge(m["o"], 4 * pair)
                    first = True
                    for n2 in range(2):
                        n = 2 * pair + n2
                        for j in range(2):
                            cols = slice(64 * n2 + 32 * j, 64 * n2 + 32 * j + 32)
                            vcol = slice(j * P, (j + 1) * P)
                            prods = [(VC_S[0:NCMP_S, n, vcol], pcT[0:NCMP_S, 1, cols])]
                            prods += [(sel[:, n2, c, 256 + j * P:256 + (j + 1) * P], pT[:, c, cols]) for c in range(8)]
                            prods += [(win[:, n2, c, 256 + j * P:256 + (j + 1) * P], pT[:, 8 + c, cols]) for c in range(4)]
                            prods += [(T.v[:, which, vcol], pTn[:, which, cols]) for which in range(2)]
                            for i, (v, p) in enumerate(prods):
                                ins = nc.tensor.matmul(B[6][:, cols], v, p, start=(i == 0), stop=(i == len(prods) - 1))
                    ins.then_inc(m["pv"], 1)

            def evacuate(engine, x):
                engine.wait_ge(m["tr"], x + 1)
                if x >= 2:
                    engine.wait_ge(m["mul"], x - 1)
                if x % 2 == 0:
                    nc.vector.tensor_copy(kT[:, 0, :], B[4][:, :]).then_inc(s_ev[0], 1)
                else:
                    nc.scalar.activation(kT[:, 1, :], B[5][:, :], ACT.Copy).then_inc(s_ev[1], 1)

            @block.scalar
            def _(act):
                for pair in range(NPAIR):
                    act.wait_ge(m["lcmp"], pair + 1)
                    if pair:
                        act.wait_ge(m["ptr"], pair)
                    nc.scalar.activation(pc[:, 0:NCMP_S], B[3][:, 64:64 + NCMP_S], ACT.Exp, bias=low[:, 0:1], scale=SCALE,
                                         accum_out=den[:, 0:1]).then_inc(m["ecmp"], 1)
                    for u in range(1, NU, 2):
                        evacuate(act, NU * pair + u)
                    act.wait_ge(m["lsel"], pair + 1)
                    nc.scalar.activation(psel[:, :], psel[:, :], ACT.Exp, bias=low[:, 1:2], scale=SCALE,
                                         accum_out=den[:, 1:2]).then_inc(m["esel"], 1)
                    act.wait_ge(m["lwin"], pair + 1)
                    nc.scalar.activation(pwin[:, :], pwin[:, :], ACT.Exp, bias=low[:, 2:3], scale=SCALE,
                                         accum_out=den[:, 2:3]).then_inc(m["ewin"], 1)
                    act.wait_ge(m["ptr"], pair + 1)
                    if pair:
                        act.wait_ge(m["pv"], pair)
                    nc.scalar.activation(pT[:, 4:8, :], B[5][:, :].rearrange("p (c r) -> p c r", c=4), ACT.Copy).then_inc(m["ptc"], 1)
                    nc.scalar.activation(pT[:, 8:12, :], B[7][:, :].rearrange("p (c r) -> p c r", c=4), ACT.Copy).then_inc(m["ptc"], 1)

            @block.vector
            def _(dve):
                link = linker(dve, m["link"])
                link(nc.vector.memset(bmask[:, :], 0.0))

                def lowest(src, i, sem):
                    link(nc.vector.tensor_reduce(mx[:, i:i + 1], src, AX, ALU.max))
                    nc.vector.tensor_scalar(low[:, i:i + 1], mx[:, i:i + 1], -SCALE, None, ALU.mult).then_inc(sem, 1)

                def weigh(pair, i, ap):
                    link(nc.vector.reciprocal(rec[:, i:i + 1], den[:, i:i + 1]))
                    link(nc.vector.tensor_tensor(wt[:, i:i + 1], rec[:, i:i + 1], T.gates[:, pair, i:i + 1], ALU.mult))
                for pair in range(NPAIR):
                    dve.wait_ge(m["small"], pair + 1)
                    lowest(B[3][:, 64:64 + NCMP_S], 0, m["lcmp"])
                    dve.wait_ge(m["ecmp"], pair + 1)
                    weigh(pair, 0, None)
                    if pair:
                        dve.wait_ge(m["pv"], pair)
                    nc.vector.tensor_scalar(pcn[:, 0:NCMP_S], pc[:, 0:NCMP_S], rec[:, 0:1], None, ALU.mult).then_inc(m["pcmp"], 1)
                    nc.vector.tensor_scalar(pc[:, 0:NCMP_S], pc[:, 0:NCMP_S], wt[:, 0:1], None, ALU.mult).then_inc(m["pcmp"], 1)
                    for u in range(0, NU, 2):
                        evacuate(dve, NU * pair + u)
                    dve.wait_ge(m["cmpT"], pair + 1)
                    nc.vector.tensor_copy(pcT[0:NCMP_S, :, :], B[7][0:NCMP_S, 0:2 * P].rearrange("p (a r) -> p a r", a=2)).then_inc(m["cmpTc"], 1)
                    dve.wait_ge(m["cov"], pair + 1)
                    nc.vector.tensor_copy(cov[:, :], B[7][:, 256:256 + NSEL_S]).then_inc(m["covc"], 1)
                    dve.wait_ge(m["imp"], pair + 1)
                    ids = S.const("block_id")
                    link(nc.vector.tensor_copy(small[:, 0, :], B[7][:, 289:289 + n_imp]))
                    link(nc.vector.tensor_reduce(least[:, 0:1], small[:, 0, :], AX, ALU.min))
                    link(nc.vector.scalar_tensor_tensor(out=small[:, 1, :], in0=small[:, 0, :], scalar=least[:, 0:1], in1=ids,
                                                        op0=ALU.is_equal, op1=ALU.mult))
                    link(nc.vector.tensor_reduce(least[:, 1:2], small[:, 1, :], AX, ALU.max))
                    link(nc.vector.tensor_scalar(bmask[:, 1:1 + n_imp], ids, least[:, 1:2], NEG, ALU.is_equal, ALU.mult))
                    dve.wait_ge(m["mul"], NU * (pair + 1))
                    for half in range(2):
                        link(nc.vector.tensor_tensor(psel[:, half * 512:(half + 1) * 512].rearrange("p (b k) -> p b k", k=SELB),
                                                     B[half][:, :].rearrange("p (b k) -> p b k", k=SELB),
                                                     bmask[:, 8 * half:8 * half + 8].unsqueeze(2).broadcast_to((P, 8, SELB)), ALU.add))
                    link(nc.vector.tensor_tensor(psel[:, PAST:], B[3][:, 0:NS], new_mask[:, pair, :], ALU.add))
                    lowest(psel[:, :], 1, m["lsel"])
                    link(nc.vector.tensor_tensor(pwin[:, 0:WIN], B[2][:, :], S.const("win_mask"), ALU.add))
                    link(nc.vector.tensor_tensor(pwin[:, WIN:], B[3][:, NS:2 * NS], new_mask[:, pair, :], ALU.add))
                    lowest(pwin[:, :], 2, m["lwin"])
                    dve.wait_ge(m["lwin"], pair + 1)
                    dve.wait_ge(m["esel"], pair + 1)
                    weigh(pair, 1, None)
                    nc.vector.tensor_scalar(psel[:, :], psel[:, :], wt[:, 1:2], None, ALU.mult).then_inc(m["psel"], 1)
                    dve.wait_ge(m["ewin"], pair + 1)
                    weigh(pair, 2, None)
                    nc.vector.tensor_scalar(pwin[:, :], pwin[:, :], wt[:, 2:3], None, ALU.mult).then_inc(m["pwin"], 1)
                    dve.wait_ge(m["ptr"], pair + 1)
                    nc.vector.tensor_copy(pT[:, 0:4, :], B[4][:, :].rearrange("p (c r) -> p c r", c=4)).then_inc(m["ptc"], 1)
                    nc.vector.tensor_copy(pTn[:, :, :], B[3][0:NS, 128:384].rearrange("p (a r) -> p a r", a=2)).then_inc(m["ptc"], 1)
                    dve.wait_ge(m["ptc"], 4 * (pair + 1))
                    nc.vector.memset(least[:, 0:1], 0.0).then_inc(m["msk"], 1)
                    dve.wait_ge(m["msk"], pair + 1)
                    dve.wait_ge(m["pv"], pair + 1)
                    src = B[6][:, 0:P].rearrange("p (n j k g t) -> p n j k g t", n=2, j=2, k=2, g=GQA)
                    for j in range(2):
                        for k2 in range(2):
                            part = slice(k2 * DH, (k2 + 1) * DH)
                            cols = slice(SEQ + 2 * pair * NT, SEQ + 2 * (pair + 1) * NT)
                            out = oT[part, 4 * j:4 * j + 4, cols].rearrange("p g (n t) -> p n g t", n=2)
                            z = T.zT[part, :].rearrange("p (j g r) -> p j g r", j=2, g=GQA)[:, j, :, 2 * pair * NT:2 * (pair + 1) * NT]
                            nc.vector.tensor_tensor(out, src[part, :, j, k2, :, :], z.rearrange("p g (n t) -> p n g t", n=2),
                                                    ALU.mult).then_inc(m["o"], 1)


def compress_samples_stage(S, KC_S, VC_S):
    A = S.dram

    def load(sp, pages, s_pg, s_tr):
        for n in range(NB):
            if n >= 2:
                sp.wait_ge(s_tr, 8 * (n - 1))
            for pg in range(NPAGES):
                page = sp.value_load(S.page_table[0:1, n * NPAGES + pg:n * NPAGES + pg + 1], min_val=0, max_val=S.n_pool - 1)
                src = A["cache_nsa_paged"][0, bass.DynSlice(page, 1)].rearrange("o (p a) s h d -> (o p) a (s h d)", a=2)
                lo = 64 * (pg % 2)
                sp.dma_start(pages[lo:lo + 64, n % 2, pg // 2, :, :], src[:, :, 0:512]).then_inc(s_pg[n % 2], 16)

    def landed(pe, it, s_pg):
        pe.wait_ge(s_pg[it % 2], 16 * NPAGES * (it // 2 + 1))
    compress_stage(S, "cs_", [4] * NB, load, landed, KC_S, VC_S)


def compress_prompt_stage(S, KC_P, VC_P):
    A = S.dram

    def load(sp, pages, s_pg, s_tr):
        sp.wait_ge(S.s_rows_out, 16 * (TILES + 1))
        rows = A["new_rows_p"][0, 0].rearrange("(b p a) s h d -> b p a (s h d)", a=2, p=64)
        for b in range(SEQ // PAGE):
            lo = 64 * (b % 2)
            sp.dma_start(pages[lo:lo + 64, 0, b // 2, :, :], rows[b, :, :, 0:512]).then_inc(s_pg[0], 16)

    def landed(pe, it, s_pg):
        pe.wait_ge(s_pg[0], 16 * (SEQ // PAGE))
    compress_stage(S, "cp_", [2], load, landed, KC_P, VC_P)


def layer_b(S):
    nc, A = S.nc, S.dram
    with ExitStack() as ctx:
        def sb(name, shape, c=ctx):
            return c.enter_context(nc.sbuf_tensor("lb_" + name, shape, F32))
        oT = sb("oT", [P, KC, TOK])
        T = Unit()
        T.q = sb("s_q", [P, 2, NB, 2, 2, GQA, NT])
        T.kT = sb("s_kT", [P, 2, 2, NS])
        T.v = sb("s_v", [NS, 2, 256])
        T.zT = sb("s_zT", [P, 2 * GQA * NS])
        T.gates = sb("s_gates", [P, NB // 2, 3])
        with ExitStack() as inner:
            KT = sb("kT", [P, 2, 2, TOK], inner)
            ROWS = sb("rows", [P, TILES + 1, 1024], inner)
            WINR = sb("win", [P, TILES + 1, 512], inner)
            Z = sb("z", [P, TILES + 1, D], inner)
            GATES = sb("gates", [P, TILES + 1, 3 * HB], inner)
            QP = sb("qp", [P, 2, 8, TOK], inner)
            norm_stage(S, "nb_", lambda e, t: None, A["b_norm"], oT)
            project_b_stage(S, oT, QP, KT, ROWS, WINR, Z, GATES)
            prepare_sample_b_stage(S, QP, KT, ROWS, WINR, Z, GATES, T)
            KC_P = sb("kc_p", [P, 1, 2, 64], inner)
            VC_P = sb("vc_p", [64, 1, 256], inner)
            compress_prompt_stage(S, KC_P, VC_P)
            with nc.sbuf_tensor("lb_oa", [P, TILES, D], F32) as OA:
                attend_b_stage(S, QP, KT, ROWS, WINR, KC_P, VC_P, GATES, OA)
                merge_b_stage(S, OA, Z, oT)
        KC_S = sb("kc_s", [P, NB, 2, 64])
        VC_S = sb("vc_s", [64, NB, 256])
        compress_samples_stage(S, KC_S, VC_S)
        sample_b_stage(S, T, KC_S, VC_S, oT)
        S.store_y = lambda t: A["y_p"][0, t * P:(t + 1) * P, :] if t < TILES else A["y_s"].rearrange("n t d -> (n t) d")
        w = A["b_w_out"][0].rearrange("(j k g d) e -> j k d g e", j=2, k=2, g=GQA)
        output_stage(S, "ob_", oT, lambda W: [(W[k2 * DH:(k2 + 1) * DH, 4 * j:4 * j + 4, :], w[j, k2])
                                              for j in range(2) for k2 in range(2)], KC, None)


def finish_stage(S):
    with S.nc.Block() as block:
        @block.sync
        def _(sp):
            for sem, value in S.outs + [(S.s_copy, S.n_copy)]:
                if value:
                    sp.wait_ge(sem, value)


def program(nc, dram, where, n_const):
    with ExitStack() as ctx:
        S = Stage(nc, dram, where, ctx)
        S.consts = ctx.enter_context(nc.sbuf_tensor("consts", [P, n_const], F32))
        S.x = ctx.enter_context(nc.sbuf_tensor("x", [P, TILES + 1, D], F32))
        S.page_table = ctx.enter_context(nc.sbuf_tensor("page_table", [1, NB * NPAGES], I32))
        S.n_pool = dram["cache_nsa_paged"].shape[1]
        S.banks = [ctx.enter_context(nc.psum_tensor(f"bank{i}", [P, 512], F32)) for i in range(8)]
        load_stage(S)
        layer_a(S)
        layer_b(S)
        finish_stage(S)


_INS = ["x_prompt", "x_sample", "cache_dil_0", "cache_dil_1", "cache_dil_2", "cache_nsa_paged", "cache_nsa_win", "page_table",
        "a_norm", "a_w_in", "a_q_norm", "a_k_norm", "a_w_out", "b_norm", "b_w_in", "b_q_norm", "b_k_norm", "b_cmp_pe",
        "b_cmp_w1", "b_cmp_w2", "b_w_out"]
_OUTS = [("y_p", (1, SEQ, D)), ("y_s", (NB, NT, D)),
         ("new_dil_0_p", (1, 1, 128, 2, HA, DH)), ("new_dil_1_p", (1, 1, 512, 2, HA, DH)), ("new_dil_2_p", (1, 1, 512, 2, HA, DH)),
         ("new_rows_p", (1, 1, SEQ, 4, KVH, DH)), ("new_win_p", (1, 1, SEQ, 2, KVH, DH)),
         ("new_dil_0_s", (1, NB, 128, 2, HA, DH)), ("new_dil_1_s", (1, NB, 512, 2, HA, DH)),
         ("new_dil_2_s", (1, NB, PAST + NT, 2, HA, DH)),
         ("new_rows_s", (1, NB, NT, 4, KVH, DH)), ("new_win_s", (1, NB, WIN, 2, KVH, DH))]


def kernel(**inputs):
    import numpy as _np
    import concourse.bacc as _bacc
    from concourse import mybir as _mybir
    from concourse.bass_utils import run_bass_kernel_spmd as _run

    nc = _bacc.Bacc("TRN2", target_bir_lowering=False, num_devices=1)
    arrays, dram = {}, {}
    table, where = constants()
    for name in _INS + ["consts"]:
        a = table if name == "consts" else _np.ascontiguousarray(inputs[name])
        arrays[f"in_{name}"] = a
        dram[name] = nc.dram_tensor(f"in_{name}", a.shape, _mybir.dt.from_np(a.dtype), kind="ExternalInput").ap()
    for name, shape in _OUTS:
        dram[name] = nc.dram_tensor(f"out_{name}", shape, _mybir.dt.float32, kind="ExternalOutput").ap()
    dram["scratch_gates"] = nc.dram_tensor("scratch_gates", (NS, 3 * HB), _mybir.dt.float32, kind="Internal").ap()
    dram["scratch_a"] = nc.dram_tensor("scratch_a", (2, SEQ, WA + 2 * HA), _mybir.dt.float32, kind="Internal").ap()
    program(nc, dram, where, where["a_mask"][0])
    r = _run(nc, [arrays], core_ids=[0])
    return tuple(r.results[0][f"out_{name}"] for name, _ in _OUTS)
```

```python
from contextlib import ExitStack, contextmanager

import numpy as np

import concourse.bass as bass
from concourse import mybir

ALU = mybir.AluOpType
ACT = mybir.ActivationFunctionType
F32 = mybir.dt.float32
I32 = mybir.dt.int32
AX = mybir.AxisListType.X

P = 128
D = 1024
SEQ = 512
NB = 8
NT = 4
NS = NB * NT
TOK = SEQ + NS
TILES = SEQ // P
DH = 64
HALF = DH // 2
SCALE = DH ** -0.5
EPS = 1e-6
KC = D // P
PATTERNS = ((128, 1), (512, 4), (2048, 16))
HA = 8
WA = HA * DH
HB = 16
KVH = 4
GQA = HB // KVH
KVW = KVH * DH
PAST = 1024
PAGE = 128
NPAGES = PAST // PAGE
WIN = 512
CSTRIDE = 16
CLEN = 32
NCMP_P = (SEQ - CLEN) // CSTRIDE + 1
NCMP_S = (PAST + NT - CLEN) // CSTRIDE + 1
SELB = 64
NSEL_S = -(-(PAST + NT) // SELB)
HID = 128
NEG = -1e30
ROPE_SETS = 2 * TILES + 1


def rows_of(t):
    return P if t < TILES else NS


def token_of(g, t, p):
    return TILES * p + t if g else t * P + p


def constants():
    f = np.float32
    parts = {}
    parts["ident"] = np.eye(P, dtype=f)
    inv = (f(10000.0) ** (-np.arange(HALF, dtype=f) / f(HALF))).astype(f)
    pos = np.zeros((P, ROPE_SETS), f)
    for g in range(2):
        for t in range(TILES):
            pos[:, g * TILES + t] = [token_of(g, t, p) for p in range(P)]
    pos[:NS, ROPE_SETS - 1] = [PAST + r % NT for r in range(NS)]
    ang = pos[:, :, None] * inv[None, None, :]
    c, s = np.cos(ang).astype(f), np.sin(ang).astype(f)
    parts["cos"] = np.concatenate([c, c], -1)
    parts["sin"] = np.concatenate([-s, s], -1)
    q, k = np.arange(P)[:, None], np.arange(P)[None, :]
    causal = np.where(k <= q, 0, NEG).astype(f)
    parts["band"] = np.concatenate([np.where(k >= q, 0, NEG).astype(f), causal], 1)
    parts["every4"] = np.where((k <= q) & ((q - k) % 4 == 0), 0, NEG).astype(f)
    parts["causal"] = np.concatenate([np.zeros((P, 3 * P), f), causal], 1)
    end = np.arange(NCMP_P) * CSTRIDE + CLEN - 1
    tok = np.arange(TILES)[None, :] * P + np.arange(P)[:, None]
    parts["cmp_mask"] = np.where(end[None, None, :] <= tok[:, :, None], 0, NEG).astype(f)
    parts["cmp_any"] = (tok >= CLEN - 1).astype(f)
    t = (np.arange(P) % NT)[:, None]
    n2 = (np.arange(P) // 64)[:, None]
    s = (np.arange(WIN) % P * 4 + np.arange(WIN) // P)[None, :]
    parts["win_mask"] = np.where(s >= t, 0, NEG).astype(f)
    new = np.arange(NS)[None, None, :]
    pair = np.arange(NB // 2)[None, :, None]
    parts["new_mask"] = np.where((new // NT == 2 * pair + n2[:, :, None]) & (new % NT <= t[:, :, None]), 0, NEG).astype(f)
    grp = np.arange(P) // 16 * 4 + np.arange(P) % 4
    parts["group_sum"] = (grp[:, None] == grp[None, :]).astype(f)
    c0 = np.arange(NCMP_S)[:, None] * CSTRIDE
    b0 = np.arange(NSEL_S)[None, :] * SELB
    cover = np.zeros((P, NSEL_S), f)
    cover[:NCMP_S] = (c0 <= b0 + SELB - 1) & (c0 + CLEN - 1 >= b0)
    parts["cover"] = cover
    parts["block_id"] = np.broadcast_to(np.arange(1, NSEL_S - 2, dtype=f), (P, NSEL_S - 3))
    parts["half_power"] = np.full((P, 16), -0.5, f)
    t = (np.arange(P) % NT)[:, None]
    n4 = (np.arange(P) // 32)[:, None]
    new = np.arange(NS)[None, :]
    a_mask = np.zeros((P, 2, 3 * P + 3 * NS), f)
    a_mask[:, :, 0:P] = np.where(k >= t, 0, NEG)[:, None]
    a_mask[:, :, 2 * P:3 * P] = np.where(k // 64 == t // 2, 0, NEG)[:, None]
    for b in range(2):
        own = new // NT == 4 * b + n4
        for g in range(3):
            seen = own & ((new % NT == t) if g else (new % NT <= t))
            a_mask[:, b, 3 * P + g * NS:3 * P + (g + 1) * NS] = np.where(seen, 0, NEG)
    parts["a_mask"] = a_mask
    where, at = {}, 0
    flat = []
    for name, a in parts.items():
        a = np.asarray(a, f).reshape(P, -1)
        where[name] = (at, at + a.shape[1])
        at += a.shape[1]
        flat.append(a)
    return np.ascontiguousarray(np.concatenate(flat, 1)), where


LASTING = (["s_const", "s_copy", "s_page_table", "pa_vout", "pb_rows_out", "pb_win_out", "oa_stored", "ob_stored", "s_og"]
           + [f"s_x{t}" for t in range(TILES + 1)] + [f"pa_kout{i}" for i in range(3)])


class Stage:

    def __init__(self, nc, dram, where, ctx):
        self.nc, self.dram, self.where, self.ctx = nc, dram, where, ctx
        self.lasting = {n: ctx.enter_context(nc.semaphore(n)) for n in LASTING}
        self.stage_sems = []
        self.n_vout = 0
        self.outs = []

    def const(self, name):
        a, b = self.where[name]
        return self.consts[:, a:b]

    def lasting_sem(self, name):
        return self.lasting[name]

    def sem(self, name):
        handle = self.nc.alloc_semaphore(name=name)
        self.stage_sems.append(handle)
        return handle

    @contextmanager
    def block(self):
        with self.nc.Block() as block:
            yield block
        self.nc.clear_and_free_semaphores(self.stage_sems)
        self.stage_sems = []
        self.nc.all_engine_barrier()


def permuted(ap, g, t):
    if t == TILES:
        return ap[:, SEQ:TOK]
    return ap[:, t:SEQ:TILES] if g else ap[:, t * P:(t + 1) * P]


def dram_rows(ap, g, t):
    return ap[t:SEQ:TILES] if g else ap[t * P:(t + 1) * P]


def linker(engine, sem):
    count = [0]

    def link(ins):
        count[0] += 1
        ins.then_inc(sem, 1)
        engine.wait_ge(sem, count[0])
    return link



def load_stage(S):
    nc, A = S.nc, S.dram
    S.s_const, S.s_x, S.s_copy = S.lasting_sem("s_const"), [S.lasting_sem(f"s_x{t}") for t in range(TILES + 1)], S.lasting_sem("s_copy")
    S.s_pages = S.lasting_sem("s_page_table")
    S.n_copy = 0
    with nc.Block() as block:
        @block.sync
        def _(sp):
            xp, xs = A["x_prompt"][0], A["x_sample"].rearrange("n t d -> (n t) d")
            for t in range(TILES):
                sp.dma_start(S.x[:, t, :], xp[t * P:(t + 1) * P, :]).then_inc(S.s_x[t], 16)
            sp.dma_start(S.x[0:NS, TILES, :], xs).then_inc(S.s_x[TILES], 16)
            sp.dma_start(S.consts[:, :], A["consts"][:, 0:S.where["a_mask"][0]]).then_inc(S.s_const, 16)
            sp.dma_start(S.page_table[:, :], A["page_table"].rearrange("(o n) p -> o (n p)", o=1)).then_inc(S.s_pages, 16)
            sp.wait_ge(S.s_pages, 16)


def copy_kept(S, engine, which, sequences):
    A = S.dram
    for n in sequences:
        if which == 3:
            cache, out, first, kept = A["cache_nsa_win"], A["new_win_s"], NT, WIN - NT
        else:
            win = PATTERNS[which][0]
            L = min(win, PAST)
            first = max(L + NT - win, 0)
            cache, out, kept = A[f"cache_dil_{which}"], A[f"new_dil_{which}_s"], L - first
        src = cache[0, n, first:first + kept].rearrange("r v h d -> (r v h d)")
        dst = out[0, n, 0:kept].rearrange("r v h d -> (r v h d)")
        engine.dma_start(dst.rearrange("(a b) -> a b", a=64), src.rearrange("(a b) -> a b", a=64)).then_inc(S.s_copy, 16)
        S.n_copy += 16


def norm_stage(S, pfx, x_ready, gain, hT):
    nc = S.nc
    with ExitStack() as ctx:
        def sb(name, shape):
            return ctx.enter_context(nc.sbuf_tensor(pfx + name, shape, F32))
        sq = sb("squares", [P, D])
        ss = sb("square_sum", [P, TILES + 1])
        ms = sb("mean_square", [P, TILES + 1])
        rstd = sb("rstd", [P, TILES + 1])
        xn = sb("x_normed", [P, 2, D])
        gain_rows = sb("gain_rows", [KC, P])
        gain_cols = sb("gain_cols", [P, KC])
        s_gain, s_gt, s_gc = S.sem(pfx + "gain"), S.sem(pfx + "gain_turned"), S.sem(pfx + "gain_cols")
        s_ss, s_ms, s_rstd = S.sem(pfx + "ss"), S.sem(pfx + "ms"), S.sem(pfx + "rstd")
        s_xn, s_tr, s_h = S.sem(pfx + "xn"), S.sem(pfx + "turned"), S.sem(pfx + "h")
        with S.block() as block:
            @block.sync
            def _(sp):
                sp.dma_start(gain_rows[:, :], gain.rearrange("o (k p) -> (o k) p", p=P)).then_inc(s_gain, 16)

            @block.scalar
            def _(act):
                for t in range(TILES + 1):
                    R = rows_of(t)
                    x_ready(act, t)
                    if t:
                        act.wait_ge(s_ss, t)
                    nc.scalar.activation(sq[0:R, :], S.x[0:R, t, :], ACT.Square,
                                         accum_out=ss[0:R, t:t + 1]).then_inc(s_ss, 1)
                for t in range(TILES + 1):
                    R = rows_of(t)
                    if t == 0:
                        act.wait_ge(s_gc, 1)
                    for k in range(KC):
                        if k % 4 == 0:
                            act.wait_ge(s_tr, 2 * t + k // 4 + 1)
                        ins = nc.scalar.activation(hT[:, k, t * P:t * P + R], S.banks[k // 4][:, (k % 4) * P:(k % 4) * P + R],
                                                   ACT.Copy, scale=gain_cols[:, k:k + 1])
                        if k % 4 == 3:
                            ins.then_inc(s_h, 1)

            @block.gpsimd
            def _(pool):
                pool.wait_ge(S.s_const, 16)
                for t in range(TILES + 1):
                    R = rows_of(t)
                    pool.wait_ge(s_ss, t + 1)
                    nc.gpsimd.tensor_scalar(ms[0:R, t:t + 1], ss[0:R, t:t + 1], 1.0 / D, EPS, ALU.mult, ALU.add).then_inc(s_ms, 1)
                    pool.wait_ge(s_ms, t + 1)
                    nc.gpsimd.tensor_tensor(rstd[0:R, t:t + 1], ms[0:R, t:t + 1], S.const("half_power")[0:R, 0:1],
                                            ALU.pow).then_inc(s_rstd, 1)

            @block.vector
            def _(dve):
                dve.wait_ge(s_gt, 1)
                nc.vector.tensor_copy(gain_cols[:, :], S.banks[2][:, 0:KC]).then_inc(s_gc, 1)
                for t in range(TILES + 1):
                    R = rows_of(t)
                    dve.wait_ge(s_rstd, t + 1)
                    x_ready(dve, t)
                    if t >= 2:
                        dve.wait_ge(s_tr, 2 * (t - 1))
                    nc.vector.tensor_scalar(xn[0:R, t % 2, :], S.x[0:R, t, :], rstd[0:R, t:t + 1], None, ALU.mult).then_inc(s_xn, 1)

            @block.tensor
            def _(pe):
                ident = S.const("ident")
                pe.wait_ge(S.s_const, 16)
                pe.wait_ge(s_gain, 16)
                nc.tensor.transpose(S.banks[2][:, 0:KC], gain_rows[:, :], ident[0:KC, 0:KC]).then_inc(s_gt, 1)
                for t in range(TILES + 1):
                    R = rows_of(t)
                    pe.wait_ge(s_xn, t + 1)
                    for k in range(KC):
                        if t and k % 4 == 0:
                            pe.wait_ge(s_h, 2 * (t - 1) + k // 4 + 1)
                        ins = nc.tensor.transpose(S.banks[k // 4][:, (k % 4) * P:(k % 4) * P + R],
                                                  xn[0:R, t % 2, k * P:(k + 1) * P], ident[0:R, 0:R])
                        if k % 4 == 3:
                            ins.then_inc(s_tr, 1)


def rope_tables(S, dve, sem, gains, tabs, spans):
    nc = S.nc
    for i in range(gains.shape[1]):
        for which, name in ((0, "cos"), (1, "sin")):
            src = S.const(name).rearrange("p (s d) -> p s d", d=DH)
            for lo in (0, HALF):
                glo = lo if which == 0 else HALF - lo
                for at, n, to in spans:
                    g = gains[:, i, glo:glo + HALF].unsqueeze(1).broadcast_to((P, n, HALF))
                    nc.vector.tensor_tensor(tabs[:, i, which, to:to + n, lo:lo + HALF], src[:, at:at + n, lo:lo + HALF], g,
                                            ALU.mult).then_inc(sem, 1)


class Unit:
    pass


def project_a_stage(S, hT, QK, V, Z):
    nc, A = S.nc, S.dram
    w = A["a_w_in"][0].rearrange("(k p) e -> p k e", p=P)
    units = []
    n_qk = n_lin = 0
    for c in range(10):
        for t in range(TILES + 1):
            u = Unit()
            u.c, u.t, u.g, u.R, u.v = c, t, (c % 3 if c < 9 else 0), rows_of(t), len(units)
            u.qk = c < 6
            u.i = n_qk if u.qk else n_lin
            if u.qk:
                n_qk += 1
            else:
                n_lin += 1
            units.append(u)
    qk_units = [u for u in units if u.qk]
    with ExitStack() as ctx:
        def sb(name, shape):
            return ctx.enter_context(nc.sbuf_tensor("pa_" + name, shape, F32))
        W = sb("w", [P, 2, KC, WA])
        gains = sb("gains", [P, 2, DH])
        tabs = sb("tables", [P, 2, 2, ROPE_SETS, DH])
        sq = sb("squares", [P, WA])
        ss = sb("square_sum", [P, 2, HA])
        ms = sb("mean_square", [P, HA])
        rstd = sb("rstd", [P, 2, HA])
        normed = sb("normed", [P, 2, WA])
        straight = sb("straight", [P, WA])
        swapped = sb("swapped", [P, 2, WA])
        rot = sb("rotated", [P, 3, WA])
        s_w = [S.sem(f"pa_w{i}") for i in range(2)]
        s_gains, s_tabs = S.sem("pa_gains"), S.sem("pa_tabs")
        s_u, s_lin, s_sq, s_ss, s_ms, s_rstd = (S.sem("pa_" + n) for n in ("u", "lin", "sq", "ss", "ms", "rstd"))
        s_n, s_st, s_sw, s_rot, s_tr, s_ev = (S.sem("pa_" + n) for n in ("n", "st", "sw", "rot", "tr", "ev"))
        s_kout = [S.lasting_sem(f"pa_kout{i}") for i in range(3)]
        S.s_vout = S.lasting_sem("pa_vout")
        n_kout, kout_at = [0, 0, 0], {}
        for u in qk_units:
            if u.c >= 3:
                stored = u.t == TILES or u.g or u.t == TILES - 1
                if stored:
                    n_kout[u.i % 3] += 16
                    kout_at[u.i] = n_kout[u.i % 3]
        U = S.banks[0:3]
        T = S.banks[3:5]

        def dest(u, kv):
            win = PATTERNS[u.g][0]
            if u.t == TILES:
                new = A[f"new_dil_{u.g}_s"]
                return new[0, :, new.shape[2] - NT:, kv].rearrange("n t h d -> n t (h d)")
            out = A[f"new_dil_{u.g}_p"][0, 0, :, kv].rearrange("r h d -> r (h d)")
            return dram_rows(out, u.g, u.t) if u.g else out

        S.n_tabs = 8
        with S.block() as block:
            @block.sync
            def _(sp):
                for i, name in enumerate(("a_q_norm", "a_k_norm")):
                    sp.dma_start(gains[:, i, :], A[name].broadcast_to((P, DH))).then_inc(s_gains, 16)
                for c in range(2):
                    sp.dma_start(W[:, c, :, :], w[:, :, c * WA:(c + 1) * WA]).then_inc(s_w[c], 16)
                for c in range(10):
                    if c + 2 < 10:
                        sp.wait_ge(s_u, 5 * (c + 1))
                        sp.dma_start(W[:, c % 2, :, :], w[:, :, (c + 2) * WA:(c + 3) * WA]).then_inc(s_w[c % 2], 16)
                        copy_kept(S, sp, 1, [c])
                    for u in units[5 * c:5 * c + 5]:
                        if u.i in kout_at and u.qk:
                            sp.wait_ge(s_rot, u.i + 1)
                            sp.dma_start(dest(u, 0), rot[0:u.R, u.i % 3, :]).then_inc(s_kout[u.i % 3], 16)
                        if 6 <= c < 9 and (u.t == TILES or u.g or u.t == TILES - 1):
                            sp.wait_ge(s_lin, u.i + 1)
                            sp.dma_start(dest(u, 1), V[0:u.R, u.g, u.t, :]).then_inc(S.s_vout, 16)
                            S.n_vout += 16
                S.outs += [(s_kout[i], n_kout[i]) for i in range(3)] + [(S.s_vout, S.n_vout)]

            @block.tensor
            def _(pe):
                ident = S.const("ident")

                def turn(u):
                    pe.wait_ge(s_rot, u.i + 1)
                    if u.i >= 2:
                        pe.wait_ge(s_ev, u.i - 1)
                    for j in range(4):
                        ins = nc.tensor.transpose(T[u.i % 2][:, j * P:j * P + u.R], rot[0:u.R, u.i % 3, j * P:(j + 1) * P],
                                                  ident[0:u.R, 0:u.R])
                    ins.then_inc(s_tr, 1)
                for u in units:
                    if u.t == 0:
                        pe.wait_ge(s_w[u.c % 2], 16 * (u.c // 2 + 1))
                    if u.v >= 3:
                        old = units[u.v - 3]
                        pe.wait_ge(s_n if old.qk else s_lin, old.i + 1)
                    for k in range(KC):
                        ins = nc.tensor.matmul(U[u.v % 3][0:u.R, :], permuted(hT[:, k, :], u.g, u.t), W[:, u.c % 2, k, :],
                                               start=(k == 0), stop=(k == KC - 1))
                    ins.then_inc(s_u, 1)
                    if u.v >= 2 and units[u.v - 2].qk:
                        turn(units[u.v - 2])

            @block.scalar
            def _(act):
                def evacuate(u):
                    act.wait_ge(s_tr, u.i + 1)
                    nc.scalar.activation(QK[:, u.c, :, u.t * P:u.t * P + u.R],
                                         T[u.i % 2][:, :].rearrange("p (j r) -> p j r", j=4)[:, :, 0:u.R], ACT.Copy).then_inc(s_ev, 1)
                for u in units:
                    act.wait_ge(s_u, u.v + 1)
                    src = U[u.v % 3][0:u.R, :]
                    if u.qk:
                        if u.i:
                            act.wait_ge(s_ss, u.i)
                        nc.scalar.activation(sq[0:u.R, :], src, ACT.Square).then_inc(s_sq, 1)
                    elif u.c < 9:
                        nc.scalar.activation(V[0:u.R, u.g, u.t, :], src, ACT.Copy).then_inc(s_lin, 1)
                    else:
                        nc.scalar.activation(Z[0:u.R, u.t, :], src, ACT.Silu).then_inc(s_lin, 1)
                    if u.v >= 2 and units[u.v - 2].qk:
                        evacuate(units[u.v - 2])

            @block.gpsimd
            def _(pool):
                for u in qk_units:
                    R, i = u.R, u.i
                    pool.wait_ge(s_ss, i + 1)
                    nc.gpsimd.tensor_scalar(ms[0:R, :], ss[0:R, i % 2, :], 1.0 / DH, EPS, ALU.mult, ALU.add).then_inc(s_ms, 1)
                    pool.wait_ge(s_ms, i + 1)
                    nc.gpsimd.tensor_tensor(rstd[0:R, i % 2, :], ms[0:R, :], S.const("half_power")[0:R, 0:HA], ALU.pow).then_inc(s_rstd, 1)
                    pool.wait_ge(s_n, i + 1)
                    if i == 0:
                        pool.wait_ge(s_tabs, S.n_tabs)
                    if i >= 2:
                        pool.wait_ge(s_rot, i - 1)
                    n3 = normed[0:R, i % 2, :].rearrange("p (h d) -> p h d", d=DH)
                    o3 = swapped[0:R, i % 2, :].rearrange("p (h d) -> p h d", d=DH)
                    for lo in (0, HALF):
                        tab = rope_tab(tabs, u.c // 3, 1, u)[0:R, lo:lo + HALF].unsqueeze(1).broadcast_to((R, HA, HALF))
                        nc.gpsimd.tensor_tensor(o3[:, :, lo:lo + HALF], n3[:, :, HALF - lo:DH - lo], tab, ALU.mult).then_inc(s_sw, 1)

            @block.vector
            def _(dve):
                dve.wait_ge(S.s_const, 16)
                dve.wait_ge(s_gains, 32)
                rope_tables(S, dve, s_tabs, gains, tabs, [(0, ROPE_SETS, 0)])

                def first(u):
                    R, i = u.R, u.i
                    dve.wait_ge(s_sq, i + 1)
                    nc.vector.tensor_reduce(ss[0:R, i % 2, :], sq[0:R, :].rearrange("p (h d) -> p h d", d=DH), AX,
                                            ALU.add).then_inc(s_ss, 1)

                def second(u):
                    R, i = u.R, u.i
                    dve.wait_ge(s_rstd, i + 1)
                    n3 = normed[0:R, i % 2, :].rearrange("p (h d) -> p h d", d=DH)
                    dve.wait_ge(s_u, u.v + 1)
                    nc.vector.tensor_tensor(n3, U[u.v % 3][0:R, :].rearrange("p (h d) -> p h d", d=DH),
                                            rstd[0:R, i % 2, :].unsqueeze(2).broadcast_to((R, HA, DH)), ALU.mult).then_inc(s_n, 1)
                    dve.wait_ge(s_n, i + 1)
                    tab = rope_tab(tabs, u.c // 3, 0, u)[0:R, :].unsqueeze(1).broadcast_to((R, HA, DH))
                    nc.vector.tensor_tensor(straight[0:R, :].rearrange("p (h d) -> p h d", d=DH), n3, tab, ALU.mult).then_inc(s_st, 1)
                    dve.wait_ge(s_st, i + 1)
                    dve.wait_ge(s_sw, 2 * (i + 1))
                    if i >= 3:
                        dve.wait_ge(s_tr, i - 2)
                        if i - 3 in kout_at:
                            dve.wait_ge(s_kout[i % 3], kout_at[i - 3])
                    nc.vector.tensor_tensor(rot[0:R, i % 3, :], straight[0:R, :], swapped[0:R, i % 2, :], ALU.add).then_inc(s_rot, 1)
                dve.wait_ge(s_tabs, S.n_tabs)
                for i, u in enumerate(qk_units):
                    first(u)
                    if i:
                        second(qk_units[i - 1])
                second(qk_units[-1])


def rope_tab(tabs, which, part, u):
    s = ROPE_SETS - 1 if u.t == TILES else (TILES if u.g else 0) + u.t
    return tabs[:, which, part, s, :]


def attend_stage(S, pfx, groups, finish, sync_program=None, loaded=None):
    nc = S.nc
    units = [u for gr in groups for u in gr.units]
    for v, u in enumerate(units):
        u.v = v
        u.gi = v // 8
    N = len(units)
    with ExitStack() as ctx:
        def sb(name, shape):
            return ctx.enter_context(nc.sbuf_tensor(pfx + name, shape, F32))
        masked = sb("masked", [P, 2, SEQ])
        probs = sb("probs", [P, 2, SEQ])
        pT = sb("probs_turned", [P, 2, 4, P])
        s_sc, s_m, s_e, s_tr, s_pv = (S.sem(pfx + n) for n in ("scores", "masked", "exp", "turned", "pv"))
        s_ev = [S.sem(pfx + "copied_by_vector"), S.sem(pfx + "copied_by_scalar")]
        s_fin, s_link = S.sem(pfx + "finished"), S.sem(pfx + "link")
        SC, TR, OB = S.banks[0:3], S.banks[3:5], S.banks[5:7]

        def copied(engine, v):
            engine.wait_ge(s_ev[v % 2], v // 2 + 1)

        def copy_out(engine, v):
            u = units[v]
            engine.wait_ge(s_tr, v + 1)
            if v >= 2:
                engine.wait_ge(s_pv, v - 1)
            n = len(u.vs)
            rows = u.vs[0].shape[0]
            src = TR[v % 2][0:rows, 0:n * P].rearrange("p (c q) -> p c q", q=P)
            if v % 2 == 0:
                nc.vector.tensor_copy(pT[0:rows, v % 2, 0:n, :], src).then_inc(s_ev[0], 1)
            else:
                nc.scalar.activation(pT[0:rows, v % 2, 0:n, :], src, ACT.Copy).then_inc(s_ev[1], 1)

        with S.block() as block:
            if sync_program:
                @block.sync
                def _(sp):
                    sync_program(sp, s_fin)

            @block.tensor
            def _(pe):
                ident = S.const("ident")
                if loaded:
                    loaded(pe)

                def scores(v):
                    u = units[v]
                    if v >= 3:
                        pe.wait_ge(s_m, v - 2)
                    nc.tensor.matmul(SC[v % 3][:, 0:u.N], u.q, u.k, start=True, stop=True).then_inc(s_sc, 1)

                def turn(v):
                    u = units[v]
                    pe.wait_ge(s_e, v + 1)
                    if v >= 2:
                        copied(pe, v - 2)
                    for c, val in enumerate(u.vs):
                        rows = val.shape[0]
                        ins = nc.tensor.transpose(TR[v % 2][0:rows, c * P:(c + 1) * P], probs[:, v % 2, c * P:c * P + rows], ident)
                    ins.then_inc(s_tr, 1)

                def values(v):
                    u = units[v]
                    copied(pe, v)
                    if v % 8 == 0 and u.gi >= 2:
                        pe.wait_ge(s_fin, u.gi - 1)
                    h = v % 8
                    for c, val in enumerate(u.vs):
                        rows = val.shape[0]
                        ins = nc.tensor.matmul(OB[u.gi % 2][:, h * DH:(h + 1) * DH], pT[0:rows, v % 2, c, :], val,
                                               start=(c == 0), stop=(c == len(u.vs) - 1))
                    ins.then_inc(s_pv, 1)
                for v in range(N + 3):
                    if v < N:
                        scores(v)
                    if 2 <= v < N + 2:
                        turn(v - 2)
                    if v >= 3:
                        values(v - 3)

            @block.scalar
            def _(act):
                for v in range(N + 2):
                    if v < N:
                        u = units[v]
                        act.wait_ge(s_m, v + 1)
                        if v >= 2:
                            act.wait_ge(s_tr, v - 1)
                        nc.scalar.activation(probs[:, v % 2, 0:u.N], masked[:, v % 2, 0:u.N], ACT.Exp, bias=u.low,
                                             scale=-1.0, accum_out=u.den).then_inc(s_e, 1)
                    if v >= 2 and (v - 2) % 2 == 1:
                        copy_out(act, v - 2)

            @block.vector
            def _(dve):
                link = linker(dve, s_link)
                for v in range(N + 12):
                    if v < N:
                        u = units[v]
                        dve.wait_ge(s_sc, v + 1)
                        if v >= 2:
                            dve.wait_ge(s_e, v - 1)
                        nc.vector.tensor_tensor_reduce(masked[:, v % 2, 0:u.N], SC[v % 3][:, 0:u.N], u.mask, -SCALE, 3e38,
                                                       ALU.add, ALU.min, u.low).then_inc(s_m, 1)
                    if 2 <= v < N + 2 and (v - 2) % 2 == 0:
                        copy_out(dve, v - 2)
                    if v >= 11 and (v - 11) % 8 == 0:
                        gi = (v - 11) // 8
                        if gi < len(groups):
                            if gi:
                                dve.wait_ge(s_fin, gi)
                            dve.wait_ge(s_pv, 8 * gi + 8)
                            finish(dve, gi, groups[gi], OB[gi % 2], link).then_inc(s_fin, 1)


def attend_a_stage(S, QK, V, OG):
    nc = S.nc
    groups = []
    with ExitStack() as ctx:
        stats = ctx.enter_context(nc.sbuf_tensor("aa_stats", [P, 3 * TILES, 2, HA], F32))
        out = ctx.enter_context(nc.sbuf_tensor("aa_out", [P, 2, WA + 2 * HA], F32))
        for g in (1, 2, 0):
            for t in range(TILES):
                gr = Unit()
                gr.g, gr.t, gr.units = g, t, []
                for h in range(HA):
                    u = Unit()
                    half, j = h % 2, h // 2
                    part = slice(half * DH, half * DH + DH)
                    keys = (max(t - 1, 0), t + 1) if g == 0 else (t, t + 1)
                    u.q = QK[part, g, j, t * P:(t + 1) * P]
                    u.k = QK[part, 3 + g, j, keys[0] * P:keys[1] * P]
                    u.N = (keys[1] - keys[0]) * P
                    band = S.const("band")
                    u.mask = {0: band if t else band[:, P:], 1: band[:, P:], 2: S.const("every4")}[g]
                    u.vs = [V[:, g, kt, h * DH:(h + 1) * DH] for kt in range(*keys)]
                    u.low = stats[:, len(groups), 0, h:h + 1]
                    u.den = stats[:, len(groups), 1, h:h + 1]
                    gr.units.append(u)
                groups.append(gr)
        s_out = [S.sem("aa_out0"), S.sem("aa_out1")]
        s_back = S.s_og
        scratch = S.dram["scratch_a"]

        def finish(dve, gi, gr, bank, link):
            if gr.g:
                if gi >= 2:
                    dve.wait_ge(s_out[gi % 2], 16 * (gi // 2))
                dst = out[:, gi % 2, :]
            else:
                dst = OG[:, gr.t, 0, :]
            nc.vector.tensor_copy(dst[:, 0:WA], bank[:, :])
            return nc.vector.tensor_copy(dst[:, WA:].rearrange("p (s h) -> p s h", s=2), stats[:, gi, :, :])

        def moves(sp, s_fin):
            for gi, gr in enumerate(groups[:8]):
                sp.wait_ge(s_fin, gi + 1)
                sp.dma_start(dram_rows(scratch[gr.g - 1], gr.g, gr.t), out[:, gi % 2, :]).then_inc(s_out[gi % 2], 16)
            sp.wait_ge(s_out[0], 64)
            sp.wait_ge(s_out[1], 64)
            for t in range(TILES):
                sp.dma_start(OG[:, t, 1:3, :], scratch[:, t * P:(t + 1) * P, :].rearrange("g p c -> p g c")).then_inc(s_back, 16)

        attend_stage(S, "aa_", groups, finish, moves)


def merge_a_stage(S, OG, QK, V, Z, T, oT):
    nc = S.nc
    with ExitStack() as ctx:
        def sb(name, shape):
            return ctx.enter_context(nc.sbuf_tensor("ma_" + name, shape, F32))
        low = sb("low", [P, TILES, HA])
        diff = sb("diff", [P, TILES, 3, HA])
        wt = sb("weight", [P, TILES, 3, HA])
        wd = sb("weighted", [P, TILES, 3, HA])
        den = sb("den", [P, TILES, HA])
        rec = sb("rec", [P, TILES, HA])
        norm = sb("norm", [P, TILES, 3, HA])
        part = sb("part", [P, 3, WA])
        o = sb("o", [P, 2, WA])
        s_diff, s_wt, s_o, s_tr, s_ev, s_link = (S.sem("ma_" + n) for n in ("diff", "wt", "o", "tr", "ev", "link"))
        s_kept = S.sem("ma_kept")
        with S.block() as block:
            @block.gpsimd
            def _(pool):
                nc.gpsimd.tensor_copy(T.q[:, :, :, :], QK[:, 0:3, :, SEQ:TOK]).then_inc(s_kept, 1)
                nc.gpsimd.tensor_copy(T.k[:, :, :, :], QK[:, 3:6, :, SEQ:TOK]).then_inc(s_kept, 1)
                nc.gpsimd.tensor_copy(T.v[:, :, :], V[0:NS, :, TILES, :]).then_inc(s_kept, 1)
                nc.gpsimd.tensor_copy(T.z[:, :], Z[0:NS, TILES, :]).then_inc(s_kept, 1)
                pool.wait_ge(s_kept, 4)

            @block.vector
            def _(dve):
                link = linker(dve, s_link)
                dve.wait_ge(S.s_og, 16 * TILES)
                stat = OG[:, :, :, WA:]
                lows = [stat[:, :, g, 0:HA] for g in range(3)]
                link(nc.vector.tensor_tensor(low[:, :, :], lows[0], lows[1], ALU.min))
                link(nc.vector.tensor_tensor(low[:, :, :], low[:, :, :], lows[2], ALU.min))
                for g in range(3):
                    nc.vector.tensor_tensor(diff[:, :, g, :], low[:, :, :], lows[g], ALU.subtract).then_inc(s_diff, 1)
                dve.wait_ge(s_wt, 1)
                for g in range(3):
                    link(nc.vector.tensor_tensor(wd[:, :, g, :], wt[:, :, g, :], stat[:, :, g, HA:], ALU.mult))
                link(nc.vector.tensor_tensor(den[:, :, :], wd[:, :, 0, :], wd[:, :, 1, :], ALU.add))
                link(nc.vector.tensor_tensor(den[:, :, :], den[:, :, :], wd[:, :, 2, :], ALU.add))
                link(nc.vector.reciprocal(rec[:, :, :], den[:, :, :]))
                for g in range(3):
                    link(nc.vector.tensor_tensor(norm[:, :, g, :], wt[:, :, g, :], rec[:, :, :], ALU.mult))
                for t in range(TILES):
                    if t:
                        dve.wait_ge(s_o, t)
                    for g in range(3):
                        link(nc.vector.tensor_tensor(part[:, g, :].rearrange("p (h d) -> p h d", d=DH),
                                                     OG[:, t, g, 0:WA].rearrange("p (h d) -> p h d", d=DH),
                                                     norm[:, t, g, :].unsqueeze(2).broadcast_to((P, HA, DH)), ALU.mult))
                    link(nc.vector.tensor_tensor(part[:, 0, :], part[:, 0, :], part[:, 1, :], ALU.add))
                    link(nc.vector.tensor_tensor(part[:, 0, :], part[:, 0, :], part[:, 2, :], ALU.add))
                    if t >= 2:
                        dve.wait_ge(s_tr, t - 1)
                    nc.vector.tensor_tensor(o[:, t % 2, :], part[:, 0, :], Z[:, t, :], ALU.mult).then_inc(s_o, 1)

            @block.scalar
            def _(act):
                act.wait_ge(s_diff, 3)
                nc.scalar.activation(wt[:, :, :, :], diff[:, :, :, :], ACT.Exp).then_inc(s_wt, 1)
                for t in range(TILES):
                    act.wait_ge(s_tr, t + 1)
                    nc.scalar.activation(oT[:, 0:4, t * P:(t + 1) * P], S.banks[t % 2][:, :].rearrange("p (j r) -> p j r", j=4),
                                         ACT.Copy).then_inc(s_ev, 1)

            @block.tensor
            def _(pe):
                for t in range(TILES):
                    pe.wait_ge(s_o, t + 1)
                    if t >= 2:
                        pe.wait_ge(s_ev, t - 1)
                    for j in range(4):
                        ins = nc.tensor.transpose(S.banks[t % 2][:, j * P:(j + 1) * P], o[:, t % 2, j * P:(j + 1) * P], S.const("ident"))
                    ins.then_inc(s_tr, 1)


KTILES_A = 7


def sample_a_stage(S, T, oT):
    nc, A = S.nc, S.dram
    NK = KTILES_A * NB
    SLOTS = 3
    BLOCK = 4 * NB * 32
    COLS = 3 * P + 3 * NS
    with ExitStack() as ctx:
        def sb(name, shape):
            return ctx.enter_context(nc.sbuf_tensor("sa_" + name, shape, F32))
        ring = sb("cache", [P, SLOTS, KTILES_A, WA])
        qz = sb("q_padded", [P, 9 * BLOCK + 32])
        kT = sb("keys_turned", [P, 2, 4, P])
        masked = sb("masked", [P, COLS])
        probs = sb("probs", [P, 2, COLS])
        low, den, rec = (sb(n, [P, 2]) for n in ("low", "den", "rec"))
        pz = sb("p_padded", [P, 2, 7, P])
        pTn = sb("p_new_turned", [NS, 2, 3, P])
        out = sb("out", [P, WA])
        mask = sb("mask", [P, 2, COLS])
        zT = sb("z_t", [P, 4, NS])
        s_ring = [[S.sem(f"sa_ring{i}_{m}") for m in range(3)] for i in range(SLOTS)]
        s_mask = S.sem("sa_mask")
        s_zero, s_pzero, s_q, s_turn, s_mul, s_sc = (S.sem("sa_" + n) for n in ("zero", "pzero", "q", "turn", "mul", "scores_done"))
        s_ev = [S.sem("sa_ev0"), S.sem("sa_ev1")]
        s_low, s_exp, s_pt, s_ptc = (S.sem("sa_" + n) for n in ("low", "exp", "pt", "ptc"))
        s_pv, s_out, s_ot, s_o, s_zt, s_ztc = (S.sem("sa_" + n) for n in ("pv", "out", "out_turned", "o", "zt", "ztc"))
        B = S.banks

        def load(sp, m):
            kv, n = divmod(m, NB)
            slot = ring[:, m % SLOTS, :, :]
            sems = s_ring[m % SLOTS]
            c0, c1, c2 = (A[f"cache_dil_{g}"][0, n, :, kv].rearrange("r h d -> r (h d)") for g in range(3))
            sp.dma_start(slot[:, 0, :], c0).then_inc(sems[0], 16)
            sp.dma_start(slot[:, 1:1 + NT, :], c1.rearrange("(p t) e -> p t e", t=NT)).then_inc(sems[1], 16)
            c2 = c2.rearrange("(p c) e -> p c e", c=16)
            for half in range(2):
                sp.dma_start(slot[64 * half:64 * half + 64, 1 + NT:, :], c2[:, 2 * half:2 * half + 2, :]).then_inc(sems[2], 16)

        def landed(engine, m):
            for i, k in enumerate((1, 1, 2)):
                engine.wait_ge(s_ring[m % SLOTS][i], 16 * k * (m // SLOTS + 1))

        def variant(kk):
            return (0, 0) if kk == 0 else (2 + kk, 1) if kk <= NT else (2 + kk, 2)

        def queries(block, j, n):
            at = block * BLOCK + j * NB * 32 + n * 32
            return qz[:, at:at + 32]

        def pad_view(block, e):
            step = NB * 32 + 8
            v = qz[e * DH:(e + 1) * DH, block * BLOCK:block * BLOCK + 4 * step].rearrange("p (j s) -> p j s", s=step)
            return v[:, :, 0:NB * 32].rearrange("p j (n c) -> p j n c", c=32)[:, :, :, e * NT:(e + 1) * NT]

        def quad(n):
            return slice(32 * (n % 4), 32 * (n % 4) + 32)

        with S.block() as block:
            @block.sync
            def _(sp):
                for m in range(2 * NB):
                    if m >= SLOTS:
                        old = m - SLOTS
                        if old < NB:
                            sp.wait_ge(s_turn, KTILES_A * (old + 1))
                        else:
                            sp.wait_ge(s_pv, KTILES_A * (old + 1 - NB))
                    load(sp, m)
                    if m == 0:
                        a, b = S.where["a_mask"]
                        sp.dma_start(mask[:, :, :].rearrange("p b c -> p (b c)"), A["consts"][:, a:b]).then_inc(s_mask, 16)

            @block.gpsimd
            def _(pool):
                half = 9 * BLOCK // 2
                nc.gpsimd.memset(qz[:, 0:half], 0.0).then_inc(s_zero, 1)
                nc.gpsimd.memset(pz[:, :, :, :], 0.0).then_inc(s_pzero, 1)

            @block.tensor
            def _(pe):
                ident = S.const("ident")
                for j in range(4):
                    ins = nc.tensor.transpose(B[5][:, j * NS:(j + 1) * NS], T.z[:, j * P:(j + 1) * P], ident[0:NS, 0:NS])
                ins.then_inc(s_zt, 1)

                def turn(i):
                    n, kk = divmod(i, KTILES_A)
                    if kk == 0:
                        landed(pe, n)
                    if i >= 2:
                        pe.wait_ge(s_ev[i % 2], i // 2)
                    for j in range(4):
                        ins = nc.tensor.transpose(B[2 + i % 2][:, j * P:(j + 1) * P], ring[:, n % SLOTS, kk, j * P:(j + 1) * P], ident)
                    ins.then_inc(s_turn, 1)

                def multiply(i):
                    n, kk = divmod(i, KTILES_A)
                    q_block, g = variant(kk)
                    pe.wait_ge(s_ev[i % 2], i // 2 + 1)
                    for j in range(4):
                        ins = nc.tensor.matmul(B[n // 4][quad(n), g * P:(g + 1) * P], queries(q_block, j, n), kT[:, i % 2, j, :],
                                               start=(kk in (0, 1, 1 + NT) and j == 0), stop=(kk in (0, NT, NT + 2) and j == 3),
                                               skip_group_check=True)
                    ins.then_inc(s_mul, 1)

                def new_scores(b):
                    for n in range(4 * b, 4 * b + 4):
                        for g in range(3):
                            for j in range(4):
                                ins = nc.tensor.matmul(B[b][quad(n), 3 * P + g * NS:3 * P + (g + 1) * NS], queries(g, j, n),
                                                       T.k[:, g, j, :], start=(j == 0), stop=(j == 3), skip_group_check=True)
                    ins.then_inc(s_sc, 1)

                def turn_probs(b):
                    pe.wait_ge(s_exp, b + 1)
                    if b:
                        pe.wait_ge(s_ptc, 8)
                    for g in range(3):
                        nc.tensor.transpose(B[4][:, g * P:(g + 1) * P], probs[:, b, g * P:(g + 1) * P], ident)
                    if b == 0:
                        pe.wait_ge(s_ztc, 1)
                    for g in range(3):
                        ins = nc.tensor.transpose(B[5][0:NS, g * P:(g + 1) * P], probs[:, b, 3 * P + g * NS:3 * P + (g + 1) * NS], ident)
                    ins.then_inc(s_pt, 1)

                def values(n):
                    b = n // 4
                    landed(pe, n + NB)
                    for g in range(3):
                        nc.tensor.matmul(B[6 + b][quad(n), :], pTn[:, b, g, quad(n)], T.v[:, g, :], start=(g == 0), stop=False,
                                         skip_group_check=True)
                    for kk in range(KTILES_A):
                        nc.tensor.matmul(B[6 + b][quad(n), :], pz[:, b, kk, quad(n)], ring[:, (n + NB) % SLOTS, kk, :],
                                         start=False, stop=(kk == KTILES_A - 1), skip_group_check=True).then_inc(s_pv, 1)

                def turn_out(b):
                    pe.wait_ge(s_out, b + 1)
                    if b == 0:
                        pe.wait_ge(s_ptc, 16)
                    else:
                        pe.wait_ge(s_o, 8)
                    for j in range(4):
                        ins = nc.tensor.transpose(B[4][:, j * P:(j + 1) * P], out[:, j * P:(j + 1) * P], ident)
                    ins.then_inc(s_ot, 1)
                pe.wait_ge(s_q, 18)
                for i in range(NK + 1):
                    if i < NK:
                        turn(i)
                    if i:
                        multiply(i - 1)
                    if i == NK // 2:
                        new_scores(0)
                    if i == NK // 2 + 6:
                        turn_probs(0)
                new_scores(1)
                pe.wait_ge(s_ptc, 8)
                for n in range(2):
                    values(n)
                turn_probs(1)
                for n in range(2, 4):
                    values(n)
                pe.wait_ge(s_ptc, 16)
                values(4)
                turn_out(0)
                for n in range(5, 8):
                    values(n)
                turn_out(1)

            def evacuate(engine, i):
                engine.wait_ge(s_turn, i + 1)
                if i >= 2:
                    engine.wait_ge(s_mul, i - 1)
                src = B[2 + i % 2][:, :].rearrange("p (j r) -> p j r", j=4)
                if i % 2 == 0:
                    nc.vector.tensor_copy(kT[:, 0, :, :], src).then_inc(s_ev[0], 1)
                else:
                    nc.scalar.activation(kT[:, 1, :, :], src, ACT.Copy).then_inc(s_ev[1], 1)

            @block.scalar
            def _(act):
                act.wait_ge(s_zt, 1)
                nc.scalar.activation(zT[:, :, :], B[5][:, 0:4 * NS].rearrange("p (j r) -> p j r", j=4), ACT.Copy).then_inc(s_ztc, 1)

                def exp(b):
                    act.wait_ge(s_low, b + 1)
                    nc.scalar.activation(probs[:, b, :], masked[:, :], ACT.Exp, bias=low[:, b:b + 1], scale=-1.0,
                                         accum_out=den[:, b:b + 1]).then_inc(s_exp, 1)
                for i in range(1, NK, 2):
                    evacuate(act, i)
                    if i == NK // 2 + 3:
                        exp(0)
                exp(1)

            @block.vector
            def _(dve):
                nc.vector.memset(qz[:, 9 * BLOCK // 2:], 0.0).then_inc(s_zero, 1)
                dve.wait_ge(s_zero, 2)
                for e in range(2):
                    part = slice(e * DH, (e + 1) * DH)
                    src = [T.q[part, g, :, :].rearrange("p j (n t) -> p j n t", t=NT) for g in range(3)]
                    for g in range(3):
                        nc.vector.tensor_copy(pad_view(g, e), src[g]).then_inc(s_q, 1)
                    for t in range(NT):
                        nc.vector.tensor_copy(pad_view(3 + t, e)[:, :, :, t], src[1][:, :, :, t]).then_inc(s_q, 1)
                    for i in range(2):
                        nc.vector.tensor_copy(pad_view(7 + i, e)[:, :, :, i::2], src[2][:, :, :, i::2]).then_inc(s_q, 1)

                def soft(b):
                    dve.wait_ge(s_sc, b + 1)
                    dve.wait_ge(s_mask, 16)
                    if b:
                        dve.wait_ge(s_exp, b)
                    nc.vector.tensor_tensor_reduce(masked[:, :], B[b][:, 0:COLS], mask[:, b, :], -SCALE,
                                                   3e38, ALU.add, ALU.min, low[:, b:b + 1]).then_inc(s_low, 1)

                def copy_probs(b):
                    dve.wait_ge(s_pt, b + 1)
                    if b == 0:
                        dve.wait_ge(s_pzero, 1)
                    src = [B[4][:, g * P:(g + 1) * P].rearrange("p (n t) -> p n t", t=NT) for g in range(3)]
                    dst = [pz[:, b, kk, :].rearrange("p (n t) -> p n t", t=NT) for kk in range(KTILES_A)]
                    nc.vector.tensor_copy(pz[:, b, 0, :], B[4][:, 0:P]).then_inc(s_ptc, 1)
                    for t in range(NT):
                        nc.vector.tensor_copy(dst[1 + t][:, :, t], src[1][:, :, t]).then_inc(s_ptc, 1)
                    for i in range(2):
                        nc.vector.tensor_copy(dst[1 + NT + i][:, :, i::2], src[2][:, :, i::2]).then_inc(s_ptc, 1)
                    nc.vector.tensor_copy(pTn[:, b, :, :], B[5][0:NS, 0:3 * P].rearrange("p (g r) -> p g r", g=3)).then_inc(s_ptc, 1)
                    nc.vector.reciprocal(rec[:, b:b + 1], den[:, b:b + 1])
                for i in range(0, NK, 2):
                    evacuate(dve, i)
                    if i == NK // 2 + 2:
                        soft(0)
                    if i == NK // 2 + 8:
                        copy_probs(0)
                soft(1)
                copy_probs(1)
                for b in range(2):
                    dve.wait_ge(s_pv, KTILES_A * 4 * (b + 1))
                    if b:
                        dve.wait_ge(s_ot, b)
                    dve.wait_ge(s_ptc, 16)
                    nc.vector.tensor_scalar(out[:, :], B[6 + b][:, :], rec[:, b:b + 1], None, ALU.mult).then_inc(s_out, 1)
                    dve.wait_ge(s_ot, b + 1)
                    dve.wait_ge(s_ztc, 1)
                    for j in range(4):
                        for e in range(2):
                            part = slice(e * DH, (e + 1) * DH)
                            h = 2 * j + e
                            src = B[4][part, j * P:(j + 1) * P].rearrange("p (n c) -> p n c", n=4)[:, :, h * NT:(h + 1) * NT]
                            dst = oT[part, j, SEQ + 16 * b:SEQ + 16 * (b + 1)].rearrange("p (n t) -> p n t", t=NT)
                            z = zT[part, j, 16 * b:16 * (b + 1)].rearrange("p (n t) -> p n t", t=NT)
                            nc.vector.tensor_tensor(dst, src, z, ALU.mult).then_inc(s_o, 1)


def output_stage(S, pfx, oT, w_dram, nk, take):
    nc = S.nc
    with ExitStack() as ctx:
        W = ctx.enter_context(nc.sbuf_tensor(pfx + "w_out", [P, nk, D], F32))
        s_w, s_mm, s_y = S.sem(pfx + "w"), S.sem(pfx + "mm"), S.sem(pfx + "y")
        s_st = S.lasting_sem(pfx + "stored")
        with S.block() as block:
            @block.sync
            def _(sp):
                for dst, src in w_dram(W):
                    sp.dma_start(dst, src).then_inc(s_w, 16)
                if S.store_y:
                    for t in range(TILES + 1):
                        sp.wait_ge(s_y, 2 * t + 2)
                        sp.dma_start(S.store_y(t), S.x[0:rows_of(t), t, :]).then_inc(s_st, 16)
                    S.outs.append((s_st, 16 * (TILES + 1)))

            n_w = len(w_dram(W))

            @block.tensor
            def _(pe):
                pe.wait_ge(s_w, 16 * n_w)
                for v in range(2 * (TILES + 1)):
                    t, half = divmod(v, 2)
                    if v >= 4:
                        pe.wait_ge(s_y, v - 3)
                    for k in range(nk):
                        ins = nc.tensor.matmul(S.banks[v % 4][0:rows_of(t), :], oT[:, k, t * P:t * P + rows_of(t)],
                                               W[:, k, half * 512:half * 512 + 512], start=(k == 0), stop=(k == nk - 1))
                    ins.then_inc(s_mm, 1)

            @block.vector
            def _(dve):
                for v in range(2 * (TILES + 1)):
                    t, half = divmod(v, 2)
                    R = rows_of(t)
                    dve.wait_ge(s_mm, v + 1)
                    xs = S.x[0:R, t, half * 512:half * 512 + 512]
                    nc.vector.tensor_tensor(xs, S.banks[v % 4][0:R, :], xs, ALU.add).then_inc(s_y, 1)


def layer_a(S):
    nc, A = S.nc, S.dram
    with ExitStack() as ctx:
        def sb(name, shape, c=ctx):
            return c.enter_context(nc.sbuf_tensor("la_" + name, shape, F32))
        T = Unit()
        T.q = sb("s_q", [P, 3, 4, NS])
        T.z = sb("s_z", [NS, WA])
        hT = sb("hT", [P, KC, TOK])
        oT = hT[:, 0:4, :]
        rest = hT[:, 4:8, :].rearrange("p k r -> p (k r)")
        T.k = rest[:, 0:12 * NS].rearrange("p (g j r) -> p g j r", g=3, j=4)
        T.v = rest[0:NS, 12 * NS:12 * NS + 3 * WA].rearrange("p (g e) -> p g e", g=3)
        with ExitStack() as inner:
            QK = sb("qk", [P, 6, 4, TOK], inner)
            V = sb("v", [P, 3, TILES + 1, WA], inner)
            Z = sb("z", [P, TILES + 1, WA], inner)
            norm_stage(S, "na_", lambda e, t: e.wait_ge(S.s_x[t], 16), A["a_norm"], hT)
            project_a_stage(S, hT, QK, V, Z)
            S.s_og = S.lasting_sem("s_og")
            with nc.sbuf_tensor("la_og", [P, TILES, 3, WA + 2 * HA], F32) as OG:
                attend_a_stage(S, QK, V, OG)
                merge_a_stage(S, OG, QK, V, Z, T, oT)
        sample_a_stage(S, T, oT)
        S.store_y = None
        w = A["a_w_out"][0].rearrange("(k p) e -> p k e", p=P)
        output_stage(S, "oa_", oT, lambda W: [(W[:, :, :], w)], 4, None)


def project_b_stage(S, hT, QP, KT, ROWS, WINR, Z, GATES):
    nc, A = S.nc, S.dram
    w = A["b_w_in"][0].rearrange("(k p) e -> p k e", p=P)
    NG = 3 * HB
    cols = [(0, 512), (512, 512), (1024, 512), (1536, 512), (2048, 512), (2560, NG), (2560 + NG, 512), (3072 + NG, 512)]
    NC = len(cols)
    units = []
    for c in range(NC):
        for t in range(TILES + 1):
            u = Unit()
            u.c, u.t, u.g, u.R, u.v = c, t, 0, rows_of(t), len(units)
            u.q, u.kv = c < 2, 2 <= c < 5
            u.qk = u.q or u.kv
            u.i = u.v if u.qk else u.v - 25
            u.heads = 8 if u.q else 4
            u.ri = u.i if c < 2 else u.i - 5
            units.append(u)
    qk_units = units[:25]
    with ExitStack() as ctx:
        def sb(name, shape):
            return ctx.enter_context(nc.sbuf_tensor("pb_" + name, shape, F32))
        W = sb("w", [P, 2, KC, 512])
        gains = sb("gains", [P, 2, DH])
        tabs = sb("tables", [P, 2, 2, TILES + 1, DH])
        sq = sb("squares", [P, 512])
        ss, rstd = sb("square_sum", [P, 2, 8]), sb("rstd", [P, 2, 8])
        ms = sb("mean_square", [P, 8])
        normed = sb("normed", [P, 2, 512])
        straight = sb("straight", [P, 512])
        swapped = sb("swapped", [P, 512])
        plain = sb("plain", [P, 2, 512])
        rot = sb("rotated", [P, 2, 512])
        s_w = [S.sem(f"pb_w{i}") for i in range(2)]
        s_gains, s_tabs = S.sem("pb_gains"), S.sem("pb_tabs")
        s_u, s_lin, s_sq, s_ss, s_ms, s_rstd = (S.sem("pb_" + n) for n in ("u", "lin", "sq", "ss", "ms", "rstd"))
        s_n, s_st, s_sw, s_pl, s_rot, s_tr, s_ev, s_v = (S.sem("pb_" + n) for n in ("n", "st", "sw", "pl", "rot", "tr", "ev", "v"))
        S.s_rows_out = S.lasting_sem("pb_rows_out")
        s_win_out = S.lasting_sem("pb_win_out")
        U = S.banks[0:3]
        TP, TR = S.banks[3:5], S.banks[5:7]
        with S.block() as block:
            @block.sync
            def _(sp):
                for i, name in enumerate(("b_q_norm", "b_k_norm")):
                    sp.dma_start(gains[:, i, :], A[name].broadcast_to((P, DH))).then_inc(s_gains, 16)
                for c in range(2):
                    sp.dma_start(W[:, c, :, :], w[:, :, cols[c][0]:sum(cols[c])]).then_inc(s_w[c], 16)
                for c in range(NC):
                    if c + 2 < NC:
                        lo, n = cols[c + 2]
                        sp.wait_ge(s_u, 5 * (c + 1))
                        sp.dma_start(W[:, c % 2, :, 0:n], w[:, :, lo:lo + n]).then_inc(s_w[c % 2], 16)
                        copy_kept(S, sp, 3, [c])
                    if c in (3, 4):
                        for t in range(TILES + 1):
                            u = units[5 * c + t]
                            sp.wait_ge(s_rot, u.i + 1)
                            sp.wait_ge(s_v, u.i - 9)
                            if c == 3 and t < TILES:
                                sp.dma_start(A["new_rows_p"][0, 0, t * P:(t + 1) * P].rearrange("r s h d -> r (s h d)"),
                                             ROWS[:, t, :]).then_inc(S.s_rows_out, 16)
                            elif c == 3:
                                sp.dma_start(A["new_rows_s"][0].rearrange("n t s h d -> (n t) (s h d)"),
                                             ROWS[0:NS, t, :]).then_inc(S.s_rows_out, 16)
                            elif t < TILES:
                                sp.dma_start(A["new_win_p"][0, 0, t * P:(t + 1) * P].rearrange("r s h d -> r (s h d)"),
                                             WINR[:, t, :]).then_inc(s_win_out, 16)
                            else:
                                sp.dma_start(A["new_win_s"][0, :, WIN - NT:].rearrange("n t s h d -> n t (s h d)"),
                                             WINR[0:NS, t, :]).then_inc(s_win_out, 16)
                S.outs += [(S.s_rows_out, 80), (s_win_out, 80)]

            @block.tensor
            def _(pe):
                ident = S.const("ident")

                def turn(u):
                    pe.wait_ge(s_rot, u.i + 1)
                    if u.ri >= 2:
                        pe.wait_ge(s_ev, u.ri - 1)
                    if u.q:
                        pe.wait_ge(s_pl, 2 * (u.i + 1))
                        for bank, src in ((TP[u.ri % 2], plain), (TR[u.ri % 2], rot)):
                            for j in range(4):
                                ins = nc.tensor.transpose(bank[:, j * P:j * P + u.R], src[0:u.R, u.i % 2, j * P:(j + 1) * P],
                                                          ident[0:u.R, 0:u.R])
                    else:
                        src = ROWS[0:u.R, u.t, 512:768] if u.c == 3 else WINR[0:u.R, u.t, 0:256]
                        for j in range(2):
                            ins = nc.tensor.transpose(TR[u.ri % 2][:, j * P:j * P + u.R], src[:, j * P:(j + 1) * P],
                                                      ident[0:u.R, 0:u.R])
                    ins.then_inc(s_tr, 1)
                for u in units:
                    n = cols[u.c][1]
                    if u.t == 0:
                        pe.wait_ge(s_w[u.c % 2], 16 * (u.c // 2 + 1))
                    if u.v >= 3:
                        old = units[u.v - 3]
                        pe.wait_ge(s_n if old.qk else s_lin, old.i + 1)
                        if old.kv:
                            pe.wait_ge(s_v, old.i - 9)
                    for k in range(KC):
                        ins = nc.tensor.matmul(U[u.v % 3][0:u.R, 0:n], hT[:, k, u.t * P:u.t * P + u.R], W[:, u.c % 2, k, 0:n],
                                               start=(k == 0), stop=(k == KC - 1))
                    ins.then_inc(s_u, 1)
                    if u.v >= 2 and (units[u.v - 2].q or units[u.v - 2].c in (3, 4)):
                        turn(units[u.v - 2])

            @block.scalar
            def _(act):
                def evacuate(u):
                    act.wait_ge(s_tr, u.ri + 1)
                    tok = slice(u.t * P, u.t * P + u.R)
                    if u.q:
                        for var, bank in enumerate((TP, TR)):
                            ins = nc.scalar.activation(QP[:, var, 4 * u.c:4 * u.c + 4, tok],
                                                       bank[u.ri % 2][:, :].rearrange("p (j r) -> p j r", j=4)[:, :, 0:u.R], ACT.Copy)
                    else:
                        ins = nc.scalar.activation(KT[:, u.c - 3, :, tok],
                                                   TR[u.ri % 2][:, 0:2 * P].rearrange("p (j r) -> p j r", j=2)[:, :, 0:u.R], ACT.Copy)
                    ins.then_inc(s_ev, 1)
                for u in units:
                    act.wait_ge(s_u, u.v + 1)
                    src = U[u.v % 3]
                    n = cols[u.c][1]
                    if u.qk:
                        if u.i:
                            act.wait_ge(s_ss, u.i)
                        w_ = DH * u.heads
                        sq_ins = nc.scalar.activation(sq[0:u.R, 0:w_], src[0:u.R, 0:w_], ACT.Square)
                        if u.kv:
                            dst = {2: ROWS[0:u.R, u.t, 256:512], 3: ROWS[0:u.R, u.t, 768:1024], 4: WINR[0:u.R, u.t, 256:512]}[u.c]
                            nc.scalar.activation(dst, src[0:u.R, 256:512], ACT.Copy).then_inc(s_v, 1)
                        sq_ins.then_inc(s_sq, 1)
                    elif u.c == 5:
                        nc.scalar.activation(GATES[0:u.R, u.t, :], src[0:u.R, 0:n], ACT.Sigmoid).then_inc(s_lin, 1)
                    else:
                        dst = Z[0:u.R, u.t, (u.c - 6) * 512:(u.c - 5) * 512]
                        if u.t < TILES:
                            nc.scalar.activation(dst.rearrange("p (g k d) -> p k g d", g=GQA, d=DH),
                                                 src[0:u.R, :].rearrange("p (k g d) -> p k g d", g=GQA, d=DH), ACT.Silu).then_inc(s_lin, 1)
                        else:
                            nc.scalar.activation(dst, src[0:u.R, :], ACT.Silu).then_inc(s_lin, 1)
                    if u.v >= 2 and (units[u.v - 2].q or units[u.v - 2].c in (3, 4)):
                        evacuate(units[u.v - 2])

            @block.gpsimd
            def _(pool):
                for u in qk_units:
                    R, i, H = u.R, u.i, u.heads
                    pool.wait_ge(s_ss, i + 1)
                    if i:
                        pool.wait_ge(s_rstd, i)
                    nc.gpsimd.tensor_scalar(ms[0:R, 0:H], ss[0:R, i % 2, 0:H], 1.0 / DH, EPS, ALU.mult, ALU.add).then_inc(s_ms, 1)
                    pool.wait_ge(s_ms, i + 1)
                    nc.gpsimd.tensor_tensor(rstd[0:R, i % 2, 0:H], ms[0:R, 0:H], S.const("half_power")[0:R, 0:H], ALU.pow).then_inc(s_rstd, 1)
                    if u.c == 2:
                        continue
                    pool.wait_ge(s_n, i + 1)
                    if i == 0:
                        pool.wait_ge(s_tabs, 16)
                    if i:
                        pool.wait_ge(s_rot, i)
                    n3 = normed[0:R, i % 2, 0:DH * H].rearrange("p (h d) -> p h d", d=DH)
                    o3 = swapped[0:R, 0:DH * H].rearrange("p (h d) -> p h d", d=DH)
                    for lo in (0, HALF):
                        tab = tabs[0:R, 1 if u.kv else 0, 1, u.t, lo:lo + HALF].unsqueeze(1).broadcast_to((R, H, HALF))
                        nc.gpsimd.tensor_tensor(o3[:, :, lo:lo + HALF], n3[:, :, HALF - lo:DH - lo], tab, ALU.mult).then_inc(s_sw, 1)
                    if u.q:
                        if i >= 2:
                            pool.wait_ge(s_tr, i - 1)
                        gain = gains[0:R, 0, :].unsqueeze(1).broadcast_to((R, GQA, DH))
                        for k2 in range(2):
                            nc.gpsimd.tensor_tensor(plain[0:R, i % 2, :].rearrange("p (g k d) -> p k g d", g=GQA, d=DH)[:, k2],
                                                    n3[:, 4 * k2:4 * k2 + 4, :], gain, ALU.mult).then_inc(s_pl, 1)

            @block.vector
            def _(dve):
                dve.wait_ge(s_gains, 32)
                rope_tables(S, dve, s_tabs, gains, tabs, [(0, TILES, 0), (ROPE_SETS - 1, 1, TILES)])

                def first(u):
                    R, i, w_ = u.R, u.i, DH * u.heads
                    dve.wait_ge(s_sq, i + 1)
                    nc.vector.tensor_reduce(ss[0:R, i % 2, 0:u.heads], sq[0:R, 0:w_].rearrange("p (h d) -> p h d", d=DH), AX,
                                            ALU.add).then_inc(s_ss, 1)

                def second(u):
                    R, i, H = u.R, u.i, u.heads
                    w_ = DH * H
                    dve.wait_ge(s_rstd, i + 1)
                    n3 = normed[0:R, i % 2, 0:w_].rearrange("p (h d) -> p h d", d=DH)
                    dve.wait_ge(s_u, u.v + 1)
                    if u.kv:
                        dve.wait_ge(s_v, i - 9)
                    nc.vector.tensor_tensor(n3, U[u.v % 3][0:R, 0:w_].rearrange("p (h d) -> p h d", d=DH),
                                            rstd[0:R, i % 2, 0:H].unsqueeze(2).broadcast_to((R, H, DH)), ALU.mult).then_inc(s_n, 1)
                    dve.wait_ge(s_n, i + 1)
                    if u.c == 2:
                        gain = gains[0:R, 1, :].unsqueeze(1).broadcast_to((R, H, DH))
                        nc.vector.tensor_tensor(ROWS[0:R, u.t, 0:256].rearrange("p (h d) -> p h d", d=DH), n3, gain,
                                                ALU.mult).then_inc(s_rot, 1)
                        return
                    tab = tabs[0:R, 1 if u.kv else 0, 0, u.t, :].unsqueeze(1).broadcast_to((R, H, DH))
                    nc.vector.tensor_tensor(straight[0:R, 0:w_].rearrange("p (h d) -> p h d", d=DH), n3, tab, ALU.mult).then_inc(s_st, 1)
                    dve.wait_ge(s_st, u.ri + 1)
                    dve.wait_ge(s_sw, 2 * (u.ri + 1))
                    if u.q:
                        if i >= 2:
                            dve.wait_ge(s_tr, i - 1)
                        out = rot[0:R, i % 2, :].rearrange("p (g k d) -> p k g d", g=GQA, d=DH)
                        a = straight[0:R, :].rearrange("p (k g d) -> p k g d", g=GQA, d=DH)
                        b = swapped[0:R, :].rearrange("p (k g d) -> p k g d", g=GQA, d=DH)
                    else:
                        out = ROWS[0:R, u.t, 512:768] if u.c == 3 else WINR[0:R, u.t, 0:256]
                        a, b = straight[0:R, 0:256], swapped[0:R, 0:256]
                    nc.vector.tensor_tensor(out, a, b, ALU.add).then_inc(s_rot, 1)
                dve.wait_ge(s_tabs, 16)
                for i, u in enumerate(qk_units):
                    first(u)
                    if i:
                        second(qk_units[i - 1])
                second(qk_units[-1])


class Compress:

    def __init__(self, S, pfx, items, landed, KC_T, VC, banks, ctx):
        def sb(name, shape):
            return ctx.enter_context(S.nc.sbuf_tensor(pfx + name, shape, F32))
        self.S, self.items, self.landed, self.KC_T, self.VC = S, items, landed, KC_T, VC
        self.turned, self.hid_bank, self.tok_bank = banks
        self.nI = len(items)
        self.last = 2 * self.nI + 3
        CH = 16 * max(items)
        self.w1 = sb("w1", [P, 2, 2, 8, HID])
        self.w2 = sb("w2", [HID, 2, DH])
        self.pe_rows = sb("pe_rows", [2 * CSTRIDE, P])
        self.peT = sb("peT", [P, 2 * CSTRIDE])
        self.pe_hid = sb("pe_hidden", [HID, 2])
        self.gains = sb("gains", [P, 2, DH])
        self.gain = sb("gain", [P, 1])
        self.pages = sb("pages", [P, min(2, self.nI), max(items), 2, 512])
        self.chunksT = sb("chunks_turned", [P, 2, KVH, 8, CH])
        self.hid = sb("hidden", [HID, 2, KVH, CH])
        self.sq = sb("squares", [64, 256])
        self.ss, self.ms, self.rstd = (sb(n, [64, KVH]) for n in ("ss", "ms", "rstd"))
        self.kn = sb("keys", [64, 256])
        self.s_w, self.s_pg = S.sem(pfx + "w"), [S.sem(pfx + "pages0"), S.sem(pfx + "pages1")]
        names = ("tr", "hm", "hid", "w2", "sq", "ss", "ms", "rstd", "kn", "knt", "kc", "vc", "pre", "pe0", "pe1", "pe2")
        self.m = {n: S.sem(pfx + n) for n in names}
        self.s_ev = [S.sem(pfx + "copied_by_vector"), S.sem(pfx + "copied_by_scalar")]
        self.tus = [(it, kv, j, a) for it in range(self.nI) for kv in range(2) for j in range(2) for a in range(2)]

    def blocks(self, it):
        return 16 * self.items[it] - 1

    def load_weights(self, sp):
        A, s_w = self.S.dram, self.s_w
        for kv in range(2):
            for a in range(2):
                src = A["b_cmp_w1"][0, kv].rearrange("(m a) d e -> a d m e", a=2)[a]
                sp.dma_start(self.w1[a * DH:(a + 1) * DH, kv, :, :, :].rearrange("p r m e -> p (r m) e"), src).then_inc(s_w, 16)
        sp.dma_start(self.w2[:, :, :], A["b_cmp_w2"][0].rearrange("v e d -> e v d")).then_inc(s_w, 16)
        sp.dma_start(self.pe_rows[:, :], A["b_cmp_pe"][0].rearrange("v (m a) d -> (v m) (a d)", a=2)).then_inc(s_w, 16)
        for i in range(2):
            sp.dma_start(self.gains[:, i, :], A["b_k_norm"].broadcast_to((P, DH))).then_inc(s_w, 16)

    def pe_start(self, pe):
        nc, m, bank, ident = self.S.nc, self.m, self.hid_bank, self.S.const("ident")
        pe.wait_ge(self.s_w, 16 * 8)
        nc.tensor.transpose(bank[:, 0:32], self.pe_rows[:, :], ident[0:32, 0:32])
        nc.tensor.transpose(bank[:, 128:256], self.gains[:, :, :].rearrange("p a d -> p (a d)"), ident).then_inc(m["pe0"], 1)
        pe.wait_ge(m["pe1"], 2)
        for kv in range(2):
            for rm in range(16):
                ins = nc.tensor.matmul(bank[:, 256 + kv:257 + kv], self.w1[:, kv, rm // 8, rm % 8, :],
                                       self.peT[:, 16 * kv + rm:16 * kv + rm + 1], start=(rm == 0), stop=(rm == 15))
        ins.then_inc(m["pe2"], 1)

    def turn(self, pe, x):
        nc, it, kv, j, a = self.S.nc, *self.tus[x]
        if kv == 0 and j == 0 and a == 0:
            self.landed(pe, it, self.s_pg)
        if x:
            pe.wait_ge(self.s_ev[0], x)
            pe.wait_ge(self.s_ev[1], x)
        for pp in range(self.items[it]):
            src = self.pages[:, it % 2, pp, a, kv * 256 + j * P:kv * 256 + (j + 1) * P]
            ins = nc.tensor.transpose(self.turned[:, pp * P:(pp + 1) * P], src, self.S.const("ident"))
        ins.then_inc(self.m["tr"], 1)

    def hidden(self, pe, y, quarter):
        nc, m = self.S.nc, self.m
        it, kv = divmod(y, 2)
        nb = self.blocks(it)
        if quarter == 0:
            for e in range(2):
                pe.wait_ge(self.s_ev[e], 4 * (y + 1))
            if y:
                pe.wait_ge(m["hid"], y)
            else:
                pe.wait_ge(m["pre"], 1)
        for rm in range(4 * quarter, 4 * quarter + 4):
            off, mm = divmod(rm, 8)
            ins = nc.tensor.matmul(self.hid_bank[:, 0:KVH * nb], self.w1[:, kv, off, mm, :],
                                   self.chunksT[:, y % 2, :, mm, off:off + nb], start=(rm == 0), stop=(rm == 15))
        if quarter == 3:
            ins.then_inc(m["hm"], 1)

    def tokens(self, pe, y):
        nc, m = self.S.nc, self.m
        it, kv = divmod(y, 2)
        nb = self.blocks(it)
        pe.wait_ge(m["hid"], y + 1)
        if kv:
            pe.wait_ge(m["kn"], it + 1)
        elif it:
            pe.wait_ge(m["kc"], it)
        for k in range(KVH):
            ins = nc.tensor.matmul(self.tok_bank[0:nb, k * DH:(k + 1) * DH], self.hid[:, y % 2, k, 0:nb], self.w2[:, kv, :],
                                   start=True, stop=True)
        ins.then_inc(m["w2"], 1)

    def turn_keys(self, pe, it):
        nc, m = self.S.nc, self.m
        nb = self.blocks(it)
        pe.wait_ge(m["kn"], it + 1)
        pe.wait_ge(m["vc"], it + 1)
        for j in range(2):
            ins = nc.tensor.transpose(self.tok_bank[:, 256 + j * 64:256 + j * 64 + nb], self.kn[0:nb, j * P:(j + 1) * P],
                                      self.S.const("ident")[0:nb, 0:nb])
        ins.then_inc(m["knt"], 1)

    def pe_step(self, pe, y):
        nI = self.nI
        if y >= 4 and y % 2 == 0 and y // 2 - 2 < nI:
            self.turn_keys(pe, y // 2 - 2)
        for quarter in range(4):
            if 1 <= y < 2 * nI + 1:
                self.hidden(pe, y - 1, quarter)
            if y < 2 * nI:
                self.turn(pe, 4 * y + quarter)
        if 2 <= y < 2 * nI + 2:
            self.tokens(pe, y - 2)

    def copy_out(self, engine, x, k2):
        nc, it, kv, j, a = self.S.nc, *self.tus[x]
        y = 2 * it + kv
        engine.wait_ge(self.m["tr"], x + 1)
        if y >= 2:
            engine.wait_ge(self.m["hm"], y - 1)
        n = 16 * self.items[it]
        src = self.turned[k2 * DH:(k2 + 1) * DH, 0:8 * n].rearrange("p (c m) -> p m c", m=8)
        dst = self.chunksT[a * DH:(a + 1) * DH, y % 2, 2 * j + k2, :, 0:n]
        if k2 == 0:
            nc.vector.tensor_copy(dst, src).then_inc(self.s_ev[0], 1)
        else:
            nc.scalar.activation(dst, src, ACT.Copy).then_inc(self.s_ev[1], 1)

    def act_start(self, act):
        act.wait_ge(self.m["pe0"], 1)

    def silu(self, act, y):
        nc, m = self.S.nc, self.m
        it, kv = divmod(y, 2)
        nb = self.blocks(it)
        act.wait_ge(m["hm"], y + 1)
        if y == 0:
            act.wait_ge(m["pre"], 1)
        if y >= 2:
            act.wait_ge(m["w2"], y - 1)
        nc.scalar.activation(self.hid[:, y % 2, :, 0:nb], self.hid_bank[:, 0:KVH * nb].rearrange("p (k c) -> p k c", k=KVH),
                             ACT.Silu, bias=self.pe_hid[:, kv:kv + 1]).then_inc(m["hid"], 1)

    def act_finish(self, act, y):
        nc, m = self.S.nc, self.m
        it, kv = divmod(y, 2)
        nb = self.blocks(it)
        act.wait_ge(m["w2"], y + 1)
        if kv == 0:
            if it:
                act.wait_ge(m["ss"], it)
            nc.scalar.activation(self.sq[0:nb, :], self.tok_bank[0:nb, 0:256], ACT.Square).then_inc(m["sq"], 1)
        else:
            nc.scalar.activation(self.VC[0:nb, it, :], self.tok_bank[0:nb, 0:256], ACT.Copy).then_inc(m["vc"], 1)

    def act_step(self, act, y):
        nI = self.nI
        if y < 2 * nI:
            for x in range(4 * y, 4 * y + 4):
                self.copy_out(act, x, 1)
        if 1 <= y < 2 * nI + 1:
            self.silu(act, y - 1)
        if 2 <= y < 2 * nI + 2:
            self.act_finish(act, y - 2)

    def pool_program(self, pool):
        nc, m = self.S.nc, self.m
        for it in range(self.nI):
            nb = self.blocks(it)
            pool.wait_ge(m["ss"], it + 1)
            if it:
                pool.wait_ge(m["kn"], it)
            nc.gpsimd.tensor_scalar(self.ms[0:nb, :], self.ss[0:nb, :], 1.0 / DH, EPS, ALU.mult, ALU.add).then_inc(m["ms"], 1)
            pool.wait_ge(m["ms"], it + 1)
            nc.gpsimd.tensor_tensor(self.rstd[0:nb, :], self.ms[0:nb, :], self.S.const("half_power")[0:nb, 0:KVH],
                                    ALU.pow).then_inc(m["rstd"], 1)

    def dve_start(self, dve):
        nc, m, bank = self.S.nc, self.m, self.hid_bank
        dve.wait_ge(m["pe0"], 1)
        nc.vector.tensor_copy(self.peT[:, :], bank[:, 0:32]).then_inc(m["pe1"], 1)
        nc.vector.tensor_copy(self.gain[:, :], bank[:, 128:129]).then_inc(m["pe1"], 1)
        dve.wait_ge(m["pe2"], 1)
        nc.vector.tensor_copy(self.pe_hid[:, :], bank[:, 256:258]).then_inc(m["pre"], 1)

    def keys(self, dve, it):
        nc, m = self.S.nc, self.m
        nb = self.blocks(it)
        dve.wait_ge(m["sq"], it + 1)
        if it:
            dve.wait_ge(m["rstd"], it)
        nc.vector.tensor_reduce(self.ss[0:nb, :], self.sq[0:nb, :].rearrange("p (k d) -> p k d", d=DH), AX, ALU.add).then_inc(m["ss"], 1)
        dve.wait_ge(m["rstd"], it + 1)
        if it:
            dve.wait_ge(m["knt"], it)
        nc.vector.tensor_tensor(self.kn[0:nb, :].rearrange("p (k d) -> p k d", d=DH),
                                self.tok_bank[0:nb, 0:256].rearrange("p (k d) -> p k d", d=DH),
                                self.rstd[0:nb, :].unsqueeze(2).broadcast_to((nb, KVH, DH)), ALU.mult).then_inc(m["kn"], 1)

    def keep(self, dve, it):
        nb = self.blocks(it)
        dve.wait_ge(self.m["knt"], it + 1)
        src = self.tok_bank[:, 256:256 + P].rearrange("p (j c) -> p j c", j=2)[:, :, 0:nb]
        self.S.nc.vector.tensor_scalar(self.KC_T[:, it, :, 0:nb], src, self.gain[:, 0:1], None, ALU.mult).then_inc(self.m["kc"], 1)

    def dve_step(self, dve, y):
        if y >= 4 and y % 2 == 0 and y // 2 - 2 < self.nI:
            self.keep(dve, y // 2 - 2)
        if y < 2 * self.nI:
            for x in range(4 * y, 4 * y + 4):
                self.copy_out(dve, x, 0)
        if y >= 2 and y % 2 == 0 and y // 2 - 1 < self.nI:
            self.keys(dve, y // 2 - 1)


def attend_b_stage(S, QP, KT, ROWS, WINR, KC_P, VC_P, GATES, Z, oT):
    nc = S.nc
    assert SEQ // SELB <= 16 and SEQ <= WIN
    units = []
    for t in range(TILES):
        for j in range(2):
            for k2 in range(2):
                for br in range(3):
                    for g in range(GQA):
                        u = Unit()
                        u.t, u.j, u.k2, u.br, u.g, u.v = t, j, k2, br, g, len(units)
                        u.gi = u.v // GQA
                        u.tj = u.v // (6 * GQA)
                        u.rows = NCMP_P if br == 0 else P
                        u.chunks = 1 if br == 0 else t + 1
                        u.N = NCMP_P if br == 0 else (t + 1) * P
                        units.append(u)
    N, NTJ = len(units), 2 * TILES
    LAG = 3
    with ExitStack() as ctx:
        def sb(name, shape):
            return ctx.enter_context(nc.sbuf_tensor("ab_" + name, shape, F32))
        masked = sb("masked", [P, 2, SEQ])
        probs = sb("probs", [P, 3, SEQ])
        low, den, rec = sb("low", [P, 4]), sb("den", [P, 4]), sb("rec", [P, 4])
        pT = sb("probs_turned", [P, 2, TILES, GQA, P])
        s_gate, s_sc, s_m, s_e, s_p, s_tr, s_pv, s_z, s_fin = (
            S.sem("ab_" + n) for n in ("gate", "scores", "masked", "exp", "weighted", "turned", "pv", "z_turned", "finished"))
        s_rec, s_zc = S.sem("ab_rec"), S.sem("ab_z_copied")
        zT = sb("z_turned", [P, 512])
        s_ev = [S.sem("ab_copied_by_vector"), S.sem("ab_copied_by_scalar")]
        SC, TR, OB, ZB = S.banks[0:3], S.banks[3:5], S.banks[5:7], S.banks[7]

        def copy_out(engine, v):
            u = units[v]
            engine.wait_ge(s_tr, v + 1)
            if u.gi >= 2:
                engine.wait_ge(s_pv, u.gi - 1)
            src = TR[v % 2][0:u.rows, 0:u.chunks * P].rearrange("p (c q) -> p c q", q=P)
            dst = pT[0:u.rows, u.gi % 2, 0:u.chunks, u.g, :]
            if v % 2 == 0:
                nc.vector.tensor_copy(dst, src).then_inc(s_ev[0], 1)
            else:
                nc.scalar.activation(dst, src, ACT.Copy).then_inc(s_ev[1], 1)

        with S.block() as block:
            @block.sync
            def _(sp):
                copy_kept(S, sp, 3, [NB - 2, NB - 1])
                copy_kept(S, sp, 0, range(NB))
                for n in range(NB):
                    if n:
                        sp.wait_ge(s_fin, n)
                    copy_kept(S, sp, 2, [n])

            @block.tensor
            def _(pe):
                ident = S.const("ident")

                def scores(u):
                    part = slice(u.k2 * DH, (u.k2 + 1) * DH)
                    if u.v >= 3:
                        pe.wait_ge(s_m, u.v - 2)
                    keys = KT[part, u.br - 1, u.j, 0:u.N] if u.br else KC_P[part, 0, u.j, 0:NCMP_P]
                    nc.tensor.matmul(SC[u.v % 3][:, 0:u.N], QP[part, 1 if u.br else 0, 4 * u.j + u.g, u.t * P:(u.t + 1) * P],
                                     keys, start=True, stop=True).then_inc(s_sc, 1)

                def turn(u):
                    pe.wait_ge(s_p, u.v + 1)
                    if u.v >= 2:
                        pe.wait_ge(s_ev[u.v % 2], u.v // 2)
                    for c in range(u.chunks):
                        ins = nc.tensor.transpose(TR[u.v % 2][0:u.rows, c * P:(c + 1) * P], probs[:, u.v % 3, c * P:c * P + u.rows], ident)
                    ins.then_inc(s_tr, 1)

                def values(u):
                    for e in range(2):
                        pe.wait_ge(s_ev[e], 2 * (u.gi + 1))
                    if u.k2 == 0 and u.br == 0 and u.tj >= 2:
                        pe.wait_ge(s_fin, u.tj - 1)
                    col = slice((2 * u.j + u.k2) * DH, (2 * u.j + u.k2 + 1) * DH)
                    for c in range(u.chunks):
                        val = VC_P[0:NCMP_P, 0, col] if u.br == 0 else ROWS[:, c, 768:1024][:, col] if u.br == 1 else WINR[:, c, 256:512][:, col]
                        ins = nc.tensor.matmul(OB[u.tj % 2][u.k2 * DH:(u.k2 + 1) * DH, :], val,
                                               pT[0:u.rows, u.gi % 2, c, :, :].rearrange("p g q -> p (g q)"),
                                               start=(u.br == 0), stop=(u.br == 2 and c == u.chunks - 1))
                    ins.then_inc(s_pv, 1)

                def turn_z(tj):
                    t, j = divmod(tj, 2)
                    if tj:
                        pe.wait_ge(s_zc, tj)
                    for g in range(GQA):
                        ins = nc.tensor.transpose(ZB[:, g * P:(g + 1) * P], Z[:, t, 512 * j + g * P:512 * j + (g + 1) * P], ident)
                    ins.then_inc(s_z, 1)
                for v in range(N + LAG + 1):
                    if v < N:
                        scores(units[v])
                        if v % (6 * GQA) == 5 * GQA:
                            turn_z(units[v].tj)
                    if LAG <= v < N + LAG:
                        turn(units[v - LAG])
                    if v > LAG and (v - LAG - 1) % GQA == GQA - 1:
                        values(units[v - LAG - 1])

            @block.scalar
            def _(act):
                for v in range(N + LAG):
                    if v < N:
                        u = units[v]
                        act.wait_ge(s_m, v + 1)
                        if v >= 3:
                            act.wait_ge(s_tr, v - 2)
                        nc.scalar.activation(probs[:, v % 3, 0:u.N], masked[:, v % 2, 0:u.N], ACT.Exp, bias=low[:, v % 4:v % 4 + 1],
                                             scale=-1.0, accum_out=den[:, v % 4:v % 4 + 1]).then_inc(s_e, 1)
                    if v >= LAG and (v - LAG) % 2 == 1:
                        copy_out(act, v - LAG)
                    if v < N and v % (6 * GQA) == 6 * GQA - 1:
                        act.wait_ge(s_z, u.tj + 1)
                        if u.tj:
                            act.wait_ge(s_fin, u.tj)
                        nc.scalar.activation(zT[:, :], ZB[:, :], ACT.Copy).then_inc(s_zc, 1)

            @block.gpsimd
            def _(pool):
                pool.wait_ge(s_gate, TILES)
                for u in units:
                    h = 8 * u.j + 4 * u.k2 + u.g
                    gate = GATES[:, u.t, u.br * HB + h:u.br * HB + h + 1]
                    pool.wait_ge(s_rec, u.v + 1)
                    p = probs[:, u.v % 3, 0:u.N]
                    nc.gpsimd.tensor_scalar(p, p, rec[:, u.v % 4:u.v % 4 + 1], gate, ALU.mult, ALU.mult).then_inc(s_p, 1)

            @block.vector
            def _(dve):
                for t in range(TILES):
                    nc.vector.tensor_scalar(GATES[:, t, 0:HB], GATES[:, t, 0:HB], S.const("cmp_any")[:, t:t + 1], None,
                                            ALU.mult).then_inc(s_gate, 1)
                for v in range(N + 2 * LAG):
                    if v < N:
                        u = units[v]
                        mask = (S.const("causal")[:, (TILES - 1 - u.t) * P:] if u.br else
                                S.const("cmp_mask").rearrange("p (t c) -> p t c", t=TILES)[:, u.t, :])
                        dve.wait_ge(s_sc, v + 1)
                        if v >= 2:
                            dve.wait_ge(s_e, v - 1)
                        nc.vector.tensor_tensor_reduce(masked[:, v % 2, 0:u.N], SC[v % 3][:, 0:u.N], mask, -SCALE, 3e38,
                                                       ALU.add, ALU.min, low[:, v % 4:v % 4 + 1]).then_inc(s_m, 1)
                    if 1 <= v < N + 1:
                        i = (v - 1) % 4
                        dve.wait_ge(s_e, v)
                        nc.vector.reciprocal(rec[:, i:i + 1], den[:, i:i + 1]).then_inc(s_rec, 1)
                    if LAG <= v < N + LAG and (v - LAG) % 2 == 0:
                        copy_out(dve, v - LAG)
                    if v >= 6 * GQA + 5 and (v - 5) % (6 * GQA) == 0:
                        tj = (v - 5) // (6 * GQA) - 1
                        t, j = divmod(tj, 2)
                        dve.wait_ge(s_pv, 6 * (tj + 1))
                        dve.wait_ge(s_zc, tj + 1)
                        nc.vector.tensor_tensor(oT[:, 4 * j:4 * j + 4, t * P:(t + 1) * P], OB[tj % 2][:, :].rearrange("p (g r) -> p g r", g=GQA),
                                                zT[:, :].rearrange("p (g r) -> p g r", g=GQA), ALU.mult).then_inc(s_fin, 1)


def prepare_sample_b_stage(S, QP, KT, ROWS, WINR, Z, GATES, T):
    nc, A = S.nc, S.dram
    sem = {n: S.sem("pp_" + n) for n in ("zero", "q", "zt", "ztc", "rest", "gs", "gl")}
    z_rows = Z[0:NS, TILES, :]
    with S.block() as block:
        @block.gpsimd
        def _(pool):
            nc.gpsimd.memset(T.q[:, :, :, :, :, :, :], 0.0).then_inc(sem["zero"], 1)

        @block.sync
        def _(sp):
            sp.dma_start(A["scratch_gates"], GATES[0:NS, TILES, :]).then_inc(sem["gs"], 16)
            sp.wait_ge(sem["gs"], 16)
            for pair in range(NB // 2):
                for n2 in range(2):
                    r = (2 * pair + n2) * NT
                    sp.dma_start(T.gates[64 * n2:64 * n2 + 64, pair, :],
                                 A["scratch_gates"][r:r + NT].rearrange("t (b h) -> h t b", b=3),
                                 allow_slow_non_contiguous=True).then_inc(sem["gl"], 16)
            sp.wait_ge(sem["gl"], 16 * NB)

        @block.tensor
        def _(pe):
            for h in range(HB):
                ins = nc.tensor.transpose(S.banks[0][0:DH, h * NS:(h + 1) * NS], z_rows[:, h * DH:(h + 1) * DH],
                                          S.const("ident")[0:NS, 0:NS])
            ins.then_inc(sem["zt"], 1)

        @block.scalar
        def _(act):
            nc.scalar.activation(T.kT[:, :, :, :], KT[:, :, :, SEQ:TOK], ACT.Copy)
            nc.scalar.activation(T.v[:, 0, :], ROWS[0:NS, TILES, 768:1024], ACT.Copy)
            nc.scalar.activation(T.v[:, 1, :], WINR[0:NS, TILES, 256:512], ACT.Copy).then_inc(sem["rest"], 1)
            act.wait_ge(sem["zt"], 1)
            for k2 in range(2):
                src = S.banks[0][0:DH, :].rearrange("p (j k c) -> p j k c", j=2, k=2)[:, :, k2, :]
                nc.scalar.activation(T.zT[k2 * DH:(k2 + 1) * DH, :].rearrange("p (j c) -> p j c", j=2), src,
                                     ACT.Copy).then_inc(sem["ztc"], 1)
            act.wait_ge(sem["ztc"], 2)
            act.wait_ge(sem["rest"], 1)

        @block.vector
        def _(dve):
            dve.wait_ge(sem["zero"], 1)
            n = 0
            for var in range(2):
                for j in range(2):
                    for k2 in range(2):
                        part = slice(k2 * DH, (k2 + 1) * DH)
                        for s in range(NB):
                            nc.vector.tensor_copy(T.q[part, var, s, j, k2, :, :],
                                                  QP[part, var, 4 * j:4 * j + 4, SEQ + s * NT:SEQ + (s + 1) * NT]).then_inc(sem["q"], 1)
                            n += 1
            dve.wait_ge(sem["q"], n)


def sample_b_stage(S, T, KC_S, VC_S, oT):
    nc, A = S.nc, S.dram
    NPAIR = NB // 2
    SELW = PAST + NS
    WINW = WIN + NS
    NU = 12
    order = [u for n2 in range(2) for u in [(n2, 0, j, half) for j in range(2) for half in range(2)] + [(n2, 1, j, 0) for j in range(2)]]
    n_imp = NSEL_S - 3
    with ExitStack() as ctx:
        def sb(name, shape, dt=F32):
            return ctx.enter_context(nc.sbuf_tensor("sb_" + name, shape, dt))
        sel = sb("sel_pages", [P, 2, NPAGES, 512])
        win = sb("win_rows", [P, 2, 4, 512])
        kT = sb("keys_turned", [P, 2, 512])
        pc = sb("p_cmp", [P, 64])
        pcn = sb("p_cmp_plain", [P, 64])
        psel = sb("p_sel", [P, SELW])
        pwin = sb("p_win", [P, WINW])
        mx, low, den, rec, wt = (sb(n, [P, 3]) for n in ("max", "low", "den", "rec", "wt"))
        pcT = sb("p_cmp_turned", [64, 2, P])
        cov = sb("covered", [P, NSEL_S])
        small = sb("small", [P, 4, n_imp])
        least_imp = sb("least", [P, 2])
        bmask = sb("block_mask", [P, 16])
        pT = sb("p_turned", [P, 12, P])
        pTn = sb("p_new_turned", [NS, 2, P])
        s_sel, s_win = [S.sem("sb_sel0"), S.sem("sb_sel1")], [S.sem("sb_win0"), S.sem("sb_win1")]
        m = {n: S.sem("sb_" + n) for n in ("tr", "mul", "small", "cmpT", "cmpTc", "cov", "covc", "imp", "impc", "ecmp", "esel",
                                           "ewin", "lcmp", "lsel", "lwin", "ptr", "ptc", "pv", "o", "link", "pcmp", "psel", "pwin", "msk", "zero")}
        s_ev = [S.sem("sb_copied_by_vector"), S.sem("sb_copied_by_scalar")]
        B = S.banks

        def landed(pe, it, s_pg):
            pe.wait_ge(s_pg[it % 2], 16 * NPAGES * (it // 2 + 1))
        C = Compress(S, "cs_", [4] * NB, landed, KC_S, VC_S, (B[5], B[6], B[7]), ctx)
        HEAD = 7

        def interleave(phases, step):
            for y in range(HEAD):
                step(y)
            y = HEAD
            for pair in range(NPAIR):
                for i, phase in enumerate(phases):
                    phase(pair)
                    if i and y < C.last:
                        step(y)
                        y += 1
        ident = S.const("ident")
        new_mask = S.const("new_mask").rearrange("p (a c) -> p a c", a=NPAIR)

        with S.block() as block:
            @block.sync
            def _(sp):
                def page_rows(n, pg):
                    page = sp.value_load(S.page_table[0:1, n * NPAGES + pg:n * NPAGES + pg + 1], min_val=0, max_val=S.n_pool - 1)
                    return A["cache_nsa_paged"][0, bass.DynSlice(page, 1)]

                def load_cmp(n):
                    if n >= 2:
                        sp.wait_ge(C.m["tr"], 8 * (n - 1))
                    for pg in range(NPAGES):
                        src = page_rows(n, pg).rearrange("o (p a) s h d -> (o p) a (s h d)", a=2)
                        lo = 64 * (pg % 2)
                        sp.dma_start(C.pages[lo:lo + 64, n % 2, pg // 2, :, :], src[:, :, 0:512]).then_inc(C.s_pg[n % 2], 16)

                def load_sel(n):
                    if n >= 2:
                        sp.wait_ge(m["pv"], n // 2)
                    for pg in range(NPAGES):
                        src = page_rows(n, pg).rearrange("o r s h d -> (o r) (s h d)")
                        sp.dma_start(sel[:, n % 2, pg, :], src[:, 512:1024]).then_inc(s_sel[n % 2], 16)
                    sp.dma_start(win[:, n % 2, :, :], A["cache_nsa_win"][0, n].rearrange("(p a) s h d -> p a (s h d)", a=4)).then_inc(s_win[n % 2], 16)
                load_cmp(0)
                C.load_weights(sp)
                load_cmp(1)
                load_sel(0)
                load_sel(1)
                load_cmp(2)
                load_cmp(3)
                for pair in range(NPAIR):
                    for n in (2 * pair + 4, 2 * pair + 5):
                        if n < NB:
                            load_cmp(n)
                    for n in (2 * pair + 2, 2 * pair + 3):
                        if n < NB:
                            load_sel(n)

            @block.tensor
            def _(pe):
                def turn(x):
                    pair, u = divmod(x, NU)
                    n2, which, j, half = order[u]
                    if u == 0:
                        pe.wait_ge(s_sel[0], 128 * (pair + 1))
                    if u == 6:
                        pe.wait_ge(s_sel[1], 128 * (pair + 1))
                    if u in (4, 10):
                        pe.wait_ge(s_win[u // 6], 16 * (pair + 1))
                    if x:
                        pe.wait_ge(s_ev[(x - 1) % 2], (x - 1) // 2 + 1)
                    if u == 0 and pair:
                        pe.wait_ge(m["o"], 4 * pair)
                    for c in range(4):
                        src = win[:, n2, c, :] if which else sel[:, n2, 4 * half + c, :]
                        ins = nc.tensor.transpose(B[4][:, c * P:(c + 1) * P], src[:, j * P:(j + 1) * P], ident)
                    ins.then_inc(m["tr"], 1)

                def multiply(x):
                    pair, u = divmod(x, NU)
                    n2, which, j, half = order[u]
                    n = 2 * pair + n2
                    if u == 0 and pair:
                        pe.wait_ge(m["msk"], pair)
                    pe.wait_ge(s_ev[x % 2], x // 2 + 1)
                    rows = slice(64 * n2 + 32 * j, 64 * n2 + 32 * j + 32)
                    q = T.q[:, 1, n, j, :, :, :].rearrange("p k g t -> p (k g t)")
                    bank = B[2] if which else B[half]
                    nc.tensor.matmul(bank[rows, :], q, kT[:, x % 2, :], start=True, stop=True, skip_group_check=True).then_inc(m["mul"], 1)

                def small_scores(pair):
                    for n2 in range(2):
                        for j in range(2):
                            n = 2 * pair + n2
                            rows = slice(64 * n2 + 32 * j, 64 * n2 + 32 * j + 32)
                            q = T.q[:, 1, n, j, :, :, :].rearrange("p k g t -> p (k g t)")
                            qc = T.q[:, 0, n, j, :, :, :].rearrange("p k g t -> p (k g t)")
                            for which in range(2):
                                nc.tensor.matmul(B[3][rows, which * NS:(which + 1) * NS], q, T.kT[:, which, j, :], start=True,
                                                 stop=True, skip_group_check=True)
                            ins = nc.tensor.matmul(B[3][rows, 64:64 + NCMP_S], qc, KC_S[:, n, j, 0:NCMP_S], start=True, stop=True,
                                                   skip_group_check=True)
                    ins.then_inc(m["small"], 1)
                def scores(pair):
                    if pair:
                        pe.wait_ge(m["msk"], pair)
                    pe.wait_ge(C.m["kc"], 2 * pair + 2)
                    small_scores(pair)
                    for u in range(NU + 1):
                        if u < NU:
                            turn(NU * pair + u)
                        if u:
                            multiply(NU * pair + u - 1)
                        if u == 4:
                            pe.wait_ge(m["pcmp"], 2 * pair + 2)
                            nc.tensor.transpose(B[3][0:NCMP_S, 128:256], pcn[:, 0:NCMP_S], ident)
                            nc.tensor.transpose(B[3][0:NCMP_S, 256:384], pc[:, 0:NCMP_S], ident).then_inc(m["cmpT"], 1)
                        if u == 6:
                            pe.wait_ge(m["cmpTc"], pair + 1)
                            nc.tensor.matmul(B[3][:, 384:384 + NSEL_S], pcT[0:NCMP_S, 0, :], S.const("cover")[0:NCMP_S, :],
                                             start=True, stop=True).then_inc(m["cov"], 1)
                        if u == 8:
                            pe.wait_ge(m["covc"], pair + 1)
                            nc.tensor.matmul(B[3][:, 416:416 + NSEL_S], S.const("group_sum"), cov[:, :], start=True,
                                             stop=True).then_inc(m["imp"], 1)

                def turns(pair):
                    pe.wait_ge(m["psel"], pair + 1)
                    for c in range(8):
                        nc.tensor.transpose(B[c // 4][:, (c % 4) * P:(c % 4 + 1) * P], psel[:, c * P:(c + 1) * P], ident)
                    pe.wait_ge(m["pwin"], pair + 1)
                    nc.tensor.transpose(B[3][0:NS, 128:256], psel[:, PAST:], ident)
                    nc.tensor.transpose(B[3][0:NS, 256:384], pwin[:, WIN:], ident)
                    for c in range(4):
                        ins = nc.tensor.transpose(B[2][:, c * P:(c + 1) * P], pwin[:, c * P:(c + 1) * P], ident)
                    ins.then_inc(m["ptr"], 1)

                def output(pair):
                    pe.wait_ge(m["ptc"], 4 * (pair + 1))
                    pe.wait_ge(C.m["vc"], 2 * pair + 2)
                    for e in range(2):
                        pe.wait_ge(s_ev[e], NU // 2 * (pair + 1))
                    for n2 in range(2):
                        n = 2 * pair + n2
                        for j in range(2):
                            cols = slice(64 * n2 + 32 * j, 64 * n2 + 32 * j + 32)
                            vcol = slice(j * P, (j + 1) * P)
                            prods = [(VC_S[0:NCMP_S, n, vcol], pcT[0:NCMP_S, 1, cols])]
                            prods += [(sel[:, n2, c, 256 + j * P:256 + (j + 1) * P], pT[:, c, cols]) for c in range(8)]
                            prods += [(win[:, n2, c, 256 + j * P:256 + (j + 1) * P], pT[:, 8 + c, cols]) for c in range(4)]
                            prods += [(T.v[:, which, vcol], pTn[:, which, cols]) for which in range(2)]
                            for i, (v, p) in enumerate(prods):
                                ins = nc.tensor.matmul(B[4][:, cols], v, p, start=(i == 0), stop=(i == len(prods) - 1))
                    ins.then_inc(m["pv"], 1)
                C.pe_start(pe)
                interleave((scores, lambda pair: None, lambda pair: None, turns, output), lambda y: C.pe_step(pe, y))

            def evacuate(engine, x):
                engine.wait_ge(m["tr"], x + 1)
                if x >= 2:
                    engine.wait_ge(m["mul"], x - 1)
                if x % 2 == 0:
                    nc.vector.tensor_copy(kT[:, 0, :], B[4][:, :]).then_inc(s_ev[0], 1)
                else:
                    nc.scalar.activation(kT[:, 1, :], B[4][:, :], ACT.Copy).then_inc(s_ev[1], 1)

            @block.scalar
            def _(act):
                def scores(pair):
                    act.wait_ge(m["lcmp"], pair + 1)
                    if pair:
                        act.wait_ge(m["ptr"], pair)
                    nc.scalar.activation(pc[:, 0:NCMP_S], B[3][:, 64:64 + NCMP_S], ACT.Exp, bias=low[:, 0:1], scale=SCALE,
                                         accum_out=den[:, 0:1]).then_inc(m["ecmp"], 1)
                    for u in range(1, NU, 2):
                        evacuate(act, NU * pair + u)

                def least(pair):
                    act.wait_ge(m["lsel"], pair + 1)
                    nc.scalar.activation(psel[:, :], psel[:, :], ACT.Exp, bias=low[:, 1:2], scale=SCALE,
                                         accum_out=den[:, 1:2]).then_inc(m["esel"], 1)
                    act.wait_ge(m["lwin"], pair + 1)
                    nc.scalar.activation(pwin[:, :], pwin[:, :], ACT.Exp, bias=low[:, 2:3], scale=SCALE,
                                         accum_out=den[:, 2:3]).then_inc(m["ewin"], 1)

                def turns(pair):
                    act.wait_ge(m["ptr"], pair + 1)
                    if pair:
                        act.wait_ge(m["pv"], pair)
                    nc.scalar.activation(pT[:, 4:8, :], B[1][:, :].rearrange("p (c r) -> p c r", c=4), ACT.Copy).then_inc(m["ptc"], 1)
                    nc.scalar.activation(pT[:, 8:12, :], B[2][:, :].rearrange("p (c r) -> p c r", c=4), ACT.Copy).then_inc(m["ptc"], 1)
                C.act_start(act)
                interleave((scores, least, lambda pair: None, turns, lambda pair: None), lambda y: C.act_step(act, y))

            @block.gpsimd
            def _(pool):
                C.pool_program(pool)

            @block.vector
            def _(dve):
                link = linker(dve, m["link"])
                link(nc.vector.memset(bmask[:, :], 0.0))

                def lowest(src, i, sem):
                    link(nc.vector.tensor_reduce(mx[:, i:i + 1], src, AX, ALU.max))
                    nc.vector.tensor_scalar(low[:, i:i + 1], mx[:, i:i + 1], -SCALE, None, ALU.mult).then_inc(sem, 1)

                def weigh(pair, i):
                    link(nc.vector.reciprocal(rec[:, i:i + 1], den[:, i:i + 1]))
                    link(nc.vector.tensor_tensor(wt[:, i:i + 1], rec[:, i:i + 1], T.gates[:, pair, i:i + 1], ALU.mult))
                def scores(pair):
                    dve.wait_ge(m["small"], pair + 1)
                    lowest(B[3][:, 64:64 + NCMP_S], 0, m["lcmp"])
                    dve.wait_ge(m["ecmp"], pair + 1)
                    weigh(pair, 0)
                    if pair:
                        dve.wait_ge(m["pv"], pair)
                    nc.vector.tensor_scalar(pcn[:, 0:NCMP_S], pc[:, 0:NCMP_S], rec[:, 0:1], None, ALU.mult).then_inc(m["pcmp"], 1)
                    nc.vector.tensor_scalar(pc[:, 0:NCMP_S], pc[:, 0:NCMP_S], wt[:, 0:1], None, ALU.mult).then_inc(m["pcmp"], 1)
                    for u in range(0, NU, 2):
                        evacuate(dve, NU * pair + u)
                        if u == 4:
                            dve.wait_ge(m["cmpT"], pair + 1)
                            nc.vector.tensor_copy(pcT[0:NCMP_S, :, :], B[3][0:NCMP_S, 128:384].rearrange("p (a r) -> p a r", a=2)
                                                  ).then_inc(m["cmpTc"], 1)
                        if u == 6:
                            dve.wait_ge(m["cov"], pair + 1)
                            nc.vector.tensor_copy(cov[:, :], B[3][:, 384:384 + NSEL_S]).then_inc(m["covc"], 1)
                        if u == 8:
                            dve.wait_ge(m["imp"], pair + 1)
                            ids = S.const("block_id")
                            link(nc.vector.tensor_copy(small[:, 0, :], B[3][:, 417:417 + n_imp]))
                            link(nc.vector.tensor_reduce(least_imp[:, 0:1], small[:, 0, :], AX, ALU.min))
                            link(nc.vector.scalar_tensor_tensor(out=small[:, 1, :], in0=small[:, 0, :], scalar=least_imp[:, 0:1],
                                                                in1=ids, op0=ALU.is_equal, op1=ALU.mult))
                            link(nc.vector.tensor_reduce(least_imp[:, 1:2], small[:, 1, :], AX, ALU.max))
                            link(nc.vector.tensor_scalar(bmask[:, 1:1 + n_imp], ids, least_imp[:, 1:2], NEG, ALU.is_equal, ALU.mult))

                def least(pair):
                    dve.wait_ge(m["mul"], NU * (pair + 1))
                    for half in range(2):
                        link(nc.vector.tensor_tensor(psel[:, half * 512:(half + 1) * 512].rearrange("p (b k) -> p b k", k=SELB),
                                                     B[half][:, :].rearrange("p (b k) -> p b k", k=SELB),
                                                     bmask[:, 8 * half:8 * half + 8].unsqueeze(2).broadcast_to((P, 8, SELB)), ALU.add))
                    link(nc.vector.tensor_tensor(psel[:, PAST:], B[3][:, 0:NS], new_mask[:, pair, :], ALU.add))
                    lowest(psel[:, :], 1, m["lsel"])
                    link(nc.vector.tensor_tensor(pwin[:, 0:WIN], B[2][:, :], S.const("win_mask"), ALU.add))
                    link(nc.vector.tensor_tensor(pwin[:, WIN:], B[3][:, NS:2 * NS], new_mask[:, pair, :], ALU.add))
                    lowest(pwin[:, :], 2, m["lwin"])

                def weights(pair):
                    dve.wait_ge(m["lwin"], pair + 1)
                    dve.wait_ge(m["esel"], pair + 1)
                    weigh(pair, 1)
                    nc.vector.tensor_scalar(psel[:, :], psel[:, :], wt[:, 1:2], None, ALU.mult).then_inc(m["psel"], 1)
                    dve.wait_ge(m["ewin"], pair + 1)
                    weigh(pair, 2)
                    nc.vector.tensor_scalar(pwin[:, :], pwin[:, :], wt[:, 2:3], None, ALU.mult).then_inc(m["pwin"], 1)

                def turns(pair):
                    dve.wait_ge(m["ptr"], pair + 1)
                    if pair:
                        dve.wait_ge(m["pv"], pair)
                    nc.vector.tensor_copy(pT[:, 0:4, :], B[0][:, :].rearrange("p (c r) -> p c r", c=4)).then_inc(m["ptc"], 1)
                    nc.vector.tensor_copy(pTn[:, :, :], B[3][0:NS, 128:384].rearrange("p (a r) -> p a r", a=2)).then_inc(m["ptc"], 1)
                    dve.wait_ge(m["ptc"], 4 * (pair + 1))
                    nc.vector.memset(least_imp[:, 0:1], 0.0).then_inc(m["msk"], 1)

                def output(pair):
                    dve.wait_ge(m["msk"], pair + 1)
                    dve.wait_ge(m["pv"], pair + 1)
                    src = B[4][:, 0:P].rearrange("p (n j k g t) -> p n j k g t", n=2, j=2, k=2, g=GQA)
                    for j in range(2):
                        for k2 in range(2):
                            part = slice(k2 * DH, (k2 + 1) * DH)
                            cols = slice(SEQ + 2 * pair * NT, SEQ + 2 * (pair + 1) * NT)
                            out = oT[part, 4 * j:4 * j + 4, cols].rearrange("p g (n t) -> p n g t", n=2)
                            z = T.zT[part, :].rearrange("p (j g r) -> p j g r", j=2, g=GQA)[:, j, :, 2 * pair * NT:2 * (pair + 1) * NT]
                            nc.vector.tensor_tensor(out, src[part, :, j, k2, :, :], z.rearrange("p g (n t) -> p n g t", n=2),
                                                    ALU.mult).then_inc(m["o"], 1)
                C.dve_start(dve)
                interleave((scores, least, weights, turns, output), lambda y: C.dve_step(dve, y))


def compress_prompt_stage(S, KC_P, VC_P):
    A = S.dram

    def landed(pe, it, s_pg):
        pe.wait_ge(s_pg[0], 16 * (SEQ // PAGE))
    with ExitStack() as ctx:
        C = Compress(S, "cp_", [2], landed, KC_P, VC_P, (S.banks[0], S.banks[1], S.banks[2]), ctx)
        with S.block() as block:
            @block.sync
            def _(sp):
                C.load_weights(sp)
                sp.wait_ge(S.s_rows_out, 16 * (TILES + 1))
                rows = A["new_rows_p"][0, 0].rearrange("(b p a) s h d -> b p a (s h d)", a=2, p=64)
                for b in range(SEQ // PAGE):
                    lo = 64 * (b % 2)
                    sp.dma_start(C.pages[lo:lo + 64, 0, b // 2, :, :], rows[b, :, :, 0:512]).then_inc(C.s_pg[0], 16)

            @block.tensor
            def _(pe):
                C.pe_start(pe)
                for y in range(C.last):
                    C.pe_step(pe, y)

            @block.scalar
            def _(act):
                C.act_start(act)
                for y in range(C.last):
                    C.act_step(act, y)

            @block.gpsimd
            def _(pool):
                C.pool_program(pool)

            @block.vector
            def _(dve):
                C.dve_start(dve)
                for y in range(C.last):
                    C.dve_step(dve, y)


def layer_b(S):
    nc, A = S.nc, S.dram
    with ExitStack() as ctx:
        def sb(name, shape, c=ctx):
            return c.enter_context(nc.sbuf_tensor("lb_" + name, shape, F32))
        oT = sb("oT", [P, KC, TOK])
        T = Unit()
        T.q = sb("s_q", [P, 2, NB, 2, 2, GQA, NT])
        T.kT = sb("s_kT", [P, 2, 2, NS])
        T.v = sb("s_v", [NS, 2, 256])
        T.zT = sb("s_zT", [P, 2 * GQA * NS])
        T.gates = sb("s_gates", [P, NB // 2, 3])
        with ExitStack() as inner:
            KT = sb("kT", [P, 2, 2, TOK], inner)
            ROWS = sb("rows", [P, TILES + 1, 1024], inner)
            WINR = sb("win", [P, TILES + 1, 512], inner)
            Z = sb("z", [P, TILES + 1, D], inner)
            GATES = sb("gates", [P, TILES + 1, 3 * HB], inner)
            QP = sb("qp", [P, 2, 8, TOK], inner)
            norm_stage(S, "nb_", lambda e, t: None, A["b_norm"], oT)
            project_b_stage(S, oT, QP, KT, ROWS, WINR, Z, GATES)
            prepare_sample_b_stage(S, QP, KT, ROWS, WINR, Z, GATES, T)
            KC_P = sb("kc_p", [P, 1, 2, 64], inner)
            VC_P = sb("vc_p", [64, 1, 256], inner)
            compress_prompt_stage(S, KC_P, VC_P)
            attend_b_stage(S, QP, KT, ROWS, WINR, KC_P, VC_P, GATES, Z, oT)
        KC_S = sb("kc_s", [P, NB, 2, 64])
        VC_S = sb("vc_s", [64, NB, 256])
        sample_b_stage(S, T, KC_S, VC_S, oT)
        S.store_y = lambda t: A["y_p"][0, t * P:(t + 1) * P, :] if t < TILES else A["y_s"].rearrange("n t d -> (n t) d")
        w = A["b_w_out"][0].rearrange("(j k g d) e -> j k d g e", j=2, k=2, g=GQA)
        output_stage(S, "ob_", oT, lambda W: [(W[k2 * DH:(k2 + 1) * DH, 4 * j:4 * j + 4, :], w[j, k2])
                                              for j in range(2) for k2 in range(2)], KC, None)


def finish_stage(S):
    with S.nc.Block() as block:
        @block.sync
        def _(sp):
            for sem, value in S.outs + [(S.s_copy, S.n_copy)]:
                if value:
                    sp.wait_ge(sem, value)


def program(nc, dram, where, n_const):
    with ExitStack() as ctx:
        S = Stage(nc, dram, where, ctx)
        S.consts = ctx.enter_context(nc.sbuf_tensor("consts", [P, n_const], F32))
        S.x = ctx.enter_context(nc.sbuf_tensor("x", [P, TILES + 1, D], F32))
        S.page_table = ctx.enter_context(nc.sbuf_tensor("page_table", [1, NB * NPAGES], I32))
        S.n_pool = dram["cache_nsa_paged"].shape[1]
        S.banks = [ctx.enter_context(nc.psum_tensor(f"bank{i}", [P, 512], F32)) for i in range(8)]
        load_stage(S)
        layer_a(S)
        layer_b(S)
        finish_stage(S)


_INS = ["x_prompt", "x_sample", "cache_dil_0", "cache_dil_1", "cache_dil_2", "cache_nsa_paged", "cache_nsa_win", "page_table",
        "a_norm", "a_w_in", "a_q_norm", "a_k_norm", "a_w_out", "b_norm", "b_w_in", "b_q_norm", "b_k_norm", "b_cmp_pe",
        "b_cmp_w1", "b_cmp_w2", "b_w_out"]
_OUTS = [("y_p", (1, SEQ, D)), ("y_s", (NB, NT, D)),
         ("new_dil_0_p", (1, 1, 128, 2, HA, DH)), ("new_dil_1_p", (1, 1, 512, 2, HA, DH)), ("new_dil_2_p", (1, 1, 512, 2, HA, DH)),
         ("new_rows_p", (1, 1, SEQ, 4, KVH, DH)), ("new_win_p", (1, 1, SEQ, 2, KVH, DH)),
         ("new_dil_0_s", (1, NB, 128, 2, HA, DH)), ("new_dil_1_s", (1, NB, 512, 2, HA, DH)),
         ("new_dil_2_s", (1, NB, PAST + NT, 2, HA, DH)),
         ("new_rows_s", (1, NB, NT, 4, KVH, DH)), ("new_win_s", (1, NB, WIN, 2, KVH, DH))]


def kernel(**inputs):
    import numpy as _np
    import concourse.bacc as _bacc
    from concourse import mybir as _mybir
    from concourse.bass_utils import run_bass_kernel_spmd as _run

    nc = _bacc.Bacc("TRN2", target_bir_lowering=False, num_devices=1)
    arrays, dram = {}, {}
    table, where = constants()
    for name in _INS + ["consts"]:
        a = table if name == "consts" else _np.ascontiguousarray(inputs[name])
        arrays[f"in_{name}"] = a
        dram[name] = nc.dram_tensor(f"in_{name}", a.shape, _mybir.dt.from_np(a.dtype), kind="ExternalInput").ap()
    for name, shape in _OUTS:
        dram[name] = nc.dram_tensor(f"out_{name}", shape, _mybir.dt.float32, kind="ExternalOutput").ap()
    dram["scratch_gates"] = nc.dram_tensor("scratch_gates", (NS, 3 * HB), _mybir.dt.float32, kind="Internal").ap()
    dram["scratch_a"] = nc.dram_tensor("scratch_a", (2, SEQ, WA + 2 * HA), _mybir.dt.float32, kind="Internal").ap()
    program(nc, dram, where, where["a_mask"][0])
    r = _run(nc, [arrays], core_ids=[0])
    return tuple(r.results[0][f"out_{name}"] for name, _ in _OUTS)
```

```python
from contextlib import ExitStack, contextmanager

import numpy as np

import concourse.bass as bass
from concourse import mybir

ALU = mybir.AluOpType
ACT = mybir.ActivationFunctionType
F32 = mybir.dt.float32
I32 = mybir.dt.int32
AX = mybir.AxisListType.X

P = 128
D = 1024
SEQ = 512
NB = 8
NT = 4
NS = NB * NT
TOK = SEQ + NS
TILES = SEQ // P
DH = 64
HALF = DH // 2
SCALE = DH ** -0.5
EPS = 1e-6
KC = D // P
PATTERNS = ((128, 1), (512, 4), (2048, 16))
HA = 8
WA = HA * DH
HB = 16
KVH = 4
GQA = HB // KVH
PAST = 1024
PAGE = 128
NPAGES = PAST // PAGE
WIN = 512
CSTRIDE = 16
CLEN = 32
NCMP_P = (SEQ - CLEN) // CSTRIDE + 1
NCMP_S = (PAST + NT - CLEN) // CSTRIDE + 1
SELB = 64
NSEL_S = -(-(PAST + NT) // SELB)
HID = 128
NEG = -1e30
ROPE_SETS = 2 * TILES + 1


def rows_of(t):
    return P if t < TILES else NS


def token_of(g, t, p):
    return TILES * p + t if g else t * P + p


def constants():
    f = np.float32
    parts = {}
    parts["ident"] = np.eye(P, dtype=f)
    inv = (f(10000.0) ** (-np.arange(HALF, dtype=f) / f(HALF))).astype(f)
    pos = np.zeros((P, ROPE_SETS), f)
    for g in range(2):
        for t in range(TILES):
            pos[:, g * TILES + t] = [token_of(g, t, p) for p in range(P)]
    pos[:NS, ROPE_SETS - 1] = [PAST + r % NT for r in range(NS)]
    ang = pos[:, :, None] * inv[None, None, :]
    c, s = np.cos(ang).astype(f), np.sin(ang).astype(f)
    parts["cos"] = np.concatenate([c, c], -1)
    parts["sin"] = np.concatenate([-s, s], -1)
    q, k = np.arange(P)[:, None], np.arange(P)[None, :]
    causal = np.where(k <= q, 0, NEG).astype(f)
    parts["causal"] = np.concatenate([np.zeros((P, 3 * P), f), causal], 1)
    end = np.arange(NCMP_P) * CSTRIDE + CLEN - 1
    tok = np.arange(TILES)[None, :] * P + np.arange(P)[:, None]
    parts["cmp_mask"] = np.where(end[None, None, :] <= tok[:, :, None], 0, NEG).astype(f)
    parts["cmp_any"] = (tok >= CLEN - 1).astype(f)
    t = (np.arange(P) % NT)[:, None]
    n2 = (np.arange(P) // 64)[:, None]
    s = (np.arange(WIN) % P * 4 + np.arange(WIN) // P)[None, :]
    parts["win_mask"] = np.where(s >= t, 0, NEG).astype(f)
    new = np.arange(NS)[None, None, :]
    pair = np.arange(NB // 2)[None, :, None]
    parts["new_mask"] = np.where((new // NT == 2 * pair + n2[:, :, None]) & (new % NT <= t[:, :, None]), 0, NEG).astype(f)
    grp = np.arange(P) // 16 * 4 + np.arange(P) % 4
    parts["group_sum"] = (grp[:, None] == grp[None, :]).astype(f)
    c0 = np.arange(NCMP_S)[:, None] * CSTRIDE
    b0 = np.arange(NSEL_S)[None, :] * SELB
    cover = np.zeros((P, NSEL_S), f)
    cover[:NCMP_S] = (c0 <= b0 + SELB - 1) & (c0 + CLEN - 1 >= b0)
    parts["cover"] = cover
    parts["block_id"] = np.broadcast_to(np.arange(1, NSEL_S - 2, dtype=f), (P, NSEL_S - 3))
    parts["half_power"] = np.full((P, 16), -0.5, f)
    t = (np.arange(P) % NT)[:, None]
    n4 = (np.arange(P) // 32)[:, None]
    new = np.arange(NS)[None, :]
    a_mask = np.zeros((P, 2, 3 * P + 3 * NS), f)
    a_mask[:, :, 0:P] = np.where(k >= t, 0, NEG)[:, None]
    a_mask[:, :, 2 * P:3 * P] = np.where(k // 64 == t // 2, 0, NEG)[:, None]
    for b in range(2):
        own = new // NT == 4 * b + n4
        for g in range(3):
            seen = own & ((new % NT == t) if g else (new % NT <= t))
            a_mask[:, b, 3 * P + g * NS:3 * P + (g + 1) * NS] = np.where(seen, 0, NEG)
    parts["a_mask"] = a_mask
    q = np.arange(P)[:, None]
    back = TILES * np.arange(P)[:, None] + TILES - 1 - np.arange(SEQ + TILES - 1)[None, :]
    parts["strided_band"] = np.where((back >= 0) & (back <= PATTERNS[0][0]), 0, NEG).astype(f)
    parts["own_tile"] = np.concatenate([causal, np.where((k <= q) & ((q - k) % 4 == 0), 0, NEG).astype(f)], 1)
    where, at = {}, 0
    flat = []
    for name, a in parts.items():
        a = np.asarray(a, f).reshape(P, -1)
        where[name] = (at, at + a.shape[1])
        at += a.shape[1]
        flat.append(a)
    return np.ascontiguousarray(np.concatenate(flat, 1)), where


LASTING = (["s_const", "s_copy", "s_page_table", "pa_vout", "pb_rows_out", "pb_win_out", "oa_stored", "ob_stored",
            "pa_w0", "pa_w1", "pb_w0", "pb_w1", "cmp_w", "cp_pages0", "oa_w", "ob_w"]
           + [f"s_x{t}" for t in range(TILES + 1)] + [f"pa_kout{i}" for i in range(3)]
           + [f"sa_ring{i}_{m}" for i in range(3) for m in range(3)])


class Stage:

    def __init__(self, nc, dram, where, ctx):
        self.nc, self.dram, self.where, self.ctx = nc, dram, where, ctx
        self.lasting = {n: ctx.enter_context(nc.semaphore(n)) for n in LASTING}
        self.stage_sems = []
        self.n_vout = 0
        self.outs = []

    def const(self, name):
        a, b = self.where[name]
        return self.consts[:, a:b]

    def lasting_sem(self, name):
        return self.lasting[name]

    def sem(self, name):
        handle = self.nc.alloc_semaphore(name=name)
        self.stage_sems.append(handle)
        return handle

    @contextmanager
    def block(self):
        with self.nc.Block() as block:
            yield block
        self.nc.clear_and_free_semaphores(self.stage_sems)
        self.stage_sems = []
        self.nc.all_engine_barrier()


def permuted(ap, g, t):
    if t == TILES:
        return ap[:, SEQ:TOK]
    return ap[:, t:SEQ:TILES] if g else ap[:, t * P:(t + 1) * P]


def dram_rows(ap, g, t):
    return ap[t:SEQ:TILES] if g else ap[t * P:(t + 1) * P]


def linker(engine, sem):
    count = [0]

    def link(ins):
        count[0] += 1
        ins.then_inc(sem, 1)
        engine.wait_ge(sem, count[0])
    return link


def load_stage(S):
    nc, A = S.nc, S.dram
    S.s_const, S.s_x, S.s_copy = S.lasting_sem("s_const"), [S.lasting_sem(f"s_x{t}") for t in range(TILES + 1)], S.lasting_sem("s_copy")
    S.s_pages = S.lasting_sem("s_page_table")
    S.n_copy = 0
    with nc.Block() as block:
        @block.sync
        def _(sp):
            xp, xs = A["x_prompt"][0], A["x_sample"].rearrange("n t d -> (n t) d")
            for t in range(TILES):
                sp.dma_start(S.x[:, t, :], xp[t * P:(t + 1) * P, :]).then_inc(S.s_x[t], 16)
            sp.dma_start(S.x[0:NS, TILES, :], xs).then_inc(S.s_x[TILES], 16)
            sp.dma_start(S.consts[:, :], A["consts"][:, 0:S.where["a_mask"][0]]).then_inc(S.s_const, 16)
            sp.dma_start(S.page_table[:, :], A["page_table"].rearrange("(o n) p -> o (n p)", o=1)).then_inc(S.s_pages, 16)
            sp.wait_ge(S.s_pages, 16)


def copy_kept(S, engine, which, sequences):
    A = S.dram
    for n in sequences:
        if which == 3:
            cache, out, first, kept = A["cache_nsa_win"], A["new_win_s"], NT, WIN - NT
        else:
            win = PATTERNS[which][0]
            L = min(win, PAST)
            first = max(L + NT - win, 0)
            cache, out, kept = A[f"cache_dil_{which}"], A[f"new_dil_{which}_s"], L - first
        src = cache[0, n, first:first + kept].rearrange("r v h d -> (r v h d)")
        dst = out[0, n, 0:kept].rearrange("r v h d -> (r v h d)")
        engine.dma_start(dst.rearrange("(a b) -> a b", a=64), src.rearrange("(a b) -> a b", a=64)).then_inc(S.s_copy, 16)
        S.n_copy += 16


def norm_stage(S, pfx, x_ready, gain, hT, prefetch):
    nc = S.nc
    with ExitStack() as ctx:
        def sb(name, shape):
            return ctx.enter_context(nc.sbuf_tensor(pfx + name, shape, F32))
        sq = sb("squares", [P, D])
        ss = sb("square_sum", [P, TILES + 1])
        ms = sb("mean_square", [P, TILES + 1])
        rstd = sb("rstd", [P, TILES + 1])
        xn = sb("x_normed", [P, 2, D])
        gain_rows = sb("gain_rows", [KC, P])
        gain_cols = sb("gain_cols", [P, KC])
        s_gain, s_gt, s_gc = S.sem(pfx + "gain"), S.sem(pfx + "gain_turned"), S.sem(pfx + "gain_cols")
        s_ss, s_ms, s_rstd = S.sem(pfx + "ss"), S.sem(pfx + "ms"), S.sem(pfx + "rstd")
        s_xn, s_tr, s_h = S.sem(pfx + "xn"), S.sem(pfx + "turned"), S.sem(pfx + "h")
        with S.block() as block:
            @block.sync
            def _(sp):
                sp.dma_start(gain_rows[:, :], gain.rearrange("o (k p) -> (o k) p", p=P)).then_inc(s_gain, 16)
                prefetch(sp)

            @block.scalar
            def _(act):
                for t in range(TILES + 1):
                    R = rows_of(t)
                    x_ready(act, t)
                    if t:
                        act.wait_ge(s_ss, t)
                    nc.scalar.activation(sq[0:R, :], S.x[0:R, t, :], ACT.Square,
                                         accum_out=ss[0:R, t:t + 1]).then_inc(s_ss, 1)
                for t in range(TILES + 1):
                    R = rows_of(t)
                    if t == 0:
                        act.wait_ge(s_gc, 1)
                    for k in range(KC):
                        if k % 4 == 0:
                            act.wait_ge(s_tr, 2 * t + k // 4 + 1)
                        ins = nc.scalar.activation(hT[:, k, t * P:t * P + R], S.banks[k // 4][:, (k % 4) * P:(k % 4) * P + R],
                                                   ACT.Copy, scale=gain_cols[:, k:k + 1])
                        if k % 4 == 3:
                            ins.then_inc(s_h, 1)

            @block.gpsimd
            def _(pool):
                pool.wait_ge(S.s_const, 16)
                for t in range(TILES + 1):
                    R = rows_of(t)
                    pool.wait_ge(s_ss, t + 1)
                    nc.gpsimd.tensor_scalar(ms[0:R, t:t + 1], ss[0:R, t:t + 1], 1.0 / D, EPS, ALU.mult, ALU.add).then_inc(s_ms, 1)
                    pool.wait_ge(s_ms, t + 1)
                    nc.gpsimd.tensor_tensor(rstd[0:R, t:t + 1], ms[0:R, t:t + 1], S.const("half_power")[0:R, 0:1],
                                            ALU.pow).then_inc(s_rstd, 1)

            @block.vector
            def _(dve):
                dve.wait_ge(s_gt, 1)
                nc.vector.tensor_copy(gain_cols[:, :], S.banks[2][:, 0:KC]).then_inc(s_gc, 1)
                for t in range(TILES + 1):
                    R = rows_of(t)
                    dve.wait_ge(s_rstd, t + 1)
                    x_ready(dve, t)
                    if t >= 2:
                        dve.wait_ge(s_tr, 2 * (t - 1))
                    nc.vector.tensor_scalar(xn[0:R, t % 2, :], S.x[0:R, t, :], rstd[0:R, t:t + 1], None, ALU.mult).then_inc(s_xn, 1)

            @block.tensor
            def _(pe):
                ident = S.const("ident")
                pe.wait_ge(S.s_const, 16)
                pe.wait_ge(s_gain, 16)
                nc.tensor.transpose(S.banks[2][:, 0:KC], gain_rows[:, :], ident[0:KC, 0:KC]).then_inc(s_gt, 1)
                for t in range(TILES + 1):
                    R = rows_of(t)
                    pe.wait_ge(s_xn, t + 1)
                    for k in range(KC):
                        if t and k % 4 == 0:
                            pe.wait_ge(s_h, 2 * (t - 1) + k // 4 + 1)
                        ins = nc.tensor.transpose(S.banks[k // 4][:, (k % 4) * P:(k % 4) * P + R],
                                                  xn[0:R, t % 2, k * P:(k + 1) * P], ident[0:R, 0:R])
                        if k % 4 == 3:
                            ins.then_inc(s_tr, 1)


def rope_tables(S, dve, sem, gains, tabs, spans):
    nc = S.nc
    for i in range(gains.shape[1]):
        for which, name in ((0, "cos"), (1, "sin")):
            src = S.const(name).rearrange("p (s d) -> p s d", d=DH)
            for lo in (0, HALF):
                glo = lo if which == 0 else HALF - lo
                for at, n, to in spans:
                    g = gains[:, i, glo:glo + HALF].unsqueeze(1).broadcast_to((P, n, HALF))
                    nc.vector.tensor_tensor(tabs[:, i, which, to:to + n, lo:lo + HALF], src[:, at:at + n, lo:lo + HALF], g,
                                            ALU.mult).then_inc(sem, 1)


class Unit:
    pass


def project_a_stage(S, hT, W, QK, V, Z):
    nc, A = S.nc, S.dram
    w = A["a_w_in"][0].rearrange("(k p) e -> p k e", p=P)
    units = []
    n_qk = n_lin = 0
    for c in range(10):
        for t in range(TILES + 1):
            u = Unit()
            u.c, u.t, u.g, u.R, u.v = c, t, (c % 3 if c < 9 else 0), rows_of(t), len(units)
            u.qk = c < 6
            u.i = n_qk if u.qk else n_lin
            if u.qk:
                n_qk += 1
            else:
                n_lin += 1
            units.append(u)
    qk_units = [u for u in units if u.qk]
    with ExitStack() as ctx:
        def sb(name, shape):
            return ctx.enter_context(nc.sbuf_tensor("pa_" + name, shape, F32))
        gains = sb("gains", [P, 2, DH])
        tabs = sb("tables", [P, 2, 2, ROPE_SETS, DH])
        sq = sb("squares", [P, WA])
        ss = sb("square_sum", [P, 2, HA])
        ms = sb("mean_square", [P, HA])
        rstd = sb("rstd", [P, 2, HA])
        normed = sb("normed", [P, 2, WA])
        straight = sb("straight", [P, WA])
        swapped = sb("swapped", [P, 2, WA])
        rot = sb("rotated", [P, 3, WA])
        s_w = [S.lasting_sem(f"pa_w{i}") for i in range(2)]
        s_gains, s_tabs = S.sem("pa_gains"), S.sem("pa_tabs")
        s_u, s_lin, s_sq, s_ss, s_ms, s_rstd = (S.sem("pa_" + n) for n in ("u", "lin", "sq", "ss", "ms", "rstd"))
        s_n, s_st, s_sw, s_rot, s_tr, s_ev = (S.sem("pa_" + n) for n in ("n", "st", "sw", "rot", "tr", "ev"))
        s_kout = [S.lasting_sem(f"pa_kout{i}") for i in range(3)]
        S.s_vout = S.lasting_sem("pa_vout")
        n_kout, kout_at = [0, 0, 0], {}
        for u in qk_units:
            if u.c >= 3:
                stored = u.t == TILES or u.g or u.t == TILES - 1
                if stored:
                    n_kout[u.i % 3] += 16
                    kout_at[u.i] = n_kout[u.i % 3]
        U = S.banks[0:3]
        T = S.banks[3:5]

        def dest(u, kv):
            win = PATTERNS[u.g][0]
            if u.t == TILES:
                new = A[f"new_dil_{u.g}_s"]
                return new[0, :, new.shape[2] - NT:, kv].rearrange("n t h d -> n t (h d)")
            out = A[f"new_dil_{u.g}_p"][0, 0, :, kv].rearrange("r h d -> r (h d)")
            return dram_rows(out, u.g, u.t) if u.g else out

        with S.block() as block:
            @block.sync
            def _(sp):
                for i, name in enumerate(("a_q_norm", "a_k_norm")):
                    sp.dma_start(gains[:, i, :], A[name].broadcast_to((P, DH))).then_inc(s_gains, 16)
                for c in range(10):
                    if c + 2 < 10:
                        sp.wait_ge(s_u, 5 * (c + 1))
                        sp.dma_start(W[:, c % 2, :, :], w[:, :, (c + 2) * WA:(c + 3) * WA]).then_inc(s_w[c % 2], 16)
                        copy_kept(S, sp, 1, [c])
                    else:
                        copy_kept(S, sp, 2, [c - 8])
                    for u in units[5 * c:5 * c + 5]:
                        if u.i in kout_at and u.qk:
                            sp.wait_ge(s_rot, u.i + 1)
                            sp.dma_start(dest(u, 0), rot[0:u.R, u.i % 3, :]).then_inc(s_kout[u.i % 3], 16)
                        if 6 <= c < 9 and (u.t == TILES or u.g or u.t == TILES - 1):
                            sp.wait_ge(s_lin, u.i + 1)
                            sp.dma_start(dest(u, 1), V[0:u.R, u.g, u.t, :]).then_inc(S.s_vout, 16)
                            S.n_vout += 16
                S.outs += [(s_kout[i], n_kout[i]) for i in range(3)] + [(S.s_vout, S.n_vout)]

            @block.tensor
            def _(pe):
                ident = S.const("ident")

                def turn(u):
                    pe.wait_ge(s_rot, u.i + 1)
                    if u.i >= 2:
                        pe.wait_ge(s_ev, u.i - 1)
                    for j in range(4):
                        ins = nc.tensor.transpose(T[u.i % 2][:, j * P:j * P + u.R], rot[0:u.R, u.i % 3, j * P:(j + 1) * P],
                                                  ident[0:u.R, 0:u.R])
                    ins.then_inc(s_tr, 1)
                for u in units:
                    if u.t == 0:
                        pe.wait_ge(s_w[u.c % 2], 16 * (u.c // 2 + 1))
                    if u.v >= 3:
                        old = units[u.v - 3]
                        pe.wait_ge(s_n if old.qk else s_lin, old.i + 1)
                    for k in range(KC):
                        ins = nc.tensor.matmul(U[u.v % 3][0:u.R, :], permuted(hT[:, k, :], u.g, u.t), W[:, u.c % 2, k, :],
                                               start=(k == 0), stop=(k == KC - 1))
                    ins.then_inc(s_u, 1)
                    if u.v >= 2 and units[u.v - 2].qk:
                        turn(units[u.v - 2])

            @block.scalar
            def _(act):
                def evacuate(u):
                    act.wait_ge(s_tr, u.i + 1)
                    nc.scalar.activation(QK[:, u.c, :, u.t * P:u.t * P + u.R],
                                         T[u.i % 2][:, :].rearrange("p (j r) -> p j r", j=4)[:, :, 0:u.R], ACT.Copy).then_inc(s_ev, 1)
                for u in units:
                    act.wait_ge(s_u, u.v + 1)
                    src = U[u.v % 3][0:u.R, :]
                    if u.qk:
                        if u.i:
                            act.wait_ge(s_ss, u.i)
                        nc.scalar.activation(sq[0:u.R, :], src, ACT.Square).then_inc(s_sq, 1)
                    elif u.c < 9:
                        nc.scalar.activation(V[0:u.R, u.g, u.t, :], src, ACT.Copy).then_inc(s_lin, 1)
                    else:
                        nc.scalar.activation(Z[0:u.R, u.t, :], src, ACT.Silu).then_inc(s_lin, 1)
                    if u.v >= 2 and units[u.v - 2].qk:
                        evacuate(units[u.v - 2])

            @block.gpsimd
            def _(pool):
                for u in qk_units:
                    R, i = u.R, u.i
                    pool.wait_ge(s_ss, i + 1)
                    nc.gpsimd.tensor_scalar(ms[0:R, :], ss[0:R, i % 2, :], 1.0 / DH, EPS, ALU.mult, ALU.add).then_inc(s_ms, 1)
                    pool.wait_ge(s_ms, i + 1)
                    nc.gpsimd.tensor_tensor(rstd[0:R, i % 2, :], ms[0:R, :], S.const("half_power")[0:R, 0:HA], ALU.pow).then_inc(s_rstd, 1)
                    pool.wait_ge(s_n, i + 1)
                    if i == 0:
                        pool.wait_ge(s_tabs, 8)
                    if i >= 2:
                        pool.wait_ge(s_rot, i - 1)
                    n3 = normed[0:R, i % 2, :].rearrange("p (h d) -> p h d", d=DH)
                    o3 = swapped[0:R, i % 2, :].rearrange("p (h d) -> p h d", d=DH)
                    for lo in (0, HALF):
                        tab = rope_tab(tabs, u.c // 3, 1, u)[0:R, lo:lo + HALF].unsqueeze(1).broadcast_to((R, HA, HALF))
                        nc.gpsimd.tensor_tensor(o3[:, :, lo:lo + HALF], n3[:, :, HALF - lo:DH - lo], tab, ALU.mult).then_inc(s_sw, 1)

            @block.vector
            def _(dve):
                dve.wait_ge(S.s_const, 16)
                dve.wait_ge(s_gains, 32)
                rope_tables(S, dve, s_tabs, gains, tabs, [(0, ROPE_SETS, 0)])

                def first(u):
                    R, i = u.R, u.i
                    dve.wait_ge(s_sq, i + 1)
                    nc.vector.tensor_reduce(ss[0:R, i % 2, :], sq[0:R, :].rearrange("p (h d) -> p h d", d=DH), AX,
                                            ALU.add).then_inc(s_ss, 1)

                def second(u):
                    R, i = u.R, u.i
                    dve.wait_ge(s_rstd, i + 1)
                    n3 = normed[0:R, i % 2, :].rearrange("p (h d) -> p h d", d=DH)
                    dve.wait_ge(s_u, u.v + 1)
                    nc.vector.tensor_tensor(n3, U[u.v % 3][0:R, :].rearrange("p (h d) -> p h d", d=DH),
                                            rstd[0:R, i % 2, :].unsqueeze(2).broadcast_to((R, HA, DH)), ALU.mult).then_inc(s_n, 1)
                    dve.wait_ge(s_n, i + 1)
                    tab = rope_tab(tabs, u.c // 3, 0, u)[0:R, :].unsqueeze(1).broadcast_to((R, HA, DH))
                    nc.vector.tensor_tensor(straight[0:R, :].rearrange("p (h d) -> p h d", d=DH), n3, tab, ALU.mult).then_inc(s_st, 1)
                    dve.wait_ge(s_st, i + 1)
                    dve.wait_ge(s_sw, 2 * (i + 1))
                    if i >= 3:
                        dve.wait_ge(s_tr, i - 2)
                        if i - 3 in kout_at:
                            dve.wait_ge(s_kout[i % 3], kout_at[i - 3])
                    nc.vector.tensor_tensor(rot[0:R, i % 3, :], straight[0:R, :], swapped[0:R, i % 2, :], ALU.add).then_inc(s_rot, 1)
                dve.wait_ge(s_tabs, 8)
                for i, u in enumerate(qk_units):
                    first(u)
                    if i:
                        second(qk_units[i - 1])
                second(qk_units[-1])


def rope_tab(tabs, which, part, u):
    s = ROPE_SETS - 1 if u.t == TILES else (TILES if u.g else 0) + u.t
    return tabs[:, which, part, s, :]


def attend_a_stage(S, QK, V, Z, T, oT, ring):
    nc = S.nc
    N = TILES * HA
    LAG = 3
    CH = TILES + 2
    W0 = CH * P
    with ExitStack() as ctx:
        def sb(name, shape):
            return ctx.enter_context(nc.sbuf_tensor("aa_" + name, shape, F32))
        s_tab = S.sem("aa_tables")
        BAND = SEQ + TILES - 1
        tables = sb("tables", [P, BAND + 2 * P])
        masked = sb("masked", [P, 2, W0])
        probs = sb("probs", [P, 4, W0])
        pT = sb("probs_turned", [P, 2, CH, P])
        lows, low, den, rec = sb("lows", [P, 8, 2]), sb("low", [P, 8]), sb("den", [P, 8]), sb("rec", [P, 8])
        s_sc, s_part, s_m, s_e, s_rec, s_p, s_tr, s_pv, s_z, s_zc, s_fin, s_kept = (
            S.sem("aa_" + n) for n in ("scores", "part", "masked", "exp", "rec", "weighted", "turned", "pv", "z_turned", "z_copied",
                                       "finished", "kept"))
        s_ev = [S.sem("aa_copied_by_vector"), S.sem("aa_copied_by_scalar")]
        SA, SB, TRA, TRB, OB, ZB = S.banks[0:2], S.banks[2:4], S.banks[4], S.banks[5], S.banks[6], S.banks[7]

        def unit(v):
            t, h = divmod(v, HA)
            return t, h, h // 2, slice((h % 2) * DH, (h % 2 + 1) * DH)

        with S.block() as block:
            @block.sync
            def _(sp):
                (a, _), (_, b) = S.where["strided_band"], S.where["own_tile"]
                sp.dma_start(tables[:, :], S.dram["consts"][:, a:b]).then_inc(s_tab, 16)
                for m in range(2):
                    load_cache_a(S, sp, m, ring[m])

            @block.tensor
            def _(pe):
                ident = S.const("ident")
                for t in range(TILES):
                    if t:
                        pe.wait_ge(s_zc, t)
                    for j in range(4):
                        ins = nc.tensor.transpose(ZB[:, j * P:(j + 1) * P], Z[:, t, j * P:(j + 1) * P], ident)
                    ins.then_inc(s_z, 1)

                def scores(v):
                    t, h, j, part = unit(v)
                    if v >= 2:
                        pe.wait_ge(s_m, v - 1)
                    nc.tensor.matmul(SA[v % 2][:, :], QK[part, 0, j, t:SEQ:TILES], QK[part, 3, j, 0:SEQ], start=True, stop=True)
                    for g in (1, 2):
                        own = slice(t * P, (t + 1) * P)
                        ins = nc.tensor.matmul(SB[v % 2][:, (g - 1) * P:g * P], QK[part, g, j, own], QK[part, 3 + g, j, own],
                                               start=True, stop=True)
                    ins.then_inc(s_sc, 1)

                def turn(v):
                    pe.wait_ge(s_p, v + 1)
                    if v:
                        pe.wait_ge(s_ev[0], v)
                        pe.wait_ge(s_ev[1], v)
                    for c in range(CH):
                        bank, at = (TRA, c) if c < TILES else (TRB, c - TILES)
                        ins = nc.tensor.transpose(bank[:, at * P:(at + 1) * P], probs[:, v % 4, c * P:(c + 1) * P], ident)
                    ins.then_inc(s_tr, 1)

                def values(v):
                    t, h, j, part = unit(v)
                    for e in range(2):
                        pe.wait_ge(s_ev[e], v + 1)
                    if h == 0 and t:
                        pe.wait_ge(s_fin, t)
                    for c in range(CH):
                        g, kt = (0, c) if c < TILES else (c - TILES + 1, t)
                        ins = nc.tensor.matmul(OB[part, j * P:(j + 1) * P], V[:, g, kt, h * DH:(h + 1) * DH], pT[:, v % 2, c, :],
                                               start=(c == 0), stop=(c == CH - 1))
                    ins.then_inc(s_pv, 1)
                for v in range(N + LAG + 1):
                    if v < N:
                        scores(v)
                    if LAG <= v < N + LAG:
                        turn(v - LAG)
                    if v > LAG:
                        values(v - LAG - 1)

            @block.scalar
            def _(act):
                for t in range(TILES):
                    act.wait_ge(s_z, t + 1)
                    nc.scalar.activation(oT[:, 0:4, t * P:(t + 1) * P], ZB[:, :].rearrange("p (j r) -> p j r", j=4),
                                         ACT.Copy).then_inc(s_zc, 1)
                nc.scalar.activation(T.q[:, :, :, :], QK[:, 0:3, :, SEQ:TOK], ACT.Copy).then_inc(s_kept, 1)
                nc.scalar.activation(T.k[:, :, :, :], QK[:, 3:6, :, SEQ:TOK], ACT.Copy).then_inc(s_kept, 1)
                act.wait_ge(s_kept, 4)
                for v in range(N + LAG):
                    if v < N:
                        act.wait_ge(s_m, v + 1)
                        if v >= 4:
                            act.wait_ge(s_tr, v - 3)
                        nc.scalar.activation(probs[:, v % 4, :], masked[:, v % 2, :], ACT.Exp, bias=low[:, v % 8:v % 8 + 1],
                                             scale=-1.0, accum_out=den[:, v % 8:v % 8 + 1]).then_inc(s_e, 1)
                    if v >= LAG:
                        u = v - LAG
                        act.wait_ge(s_tr, u + 1)
                        if u >= 2:
                            act.wait_ge(s_pv, u - 1)
                        nc.scalar.activation(pT[:, u % 2, TILES:, :], TRB[:, 0:2 * P].rearrange("p (c q) -> p c q", q=P),
                                             ACT.Copy).then_inc(s_ev[1], 1)

            @block.gpsimd
            def _(pool):
                for v in range(N):
                    pool.wait_ge(s_rec, v + 1)
                    p = probs[:, v % 4, :]
                    nc.gpsimd.tensor_scalar(p, p, rec[:, v % 8:v % 8 + 1], None, ALU.mult).then_inc(s_p, 1)

            @block.vector
            def _(dve):
                nc.vector.tensor_copy(T.v[:, :, :], V[0:NS, :, TILES, :]).then_inc(s_kept, 1)
                nc.vector.tensor_copy(T.z[:, :], Z[0:NS, TILES, :]).then_inc(s_kept, 1)
                dve.wait_ge(s_tab, 16)
                for v in range(N + LAG + 3):
                    if v < N:
                        t = v // HA
                        i = v % 8
                        dve.wait_ge(s_sc, v + 1)
                        if v >= 2:
                            dve.wait_ge(s_e, v - 1)
                        nc.vector.tensor_tensor_reduce(masked[:, v % 2, 0:SEQ], SA[v % 2][:, :],
                                                       tables[:, TILES - 1 - t:TILES - 1 - t + SEQ], -SCALE, 3e38,
                                                       ALU.add, ALU.min, lows[:, i, 0:1]).then_inc(s_part, 1)
                        nc.vector.tensor_tensor_reduce(masked[:, v % 2, SEQ:], SB[v % 2][:, 0:2 * P], tables[:, BAND:], -SCALE, 3e38,
                                                       ALU.add, ALU.min, lows[:, i, 1:2]).then_inc(s_part, 1)
                        dve.wait_ge(s_part, 2 * (v + 1))
                        nc.vector.tensor_tensor(low[:, i:i + 1], lows[:, i, 0:1], lows[:, i, 1:2], ALU.min).then_inc(s_m, 1)
                    if 1 <= v < N + 1:
                        i = (v - 1) % 8
                        dve.wait_ge(s_e, v)
                        nc.vector.reciprocal(rec[:, i:i + 1], den[:, i:i + 1]).then_inc(s_rec, 1)
                    if LAG <= v < N + LAG:
                        u = v - LAG
                        dve.wait_ge(s_tr, u + 1)
                        if u >= 2:
                            dve.wait_ge(s_pv, u - 1)
                        nc.vector.tensor_copy(pT[:, u % 2, 0:TILES, :], TRA[:, :].rearrange("p (c q) -> p c q", q=P)).then_inc(s_ev[0], 1)
                    if v >= LAG + 1 + HA and (v - LAG - 1) % HA == 0:
                        t = (v - LAG - 1) // HA - 1
                        dve.wait_ge(s_pv, HA * (t + 1))
                        dve.wait_ge(s_zc, TILES)
                        cols = oT[:, 0:4, t:SEQ:TILES]
                        nc.vector.tensor_tensor(cols, OB[:, :].rearrange("p (j q) -> p j q", j=4), cols, ALU.mult).then_inc(s_fin, 1)


KTILES_A = 7


SLOTS_A = 3


def load_cache_a(S, sp, m, slot):
    kv, n = divmod(m, NB)
    sems = [S.lasting_sem(f"sa_ring{m % SLOTS_A}_{i}") for i in range(3)]
    c0, c1, c2 = (S.dram[f"cache_dil_{g}"][0, n, :, kv].rearrange("r h d -> r (h d)") for g in range(3))
    sp.dma_start(slot[:, 0, :], c0).then_inc(sems[0], 16)
    sp.dma_start(slot[:, 1:1 + NT, :], c1.rearrange("(p t) e -> p t e", t=NT)).then_inc(sems[1], 16)
    c2 = c2.rearrange("(p c) e -> p c e", c=16)
    for half in range(2):
        sp.dma_start(slot[64 * half:64 * half + 64, 1 + NT:, :], c2[:, 2 * half:2 * half + 2, :]).then_inc(sems[2], 16)


def sample_a_stage(S, T, oT, W_out, ring):
    nc, A = S.nc, S.dram
    NK = KTILES_A * NB
    SLOTS = SLOTS_A
    BLOCK = 4 * NB * 32
    COLS = 3 * P + 3 * NS
    with ExitStack() as ctx:
        def sb(name, shape):
            return ctx.enter_context(nc.sbuf_tensor("sa_" + name, shape, F32))
        ring = ring + [sb("cache", [P, KTILES_A, WA])]
        qz = sb("q_padded", [P, 9 * BLOCK + 32])
        kT = sb("keys_turned", [P, 2, 4, P])
        masked = sb("masked", [P, COLS])
        probs = sb("probs", [P, 2, COLS])
        low, den, rec = (sb(n, [P, 2]) for n in ("low", "den", "rec"))
        pz = sb("p_padded", [P, 2, 7, P])
        pTn = sb("p_new_turned", [NS, 2, 3, P])
        out = sb("out", [P, WA])
        mask = sb("mask", [P, 2, COLS])
        zT = sb("z_t", [P, 4, NS])
        s_ring = [[S.lasting_sem(f"sa_ring{i}_{m}") for m in range(3)] for i in range(SLOTS)]
        s_mask = S.sem("sa_mask")
        s_zero, s_pzero, s_q, s_turn, s_mul, s_sc = (S.sem("sa_" + n) for n in ("zero", "pzero", "q", "turn", "mul", "scores_done"))
        s_ev = [S.sem("sa_ev0"), S.sem("sa_ev1")]
        s_low, s_exp, s_pt, s_ptc = (S.sem("sa_" + n) for n in ("low", "exp", "pt", "ptc"))
        s_pv, s_out, s_ot, s_o, s_zt, s_ztc = (S.sem("sa_" + n) for n in ("pv", "out", "out_turned", "o", "zt", "ztc"))
        B = S.banks

        def landed(engine, m):
            for i, k in enumerate((1, 1, 2)):
                engine.wait_ge(s_ring[m % SLOTS][i], 16 * k * (m // SLOTS + 1))

        def variant(kk):
            return (0, 0) if kk == 0 else (2 + kk, 1) if kk <= NT else (2 + kk, 2)

        def queries(block, j, n):
            at = block * BLOCK + j * NB * 32 + n * 32
            return qz[:, at:at + 32]

        def pad_view(block, e):
            step = NB * 32 + 8
            v = qz[e * DH:(e + 1) * DH, block * BLOCK:block * BLOCK + 4 * step].rearrange("p (j s) -> p j s", s=step)
            return v[:, :, 0:NB * 32].rearrange("p j (n c) -> p j n c", c=32)[:, :, :, e * NT:(e + 1) * NT]

        def quad(n):
            return slice(32 * (n % 4), 32 * (n % 4) + 32)

        with S.block() as block:
            @block.sync
            def _(sp):
                for m in range(2, 2 * NB):
                    if m >= SLOTS:
                        old = m - SLOTS
                        if old < NB:
                            sp.wait_ge(s_turn, KTILES_A * (old + 1))
                        else:
                            sp.wait_ge(s_pv, KTILES_A * (old + 1 - NB))
                    load_cache_a(S, sp, m, ring[m % SLOTS])
                    if m == 4:
                        sp.dma_start(W_out[:, :, :], A["a_w_out"][0].rearrange("(k p) e -> p k e", p=P)).then_inc(S.lasting_sem("oa_w"), 16)
                    if m == 2:
                        a, b = S.where["a_mask"]
                        sp.dma_start(mask[:, :, :].rearrange("p b c -> p (b c)"), A["consts"][:, a:b]).then_inc(s_mask, 16)

            @block.gpsimd
            def _(pool):
                half = 9 * BLOCK // 2
                nc.gpsimd.memset(qz[:, 0:half], 0.0).then_inc(s_zero, 1)
                nc.gpsimd.memset(pz[:, :, :, :], 0.0).then_inc(s_pzero, 1)

            @block.tensor
            def _(pe):
                ident = S.const("ident")
                for j in range(4):
                    ins = nc.tensor.transpose(B[5][:, j * NS:(j + 1) * NS], T.z[:, j * P:(j + 1) * P], ident[0:NS, 0:NS])
                ins.then_inc(s_zt, 1)

                def turn(i):
                    n, kk = divmod(i, KTILES_A)
                    if kk == 0:
                        landed(pe, n)
                    if i >= 2:
                        pe.wait_ge(s_ev[i % 2], i // 2)
                    for j in range(4):
                        ins = nc.tensor.transpose(B[2 + i % 2][:, j * P:(j + 1) * P], ring[n % SLOTS][:, kk, j * P:(j + 1) * P], ident)
                    ins.then_inc(s_turn, 1)

                def multiply(i):
                    n, kk = divmod(i, KTILES_A)
                    q_block, g = variant(kk)
                    pe.wait_ge(s_ev[i % 2], i // 2 + 1)
                    for j in range(4):
                        ins = nc.tensor.matmul(B[n // 4][quad(n), g * P:(g + 1) * P], queries(q_block, j, n), kT[:, i % 2, j, :],
                                               start=(kk in (0, 1, 1 + NT) and j == 0), stop=(kk in (0, NT, NT + 2) and j == 3),
                                               skip_group_check=True)
                    ins.then_inc(s_mul, 1)

                def new_scores(b):
                    for n in range(4 * b, 4 * b + 4):
                        for g in range(3):
                            for j in range(4):
                                ins = nc.tensor.matmul(B[b][quad(n), 3 * P + g * NS:3 * P + (g + 1) * NS], queries(g, j, n),
                                                       T.k[:, g, j, :], start=(j == 0), stop=(j == 3), skip_group_check=True)
                    ins.then_inc(s_sc, 1)

                def turn_probs(b):
                    pe.wait_ge(s_exp, b + 1)
                    if b:
                        pe.wait_ge(s_ptc, 8)
                    for g in range(3):
                        nc.tensor.transpose(B[4][:, g * P:(g + 1) * P], probs[:, b, g * P:(g + 1) * P], ident)
                    if b == 0:
                        pe.wait_ge(s_ztc, 1)
                    for g in range(3):
                        ins = nc.tensor.transpose(B[5][0:NS, g * P:(g + 1) * P], probs[:, b, 3 * P + g * NS:3 * P + (g + 1) * NS], ident)
                    ins.then_inc(s_pt, 1)

                def values(n):
                    b = n // 4
                    landed(pe, n + NB)
                    for g in range(3):
                        nc.tensor.matmul(B[6 + b][quad(n), :], pTn[:, b, g, quad(n)], T.v[:, g, :], start=(g == 0), stop=False,
                                         skip_group_check=True)
                    for kk in range(KTILES_A):
                        nc.tensor.matmul(B[6 + b][quad(n), :], pz[:, b, kk, quad(n)], ring[(n + NB) % SLOTS][:, kk, :],
                                         start=False, stop=(kk == KTILES_A - 1), skip_group_check=True).then_inc(s_pv, 1)

                def turn_out(b):
                    pe.wait_ge(s_out, b + 1)
                    if b == 0:
                        pe.wait_ge(s_ptc, 16)
                    else:
                        pe.wait_ge(s_o, 8)
                    for j in range(4):
                        ins = nc.tensor.transpose(B[4][:, j * P:(j + 1) * P], out[:, j * P:(j + 1) * P], ident)
                    ins.then_inc(s_ot, 1)
                pe.wait_ge(s_q, 18)
                for i in range(NK + 1):
                    if i < NK:
                        turn(i)
                    if i:
                        multiply(i - 1)
                    if i == NK // 2:
                        new_scores(0)
                    if i == NK // 2 + 6:
                        turn_probs(0)
                new_scores(1)
                pe.wait_ge(s_ptc, 8)
                for n in range(2):
                    values(n)
                turn_probs(1)
                for n in range(2, 4):
                    values(n)
                pe.wait_ge(s_ptc, 16)
                values(4)
                turn_out(0)
                for n in range(5, 8):
                    values(n)
                turn_out(1)

            def evacuate(engine, i):
                engine.wait_ge(s_turn, i + 1)
                if i >= 2:
                    engine.wait_ge(s_mul, i - 1)
                src = B[2 + i % 2][:, :].rearrange("p (j r) -> p j r", j=4)
                if i % 2 == 0:
                    nc.vector.tensor_copy(kT[:, 0, :, :], src).then_inc(s_ev[0], 1)
                else:
                    nc.scalar.activation(kT[:, 1, :, :], src, ACT.Copy).then_inc(s_ev[1], 1)

            @block.scalar
            def _(act):
                act.wait_ge(s_zt, 1)
                nc.scalar.activation(zT[:, :, :], B[5][:, 0:4 * NS].rearrange("p (j r) -> p j r", j=4), ACT.Copy).then_inc(s_ztc, 1)

                def exp(b):
                    act.wait_ge(s_low, b + 1)
                    nc.scalar.activation(probs[:, b, :], masked[:, :], ACT.Exp, bias=low[:, b:b + 1], scale=-1.0,
                                         accum_out=den[:, b:b + 1]).then_inc(s_exp, 1)
                for i in range(1, NK, 2):
                    evacuate(act, i)
                    if i == NK // 2 + 3:
                        exp(0)
                exp(1)

            @block.vector
            def _(dve):
                nc.vector.memset(qz[:, 9 * BLOCK // 2:], 0.0).then_inc(s_zero, 1)
                dve.wait_ge(s_zero, 2)
                for e in range(2):
                    part = slice(e * DH, (e + 1) * DH)
                    src = [T.q[part, g, :, :].rearrange("p j (n t) -> p j n t", t=NT) for g in range(3)]
                    for g in range(3):
                        nc.vector.tensor_copy(pad_view(g, e), src[g]).then_inc(s_q, 1)
                    for t in range(NT):
                        nc.vector.tensor_copy(pad_view(3 + t, e)[:, :, :, t], src[1][:, :, :, t]).then_inc(s_q, 1)
                    for i in range(2):
                        nc.vector.tensor_copy(pad_view(7 + i, e)[:, :, :, i::2], src[2][:, :, :, i::2]).then_inc(s_q, 1)

                def soft(b):
                    dve.wait_ge(s_sc, b + 1)
                    dve.wait_ge(s_mask, 16)
                    if b:
                        dve.wait_ge(s_exp, b)
                    nc.vector.tensor_tensor_reduce(masked[:, :], B[b][:, 0:COLS], mask[:, b, :], -SCALE,
                                                   3e38, ALU.add, ALU.min, low[:, b:b + 1]).then_inc(s_low, 1)

                def copy_probs(b):
                    dve.wait_ge(s_pt, b + 1)
                    if b == 0:
                        dve.wait_ge(s_pzero, 1)
                    src = [B[4][:, g * P:(g + 1) * P].rearrange("p (n t) -> p n t", t=NT) for g in range(3)]
                    dst = [pz[:, b, kk, :].rearrange("p (n t) -> p n t", t=NT) for kk in range(KTILES_A)]
                    nc.vector.tensor_copy(pz[:, b, 0, :], B[4][:, 0:P]).then_inc(s_ptc, 1)
                    for t in range(NT):
                        nc.vector.tensor_copy(dst[1 + t][:, :, t], src[1][:, :, t]).then_inc(s_ptc, 1)
                    for i in range(2):
                        nc.vector.tensor_copy(dst[1 + NT + i][:, :, i::2], src[2][:, :, i::2]).then_inc(s_ptc, 1)
                    nc.vector.tensor_copy(pTn[:, b, :, :], B[5][0:NS, 0:3 * P].rearrange("p (g r) -> p g r", g=3)).then_inc(s_ptc, 1)
                    nc.vector.reciprocal(rec[:, b:b + 1], den[:, b:b + 1])
                for i in range(0, NK, 2):
                    evacuate(dve, i)
                    if i == NK // 2 + 2:
                        soft(0)
                    if i == NK // 2 + 8:
                        copy_probs(0)
                soft(1)
                copy_probs(1)
                for b in range(2):
                    dve.wait_ge(s_pv, KTILES_A * 4 * (b + 1))
                    if b:
                        dve.wait_ge(s_ot, b)
                    dve.wait_ge(s_ptc, 16)
                    nc.vector.tensor_scalar(out[:, :], B[6 + b][:, :], rec[:, b:b + 1], None, ALU.mult).then_inc(s_out, 1)
                    dve.wait_ge(s_ot, b + 1)
                    dve.wait_ge(s_ztc, 1)
                    for j in range(4):
                        for e in range(2):
                            part = slice(e * DH, (e + 1) * DH)
                            h = 2 * j + e
                            src = B[4][part, j * P:(j + 1) * P].rearrange("p (n c) -> p n c", n=4)[:, :, h * NT:(h + 1) * NT]
                            dst = oT[part, j, SEQ + 16 * b:SEQ + 16 * (b + 1)].rearrange("p (n t) -> p n t", t=NT)
                            z = zT[part, j, 16 * b:16 * (b + 1)].rearrange("p (n t) -> p n t", t=NT)
                            nc.vector.tensor_tensor(dst, src, z, ALU.mult).then_inc(s_o, 1)


def output_stage(S, pfx, oT, W, w_count, nk, y_rows=None):
    nc = S.nc
    s_w, s_mm, s_y = S.lasting_sem(pfx + "w"), S.sem(pfx + "mm"), S.sem(pfx + "y")
    s_st = S.lasting_sem(pfx + "stored")
    with S.block() as block:
        @block.sync
        def _(sp):
            if y_rows:
                for t in range(TILES + 1):
                    sp.wait_ge(s_y, 2 * t + 2)
                    sp.dma_start(y_rows(t), S.x[0:rows_of(t), t, :]).then_inc(s_st, 16)
                S.outs.append((s_st, 16 * (TILES + 1)))

        @block.tensor
        def _(pe):
            pe.wait_ge(s_w, w_count)
            for v in range(2 * (TILES + 1)):
                t, half = divmod(v, 2)
                if v >= 4:
                    pe.wait_ge(s_y, v - 3)
                for k in range(nk):
                    ins = nc.tensor.matmul(S.banks[v % 4][0:rows_of(t), :], oT[:, k, t * P:t * P + rows_of(t)],
                                           W[:, k, half * 512:half * 512 + 512], start=(k == 0), stop=(k == nk - 1))
                ins.then_inc(s_mm, 1)

        @block.vector
        def _(dve):
            for v in range(2 * (TILES + 1)):
                t, half = divmod(v, 2)
                R = rows_of(t)
                dve.wait_ge(s_mm, v + 1)
                xs = S.x[0:R, t, half * 512:half * 512 + 512]
                nc.vector.tensor_tensor(xs, S.banks[v % 4][0:R, :], xs, ALU.add).then_inc(s_y, 1)


def layer_a(S):
    nc, A = S.nc, S.dram
    with ExitStack() as ctx:
        def sb(name, shape, c=ctx):
            return c.enter_context(nc.sbuf_tensor("la_" + name, shape, F32))
        T = Unit()
        T.q = sb("s_q", [P, 3, 4, NS])
        T.z = sb("s_z", [NS, WA])
        hT = sb("hT", [P, KC, TOK])
        oT = hT[:, 0:4, :]
        rest = hT[:, 4:8, :].rearrange("p k r -> p (k r)")
        region = sb("region", [P, 2 * KC * WA])
        W = region[:, :].rearrange("p (c k e) -> p c k e", c=2, k=KC)
        ring = [region[:, i * KTILES_A * WA:(i + 1) * KTILES_A * WA].rearrange("p (k e) -> p k e", k=KTILES_A) for i in range(2)]
        T.k = rest[:, 0:12 * NS].rearrange("p (g j r) -> p g j r", g=3, j=4)
        T.v = rest[0:NS, 12 * NS:12 * NS + 3 * WA].rearrange("p (g e) -> p g e", g=3)
        with ExitStack() as inner:
            QK = sb("qk", [P, 6, 4, TOK], inner)
            V = sb("v", [P, 3, TILES + 1, WA], inner)
            Z = sb("z", [P, TILES + 1, WA], inner)

            def first_weights(sp):
                w = A["a_w_in"][0].rearrange("(k p) e -> p k e", p=P)
                for c in range(2):
                    sp.dma_start(W[:, c, :, :], w[:, :, c * WA:(c + 1) * WA]).then_inc(S.lasting_sem(f"pa_w{c}"), 16)
            norm_stage(S, "na_", lambda e, t: e.wait_ge(S.s_x[t], 16), A["a_norm"], hT, first_weights)
            project_a_stage(S, hT, W, QK, V, Z)
            attend_a_stage(S, QK, V, Z, T, oT, ring)
        W_out = sb("w_out", [P, 4, D])
        sample_a_stage(S, T, oT, W_out, ring)
        output_stage(S, "oa_", oT, W_out, 16, 4)


def project_b_stage(S, hT, W, QP, KT, ROWS, WINR, Z, GATES, weights):
    nc, A = S.nc, S.dram
    w = A["b_w_in"][0].rearrange("(k p) e -> p k e", p=P)
    NG = 3 * HB
    cols = [(0, 512), (512, 512), (1024, 512), (1536, 512), (2048, 512), (2560, NG), (2560 + NG, 512), (3072 + NG, 512)]
    NC = len(cols)
    units = []
    for c in range(NC):
        for t in range(TILES + 1):
            u = Unit()
            u.c, u.t, u.g, u.R, u.v = c, t, 0, rows_of(t), len(units)
            u.q, u.kv = c < 2, 2 <= c < 5
            u.qk = u.q or u.kv
            u.i = u.v if u.qk else u.v - 25
            u.heads = 8 if u.q else 4
            u.ri = u.i if c < 2 else u.i - 5
            units.append(u)
    qk_units = units[:25]
    with ExitStack() as ctx:
        def sb(name, shape):
            return ctx.enter_context(nc.sbuf_tensor("pb_" + name, shape, F32))
        gains = sb("gains", [P, 2, DH])
        tabs = sb("tables", [P, 2, 2, TILES + 1, DH])
        sq = sb("squares", [P, 512])
        ss, rstd = sb("square_sum", [P, 2, 8]), sb("rstd", [P, 2, 8])
        ms = sb("mean_square", [P, 8])
        normed = sb("normed", [P, 2, 512])
        straight = sb("straight", [P, 512])
        swapped = sb("swapped", [P, 512])
        plain = sb("plain", [P, 2, 512])
        rot = sb("rotated", [P, 2, 512])
        s_w = [S.lasting_sem(f"pb_w{i}") for i in range(2)]
        s_gains, s_tabs = S.sem("pb_gains"), S.sem("pb_tabs")
        s_u, s_lin, s_sq, s_ss, s_ms, s_rstd = (S.sem("pb_" + n) for n in ("u", "lin", "sq", "ss", "ms", "rstd"))
        s_n, s_st, s_sw, s_pl, s_rot, s_tr, s_ev, s_v = (S.sem("pb_" + n) for n in ("n", "st", "sw", "pl", "rot", "tr", "ev", "v"))
        S.s_rows_out = S.lasting_sem("pb_rows_out")
        s_win_out = S.lasting_sem("pb_win_out")
        U = S.banks[0:3]
        TP, TR = S.banks[3:5], S.banks[5:7]
        with S.block() as block:
            @block.sync
            def _(sp):
                for i, name in enumerate(("b_q_norm", "b_k_norm")):
                    sp.dma_start(gains[:, i, :], A[name].broadcast_to((P, DH))).then_inc(s_gains, 16)
                for c in range(NC):
                    if c + 2 < NC:
                        lo, n = cols[c + 2]
                        sp.wait_ge(s_u, 5 * (c + 1))
                        sp.dma_start(W[:, c % 2, :, 0:n], w[:, :, lo:lo + n]).then_inc(s_w[c % 2], 16)
                        copy_kept(S, sp, 3, [c])
                    copy_kept(S, sp, 0, [c])
                    if c == 6:
                        copy_kept(S, sp, 2, [2])
                    if c in (3, 4):
                        for t in range(TILES + 1):
                            u = units[5 * c + t]
                            sp.wait_ge(s_rot, u.i + 1)
                            sp.wait_ge(s_v, u.i - 9)
                            if c == 3 and t < TILES:
                                sp.dma_start(A["new_rows_p"][0, 0, t * P:(t + 1) * P].rearrange("r s h d -> r (s h d)"),
                                             ROWS[:, t, :]).then_inc(S.s_rows_out, 16)
                            elif c == 3:
                                sp.dma_start(A["new_rows_s"][0].rearrange("n t s h d -> (n t) (s h d)"),
                                             ROWS[0:NS, t, :]).then_inc(S.s_rows_out, 16)
                            elif t < TILES:
                                sp.dma_start(A["new_win_p"][0, 0, t * P:(t + 1) * P].rearrange("r s h d -> r (s h d)"),
                                             WINR[:, t, :]).then_inc(s_win_out, 16)
                            else:
                                sp.dma_start(A["new_win_s"][0, :, WIN - NT:].rearrange("n t s h d -> n t (s h d)"),
                                             WINR[0:NS, t, :]).then_inc(s_win_out, 16)
                S.outs += [(S.s_rows_out, 80), (s_win_out, 80)]
                sp.wait_ge(s_u, 5 * (NC - 1))
                load_compress_weights(S, sp, weights)

            @block.tensor
            def _(pe):
                ident = S.const("ident")

                def turn(u):
                    pe.wait_ge(s_rot, u.i + 1)
                    if u.ri >= 2:
                        pe.wait_ge(s_ev, u.ri - 1)
                    if u.q:
                        pe.wait_ge(s_pl, 2 * (u.i + 1))
                        for bank, src in ((TP[u.ri % 2], plain), (TR[u.ri % 2], rot)):
                            for j in range(4):
                                ins = nc.tensor.transpose(bank[:, j * P:j * P + u.R], src[0:u.R, u.i % 2, j * P:(j + 1) * P],
                                                          ident[0:u.R, 0:u.R])
                    else:
                        src = ROWS[0:u.R, u.t, 512:768] if u.c == 3 else WINR[0:u.R, u.t, 0:256]
                        for j in range(2):
                            ins = nc.tensor.transpose(TR[u.ri % 2][:, j * P:j * P + u.R], src[:, j * P:(j + 1) * P],
                                                      ident[0:u.R, 0:u.R])
                    ins.then_inc(s_tr, 1)
                for u in units:
                    n = cols[u.c][1]
                    if u.t == 0:
                        pe.wait_ge(s_w[u.c % 2], 16 * (u.c // 2 + 1))
                    if u.v >= 3:
                        old = units[u.v - 3]
                        pe.wait_ge(s_n if old.qk else s_lin, old.i + 1)
                        if old.kv:
                            pe.wait_ge(s_v, old.i - 9)
                    for k in range(KC):
                        ins = nc.tensor.matmul(U[u.v % 3][0:u.R, 0:n], hT[:, k, u.t * P:u.t * P + u.R], W[:, u.c % 2, k, 0:n],
                                               start=(k == 0), stop=(k == KC - 1))
                    ins.then_inc(s_u, 1)
                    if u.v >= 2 and (units[u.v - 2].q or units[u.v - 2].c in (3, 4)):
                        turn(units[u.v - 2])

            @block.scalar
            def _(act):
                def evacuate(u):
                    act.wait_ge(s_tr, u.ri + 1)
                    tok = slice(u.t * P, u.t * P + u.R)
                    if u.q:
                        for var, bank in enumerate((TP, TR)):
                            ins = nc.scalar.activation(QP[:, var, 4 * u.c:4 * u.c + 4, tok],
                                                       bank[u.ri % 2][:, :].rearrange("p (j r) -> p j r", j=4)[:, :, 0:u.R], ACT.Copy)
                    else:
                        ins = nc.scalar.activation(KT[:, u.c - 3, :, tok],
                                                   TR[u.ri % 2][:, 0:2 * P].rearrange("p (j r) -> p j r", j=2)[:, :, 0:u.R], ACT.Copy)
                    ins.then_inc(s_ev, 1)
                for u in units:
                    act.wait_ge(s_u, u.v + 1)
                    src = U[u.v % 3]
                    n = cols[u.c][1]
                    if u.qk:
                        if u.i:
                            act.wait_ge(s_ss, u.i)
                        w_ = DH * u.heads
                        sq_ins = nc.scalar.activation(sq[0:u.R, 0:w_], src[0:u.R, 0:w_], ACT.Square)
                        if u.kv:
                            dst = {2: ROWS[0:u.R, u.t, 256:512], 3: ROWS[0:u.R, u.t, 768:1024], 4: WINR[0:u.R, u.t, 256:512]}[u.c]
                            nc.scalar.activation(dst, src[0:u.R, 256:512], ACT.Copy).then_inc(s_v, 1)
                        sq_ins.then_inc(s_sq, 1)
                    elif u.c == 5:
                        nc.scalar.activation(GATES[0:u.R, u.t, :], src[0:u.R, 0:n], ACT.Sigmoid).then_inc(s_lin, 1)
                    else:
                        dst = Z[0:u.R, u.t, (u.c - 6) * 512:(u.c - 5) * 512]
                        if u.t < TILES:
                            nc.scalar.activation(dst.rearrange("p (g k d) -> p k g d", g=GQA, d=DH),
                                                 src[0:u.R, :].rearrange("p (k g d) -> p k g d", g=GQA, d=DH), ACT.Silu).then_inc(s_lin, 1)
                        else:
                            nc.scalar.activation(dst, src[0:u.R, :], ACT.Silu).then_inc(s_lin, 1)
                    if u.v >= 2 and (units[u.v - 2].q or units[u.v - 2].c in (3, 4)):
                        evacuate(units[u.v - 2])

            @block.gpsimd
            def _(pool):
                for u in qk_units:
                    R, i, H = u.R, u.i, u.heads
                    pool.wait_ge(s_ss, i + 1)
                    if i:
                        pool.wait_ge(s_rstd, i)
                    nc.gpsimd.tensor_scalar(ms[0:R, 0:H], ss[0:R, i % 2, 0:H], 1.0 / DH, EPS, ALU.mult, ALU.add).then_inc(s_ms, 1)
                    pool.wait_ge(s_ms, i + 1)
                    nc.gpsimd.tensor_tensor(rstd[0:R, i % 2, 0:H], ms[0:R, 0:H], S.const("half_power")[0:R, 0:H], ALU.pow).then_inc(s_rstd, 1)
                    if u.c == 2:
                        continue
                    pool.wait_ge(s_n, i + 1)
                    if i == 0:
                        pool.wait_ge(s_tabs, 16)
                    if i:
                        pool.wait_ge(s_rot, i)
                    n3 = normed[0:R, i % 2, 0:DH * H].rearrange("p (h d) -> p h d", d=DH)
                    o3 = swapped[0:R, 0:DH * H].rearrange("p (h d) -> p h d", d=DH)
                    for lo in (0, HALF):
                        tab = tabs[0:R, 1 if u.kv else 0, 1, u.t, lo:lo + HALF].unsqueeze(1).broadcast_to((R, H, HALF))
                        nc.gpsimd.tensor_tensor(o3[:, :, lo:lo + HALF], n3[:, :, HALF - lo:DH - lo], tab, ALU.mult).then_inc(s_sw, 1)
                    if u.q:
                        if i >= 2:
                            pool.wait_ge(s_tr, i - 1)
                        gain = gains[0:R, 0, :].unsqueeze(1).broadcast_to((R, GQA, DH))
                        for k2 in range(2):
                            nc.gpsimd.tensor_tensor(plain[0:R, i % 2, :].rearrange("p (g k d) -> p k g d", g=GQA, d=DH)[:, k2],
                                                    n3[:, 4 * k2:4 * k2 + 4, :], gain, ALU.mult).then_inc(s_pl, 1)

            @block.vector
            def _(dve):
                dve.wait_ge(s_gains, 32)
                rope_tables(S, dve, s_tabs, gains, tabs, [(0, TILES, 0), (ROPE_SETS - 1, 1, TILES)])

                def first(u):
                    R, i, w_ = u.R, u.i, DH * u.heads
                    dve.wait_ge(s_sq, i + 1)
                    nc.vector.tensor_reduce(ss[0:R, i % 2, 0:u.heads], sq[0:R, 0:w_].rearrange("p (h d) -> p h d", d=DH), AX,
                                            ALU.add).then_inc(s_ss, 1)

                def second(u):
                    R, i, H = u.R, u.i, u.heads
                    w_ = DH * H
                    dve.wait_ge(s_rstd, i + 1)
                    n3 = normed[0:R, i % 2, 0:w_].rearrange("p (h d) -> p h d", d=DH)
                    dve.wait_ge(s_u, u.v + 1)
                    if u.kv:
                        dve.wait_ge(s_v, i - 9)
                    nc.vector.tensor_tensor(n3, U[u.v % 3][0:R, 0:w_].rearrange("p (h d) -> p h d", d=DH),
                                            rstd[0:R, i % 2, 0:H].unsqueeze(2).broadcast_to((R, H, DH)), ALU.mult).then_inc(s_n, 1)
                    dve.wait_ge(s_n, i + 1)
                    if u.c == 2:
                        gain = gains[0:R, 1, :].unsqueeze(1).broadcast_to((R, H, DH))
                        nc.vector.tensor_tensor(ROWS[0:R, u.t, 0:256].rearrange("p (h d) -> p h d", d=DH), n3, gain,
                                                ALU.mult).then_inc(s_rot, 1)
                        return
                    tab = tabs[0:R, 1 if u.kv else 0, 0, u.t, :].unsqueeze(1).broadcast_to((R, H, DH))
                    nc.vector.tensor_tensor(straight[0:R, 0:w_].rearrange("p (h d) -> p h d", d=DH), n3, tab, ALU.mult).then_inc(s_st, 1)
                    dve.wait_ge(s_st, u.ri + 1)
                    dve.wait_ge(s_sw, 2 * (u.ri + 1))
                    if u.q:
                        if i >= 2:
                            dve.wait_ge(s_tr, i - 1)
                        out = rot[0:R, i % 2, :].rearrange("p (g k d) -> p k g d", g=GQA, d=DH)
                        a = straight[0:R, :].rearrange("p (k g d) -> p k g d", g=GQA, d=DH)
                        b = swapped[0:R, :].rearrange("p (k g d) -> p k g d", g=GQA, d=DH)
                    else:
                        out = ROWS[0:R, u.t, 512:768] if u.c == 3 else WINR[0:R, u.t, 0:256]
                        a, b = straight[0:R, 0:256], swapped[0:R, 0:256]
                    nc.vector.tensor_tensor(out, a, b, ALU.add).then_inc(s_rot, 1)
                dve.wait_ge(s_tabs, 16)
                for i, u in enumerate(qk_units):
                    first(u)
                    if i:
                        second(qk_units[i - 1])
                second(qk_units[-1])


class Compress:

    def __init__(self, S, pfx, items, weights, pages, s_pg, landed, KC_T, VC, banks, ctx):
        def sb(name, shape):
            return ctx.enter_context(S.nc.sbuf_tensor(pfx + name, shape, F32))
        self.S, self.items, self.landed, self.KC_T, self.VC = S, items, landed, KC_T, VC
        self.turned, self.hid_bank, self.tok_bank = banks
        self.nI = len(items)
        self.last = 2 * self.nI + 3
        CH = 16 * max(items)
        self.w1, self.w2, self.pe_rows, self.peT, self.pe_hid, self.gains, self.gain = weights
        self.pages = pages
        self.chunksT = sb("chunks_turned", [P, 2, KVH, 8, CH])
        self.hid = sb("hidden", [HID, 2, KVH, CH])
        self.sq = sb("squares", [64, 256])
        self.ss, self.ms, self.rstd = (sb(n, [64, KVH]) for n in ("ss", "ms", "rstd"))
        self.kn = sb("keys", [64, 256])
        self.s_w, self.s_pg = S.lasting_sem("cmp_w"), s_pg
        names = ("tr", "hm", "hid", "w2", "sq", "ss", "ms", "rstd", "kn", "knt", "kc", "vc")
        self.m = {n: S.sem(pfx + n) for n in names}
        self.s_ev = [S.sem(pfx + "copied_by_vector"), S.sem(pfx + "copied_by_scalar")]
        self.tus = [(it, kv, j, a) for it in range(self.nI) for kv in range(2) for j in range(2) for a in range(2)]

    def blocks(self, it):
        return 16 * self.items[it] - 1

    def turn(self, pe, x):
        nc, it, kv, j, a = self.S.nc, *self.tus[x]
        if kv == 0 and j == 0 and a == 0:
            self.landed(pe, it, self.s_pg)
        if x:
            pe.wait_ge(self.s_ev[0], x)
            pe.wait_ge(self.s_ev[1], x)
        for pp in range(self.items[it]):
            src = self.pages[it % 2][:, pp, a, kv * 256 + j * P:kv * 256 + (j + 1) * P]
            ins = nc.tensor.transpose(self.turned[:, pp * P:(pp + 1) * P], src, self.S.const("ident"))
        ins.then_inc(self.m["tr"], 1)

    def hidden(self, pe, y, quarter):
        nc, m = self.S.nc, self.m
        it, kv = divmod(y, 2)
        nb = self.blocks(it)
        if quarter == 0:
            for e in range(2):
                pe.wait_ge(self.s_ev[e], 4 * (y + 1))
            if y:
                pe.wait_ge(m["hid"], y)
        for rm in range(4 * quarter, 4 * quarter + 4):
            off, mm = divmod(rm, 8)
            ins = nc.tensor.matmul(self.hid_bank[:, 0:KVH * nb], self.w1[:, kv, off, mm, :],
                                   self.chunksT[:, y % 2, :, mm, off:off + nb], start=(rm == 0), stop=(rm == 15))
        if quarter == 3:
            ins.then_inc(m["hm"], 1)

    def tokens(self, pe, y):
        nc, m = self.S.nc, self.m
        it, kv = divmod(y, 2)
        nb = self.blocks(it)
        pe.wait_ge(m["hid"], y + 1)
        if kv:
            pe.wait_ge(m["kn"], it + 1)
        elif it:
            pe.wait_ge(m["kc"], it)
        for k in range(KVH):
            ins = nc.tensor.matmul(self.tok_bank[0:nb, k * DH:(k + 1) * DH], self.hid[:, y % 2, k, 0:nb], self.w2[:, kv, :],
                                   start=True, stop=True)
        ins.then_inc(m["w2"], 1)

    def turn_keys(self, pe, it):
        nc, m = self.S.nc, self.m
        nb = self.blocks(it)
        pe.wait_ge(m["kn"], it + 1)
        pe.wait_ge(m["vc"], it + 1)
        for j in range(2):
            ins = nc.tensor.transpose(self.tok_bank[:, 256 + j * 64:256 + j * 64 + nb], self.kn[0:nb, j * P:(j + 1) * P],
                                      self.S.const("ident")[0:nb, 0:nb])
        ins.then_inc(m["knt"], 1)

    def pe_step(self, pe, y):
        nI = self.nI
        if y >= 4 and y % 2 == 0 and y // 2 - 2 < nI:
            self.turn_keys(pe, y // 2 - 2)
        for quarter in range(4):
            if 1 <= y < 2 * nI + 1:
                self.hidden(pe, y - 1, quarter)
            if y < 2 * nI:
                self.turn(pe, 4 * y + quarter)
        if 2 <= y < 2 * nI + 2:
            self.tokens(pe, y - 2)

    def copy_out(self, engine, x, k2):
        nc, it, kv, j, a = self.S.nc, *self.tus[x]
        y = 2 * it + kv
        engine.wait_ge(self.m["tr"], x + 1)
        if y >= 2:
            engine.wait_ge(self.m["hm"], y - 1)
        n = 16 * self.items[it]
        src = self.turned[k2 * DH:(k2 + 1) * DH, 0:8 * n].rearrange("p (c m) -> p m c", m=8)
        dst = self.chunksT[a * DH:(a + 1) * DH, y % 2, 2 * j + k2, :, 0:n]
        if k2 == 0:
            nc.vector.tensor_copy(dst, src).then_inc(self.s_ev[0], 1)
        else:
            nc.scalar.activation(dst, src, ACT.Copy).then_inc(self.s_ev[1], 1)

    def silu(self, act, y):
        nc, m = self.S.nc, self.m
        it, kv = divmod(y, 2)
        nb = self.blocks(it)
        act.wait_ge(m["hm"], y + 1)
        if y >= 2:
            act.wait_ge(m["w2"], y - 1)
        nc.scalar.activation(self.hid[:, y % 2, :, 0:nb], self.hid_bank[:, 0:KVH * nb].rearrange("p (k c) -> p k c", k=KVH),
                             ACT.Silu, bias=self.pe_hid[:, kv:kv + 1]).then_inc(m["hid"], 1)

    def act_finish(self, act, y):
        nc, m = self.S.nc, self.m
        it, kv = divmod(y, 2)
        nb = self.blocks(it)
        act.wait_ge(m["w2"], y + 1)
        if kv == 0:
            if it:
                act.wait_ge(m["ss"], it)
            nc.scalar.activation(self.sq[0:nb, :], self.tok_bank[0:nb, 0:256], ACT.Square).then_inc(m["sq"], 1)
        else:
            nc.scalar.activation(self.VC[0:nb, it, :], self.tok_bank[0:nb, 0:256], ACT.Copy).then_inc(m["vc"], 1)

    def act_step(self, act, y):
        nI = self.nI
        if y < 2 * nI:
            for x in range(4 * y, 4 * y + 4):
                self.copy_out(act, x, 1)
        if 1 <= y < 2 * nI + 1:
            self.silu(act, y - 1)
        if 2 <= y < 2 * nI + 2:
            self.act_finish(act, y - 2)

    def pool_program(self, pool):
        nc, m = self.S.nc, self.m
        for it in range(self.nI):
            nb = self.blocks(it)
            pool.wait_ge(m["ss"], it + 1)
            if it:
                pool.wait_ge(m["kn"], it)
            nc.gpsimd.tensor_scalar(self.ms[0:nb, :], self.ss[0:nb, :], 1.0 / DH, EPS, ALU.mult, ALU.add).then_inc(m["ms"], 1)
            pool.wait_ge(m["ms"], it + 1)
            nc.gpsimd.tensor_tensor(self.rstd[0:nb, :], self.ms[0:nb, :], self.S.const("half_power")[0:nb, 0:KVH],
                                    ALU.pow).then_inc(m["rstd"], 1)

    def keys(self, dve, it):
        nc, m = self.S.nc, self.m
        nb = self.blocks(it)
        dve.wait_ge(m["sq"], it + 1)
        if it:
            dve.wait_ge(m["rstd"], it)
        nc.vector.tensor_reduce(self.ss[0:nb, :], self.sq[0:nb, :].rearrange("p (k d) -> p k d", d=DH), AX, ALU.add).then_inc(m["ss"], 1)
        dve.wait_ge(m["rstd"], it + 1)
        if it:
            dve.wait_ge(m["knt"], it)
        nc.vector.tensor_tensor(self.kn[0:nb, :].rearrange("p (k d) -> p k d", d=DH),
                                self.tok_bank[0:nb, 0:256].rearrange("p (k d) -> p k d", d=DH),
                                self.rstd[0:nb, :].unsqueeze(2).broadcast_to((nb, KVH, DH)), ALU.mult).then_inc(m["kn"], 1)

    def keep(self, dve, it):
        nb = self.blocks(it)
        dve.wait_ge(self.m["knt"], it + 1)
        src = self.tok_bank[:, 256:256 + P].rearrange("p (j c) -> p j c", j=2)[:, :, 0:nb]
        self.S.nc.vector.tensor_scalar(self.KC_T[:, it, :, 0:nb], src, self.gain[:, 0:1], None, ALU.mult).then_inc(self.m["kc"], 1)

    def dve_step(self, dve, y):
        if y >= 4 and y % 2 == 0 and y // 2 - 2 < self.nI:
            self.keep(dve, y // 2 - 2)
        if y < 2 * self.nI:
            for x in range(4 * y, 4 * y + 4):
                self.copy_out(dve, x, 0)
        if y >= 2 and y % 2 == 0 and y // 2 - 1 < self.nI:
            self.keys(dve, y // 2 - 1)


def load_compress_weights(S, sp, weights):
    A, s_w = S.dram, S.lasting_sem("cmp_w")
    w1, w2, pe_rows, _, _, gains, _ = weights
    for kv in range(2):
        for a in range(2):
            src = A["b_cmp_w1"][0, kv].rearrange("(m a) d e -> a d m e", a=2)[a]
            sp.dma_start(w1[a * DH:(a + 1) * DH, kv, :, :, :].rearrange("p r m e -> p (r m) e"), src).then_inc(s_w, 16)
    sp.dma_start(w2[:, :, :], A["b_cmp_w2"][0].rearrange("v e d -> e v d")).then_inc(s_w, 16)
    sp.dma_start(pe_rows[:, :], A["b_cmp_pe"][0].rearrange("v (m a) d -> (v m) (a d)", a=2)).then_inc(s_w, 16)
    for i in range(2):
        sp.dma_start(gains[:, i, :], A["b_k_norm"].broadcast_to((P, DH))).then_inc(s_w, 16)


def load_cmp_pages(S, sp, n, pages, sem):
    for pg in range(NPAGES):
        page = sp.value_load(S.page_table[0:1, n * NPAGES + pg:n * NPAGES + pg + 1], min_val=0, max_val=S.n_pool - 1)
        src = S.dram["cache_nsa_paged"][0, bass.DynSlice(page, 1)].rearrange("o (p a) s h d -> (o p) a (s h d)", a=2)
        lo = 64 * (pg % 2)
        sp.dma_start(pages[lo:lo + 64, pg // 2, :, :], src[:, :, 0:512]).then_inc(sem, 16)


def attend_b_stage(S, QP, KT, ROWS, WINR, KC_P, VC_P, GATES, Z, oT, pT):
    nc = S.nc
    assert SEQ // SELB <= 16 and SEQ <= WIN
    units = []
    for t in range(TILES):
        for j in range(2):
            for k2 in range(2):
                for br in range(3):
                    for g in range(GQA):
                        u = Unit()
                        u.t, u.j, u.k2, u.br, u.g, u.v = t, j, k2, br, g, len(units)
                        u.gi = u.v // GQA
                        u.tj = u.v // (6 * GQA)
                        u.rows = NCMP_P if br == 0 else P
                        u.chunks = 1 if br == 0 else t + 1
                        u.N = NCMP_P if br == 0 else (t + 1) * P
                        units.append(u)
    N, NTJ = len(units), 2 * TILES
    LAG = 4
    with ExitStack() as ctx:
        def sb(name, shape):
            return ctx.enter_context(nc.sbuf_tensor("ab_" + name, shape, F32))
        masked = sb("masked", [P, 3, SEQ])
        probs = sb("probs", [P, 4, SEQ])
        low, den, rec = sb("low", [P, 8]), sb("den", [P, 8]), sb("rec", [P, 8])
        s_gate, s_sc, s_m, s_e, s_p, s_tr, s_pv, s_z, s_fin = (
            S.sem("ab_" + n) for n in ("gate", "scores", "masked", "exp", "weighted", "turned", "pv", "z_turned", "finished"))
        s_rec, s_zc = S.sem("ab_rec"), S.sem("ab_z_copied")
        zT = sb("z_turned", [P, 512])
        s_ev = [S.sem("ab_copied_by_vector"), S.sem("ab_copied_by_scalar")]
        SC, TR, OB, ZB = S.banks[0:3], S.banks[3:5], S.banks[5:7], S.banks[7]

        def copy_out(engine, v):
            u = units[v]
            engine.wait_ge(s_tr, v + 1)
            if u.gi >= 2:
                engine.wait_ge(s_pv, u.gi - 1)
            src = TR[v % 2][0:u.rows, 0:u.chunks * P].rearrange("p (c q) -> p c q", q=P)
            dst = pT[0:u.rows, u.gi % 2, 0:u.chunks, u.g, :]
            if v % 2 == 0:
                nc.vector.tensor_copy(dst, src).then_inc(s_ev[0], 1)
            else:
                nc.scalar.activation(dst, src, ACT.Copy).then_inc(s_ev[1], 1)

        with S.block() as block:
            @block.sync
            def _(sp):
                copy_kept(S, sp, 3, [NB - 2, NB - 1])
                for n in range(3, NB):
                    if n > 3:
                        sp.wait_ge(s_fin, n - 2)
                    copy_kept(S, sp, 2, [n])

            @block.tensor
            def _(pe):
                ident = S.const("ident")

                def scores(u):
                    part = slice(u.k2 * DH, (u.k2 + 1) * DH)
                    if u.v >= 3:
                        pe.wait_ge(s_m, u.v - 2)
                    keys = KT[part, u.br - 1, u.j, 0:u.N] if u.br else KC_P[part, 0, u.j, 0:NCMP_P]
                    nc.tensor.matmul(SC[u.v % 3][:, 0:u.N], QP[part, 1 if u.br else 0, 4 * u.j + u.g, u.t * P:(u.t + 1) * P],
                                     keys, start=True, stop=True).then_inc(s_sc, 1)

                def turn(u):
                    pe.wait_ge(s_p, u.v + 1)
                    if u.v >= 2:
                        pe.wait_ge(s_ev[u.v % 2], u.v // 2)
                    for c in range(u.chunks):
                        ins = nc.tensor.transpose(TR[u.v % 2][0:u.rows, c * P:(c + 1) * P], probs[:, u.v % 4, c * P:c * P + u.rows], ident)
                    ins.then_inc(s_tr, 1)

                def values(u):
                    for e in range(2):
                        pe.wait_ge(s_ev[e], 2 * (u.gi + 1))
                    if u.k2 == 0 and u.br == 0 and u.tj >= 2:
                        pe.wait_ge(s_fin, u.tj - 1)
                    col = slice((2 * u.j + u.k2) * DH, (2 * u.j + u.k2 + 1) * DH)
                    for c in range(u.chunks):
                        val = VC_P[0:NCMP_P, 0, col] if u.br == 0 else ROWS[:, c, 768:1024][:, col] if u.br == 1 else WINR[:, c, 256:512][:, col]
                        ins = nc.tensor.matmul(OB[u.tj % 2][u.k2 * DH:(u.k2 + 1) * DH, :], val,
                                               pT[0:u.rows, u.gi % 2, c, :, :].rearrange("p g q -> p (g q)"),
                                               start=(u.br == 0), stop=(u.br == 2 and c == u.chunks - 1))
                    ins.then_inc(s_pv, 1)

                def turn_z(tj):
                    t, j = divmod(tj, 2)
                    if tj:
                        pe.wait_ge(s_zc, tj)
                    for g in range(GQA):
                        ins = nc.tensor.transpose(ZB[:, g * P:(g + 1) * P], Z[:, t, 512 * j + g * P:512 * j + (g + 1) * P], ident)
                    ins.then_inc(s_z, 1)
                for v in range(N + LAG + 1):
                    if v < N:
                        scores(units[v])
                        if v % (6 * GQA) == 5 * GQA:
                            turn_z(units[v].tj)
                    if LAG <= v < N + LAG:
                        turn(units[v - LAG])
                    if v > LAG and (v - LAG - 1) % GQA == GQA - 1:
                        values(units[v - LAG - 1])

            @block.scalar
            def _(act):
                for v in range(N + LAG):
                    if v < N:
                        u = units[v]
                        act.wait_ge(s_m, v + 1)
                        if v >= 4:
                            act.wait_ge(s_tr, v - 3)
                        nc.scalar.activation(probs[:, v % 4, 0:u.N], masked[:, v % 3, 0:u.N], ACT.Exp, bias=low[:, v % 8:v % 8 + 1],
                                             scale=-1.0, accum_out=den[:, v % 8:v % 8 + 1]).then_inc(s_e, 1)
                    if v >= LAG and (v - LAG) % 2 == 1:
                        copy_out(act, v - LAG)
                    if v < N and v % (6 * GQA) == 6 * GQA - 1:
                        act.wait_ge(s_z, u.tj + 1)
                        if u.tj:
                            act.wait_ge(s_fin, u.tj)
                        nc.scalar.activation(zT[:, :], ZB[:, :], ACT.Copy).then_inc(s_zc, 1)

            @block.gpsimd
            def _(pool):
                pool.wait_ge(s_gate, TILES)
                for u in units:
                    h = 8 * u.j + 4 * u.k2 + u.g
                    gate = GATES[:, u.t, u.br * HB + h:u.br * HB + h + 1]
                    pool.wait_ge(s_rec, u.v + 1)
                    p = probs[:, u.v % 4, 0:u.N]
                    nc.gpsimd.tensor_scalar(p, p, rec[:, u.v % 8:u.v % 8 + 1], gate, ALU.mult, ALU.mult).then_inc(s_p, 1)

            @block.vector
            def _(dve):
                for t in range(TILES):
                    nc.vector.tensor_scalar(GATES[:, t, 0:HB], GATES[:, t, 0:HB], S.const("cmp_any")[:, t:t + 1], None,
                                            ALU.mult).then_inc(s_gate, 1)
                for v in range(N + 2 * LAG):
                    if v < N:
                        u = units[v]
                        mask = (S.const("causal")[:, (TILES - 1 - u.t) * P:] if u.br else
                                S.const("cmp_mask").rearrange("p (t c) -> p t c", t=TILES)[:, u.t, :])
                        dve.wait_ge(s_sc, v + 1)
                        if v >= 3:
                            dve.wait_ge(s_e, v - 2)
                        nc.vector.tensor_tensor_reduce(masked[:, v % 3, 0:u.N], SC[v % 3][:, 0:u.N], mask, -SCALE, 3e38,
                                                       ALU.add, ALU.min, low[:, v % 8:v % 8 + 1]).then_inc(s_m, 1)
                    if 1 <= v < N + 1:
                        i = (v - 1) % 8
                        dve.wait_ge(s_e, v)
                        nc.vector.reciprocal(rec[:, i:i + 1], den[:, i:i + 1]).then_inc(s_rec, 1)
                    if LAG <= v < N + LAG and (v - LAG) % 2 == 0:
                        copy_out(dve, v - LAG)
                    if v >= 6 * GQA + LAG + 2 and (v - LAG - 2) % (6 * GQA) == 0:
                        tj = (v - LAG - 2) // (6 * GQA) - 1
                        t, j = divmod(tj, 2)
                        dve.wait_ge(s_pv, 6 * (tj + 1))
                        dve.wait_ge(s_zc, tj + 1)
                        nc.vector.tensor_tensor(oT[:, 4 * j:4 * j + 4, t * P:(t + 1) * P], OB[tj % 2][:, :].rearrange("p (g r) -> p g r", g=GQA),
                                                zT[:, :].rearrange("p (g r) -> p g r", g=GQA), ALU.mult).then_inc(s_fin, 1)


def prepare_sample_b_stage(S, QP, KT, ROWS, WINR, Z, GATES, T, weights, pages):
    nc, A = S.nc, S.dram
    sem = {n: S.sem("pp_" + n) for n in ("zero", "q", "zt", "ztc", "rest", "gs", "gl", "pe0", "pe1", "pe2", "pre")}
    w1, _, pe_rows, peT, pe_hid, gains, gain = weights
    bank = S.banks[1]
    z_rows = Z[0:NS, TILES, :]
    with S.block() as block:
        @block.gpsimd
        def _(pool):
            nc.gpsimd.memset(T.q[:, :, :, :, :, :, :], 0.0).then_inc(sem["zero"], 1)

        @block.sync
        def _(sp):
            sp.dma_start(A["scratch_gates"], GATES[0:NS, TILES, :]).then_inc(sem["gs"], 16)
            sp.wait_ge(S.s_rows_out, 16 * (TILES + 1))
            rows = A["new_rows_p"][0, 0].rearrange("(b p a) s h d -> b p a (s h d)", a=2, p=64)
            for b in range(SEQ // PAGE):
                lo = 64 * (b % 2)
                sp.dma_start(pages[lo:lo + 64, b // 2, :, :], rows[b, :, :, 0:512]).then_inc(S.lasting_sem("cp_pages0"), 16)
            sp.wait_ge(sem["gs"], 16)
            for pair in range(NB // 2):
                for n2 in range(2):
                    r = (2 * pair + n2) * NT
                    sp.dma_start(T.gates[64 * n2:64 * n2 + 64, pair, :],
                                 A["scratch_gates"][r:r + NT].rearrange("t (b h) -> h t b", b=3),
                                 allow_slow_non_contiguous=True).then_inc(sem["gl"], 16)
            sp.wait_ge(sem["gl"], 16 * NB)

        @block.tensor
        def _(pe):
            for h in range(HB):
                ins = nc.tensor.transpose(S.banks[0][0:DH, h * NS:(h + 1) * NS], z_rows[:, h * DH:(h + 1) * DH],
                                          S.const("ident")[0:NS, 0:NS])
            ins.then_inc(sem["zt"], 1)
            ident = S.const("ident")
            pe.wait_ge(S.lasting_sem("cmp_w"), 16 * 8)
            nc.tensor.transpose(bank[:, 0:32], pe_rows[:, :], ident[0:32, 0:32])
            nc.tensor.transpose(bank[:, 128:256], gains[:, :, :].rearrange("p a d -> p (a d)"), ident).then_inc(sem["pe0"], 1)
            pe.wait_ge(sem["pe1"], 2)
            for kv in range(2):
                for rm in range(16):
                    ins = nc.tensor.matmul(bank[:, 256 + kv:257 + kv], w1[:, kv, rm // 8, rm % 8, :],
                                           peT[:, 16 * kv + rm:16 * kv + rm + 1], start=(rm == 0), stop=(rm == 15))
            ins.then_inc(sem["pe2"], 1)

        @block.scalar
        def _(act):
            nc.scalar.activation(T.kT[:, :, :, :], KT[:, :, :, SEQ:TOK], ACT.Copy)
            nc.scalar.activation(T.v[:, 0, :], ROWS[0:NS, TILES, 768:1024], ACT.Copy)
            nc.scalar.activation(T.v[:, 1, :], WINR[0:NS, TILES, 256:512], ACT.Copy).then_inc(sem["rest"], 1)
            act.wait_ge(sem["zt"], 1)
            for k2 in range(2):
                src = S.banks[0][0:DH, :].rearrange("p (j k c) -> p j k c", j=2, k=2)[:, :, k2, :]
                nc.scalar.activation(T.zT[k2 * DH:(k2 + 1) * DH, :].rearrange("p (j c) -> p j c", j=2), src,
                                     ACT.Copy).then_inc(sem["ztc"], 1)
            act.wait_ge(sem["ztc"], 2)
            act.wait_ge(sem["rest"], 1)

        @block.vector
        def _(dve):
            dve.wait_ge(sem["pe0"], 1)
            nc.vector.tensor_copy(peT[:, :], bank[:, 0:32]).then_inc(sem["pe1"], 1)
            nc.vector.tensor_copy(gain[:, :], bank[:, 128:129]).then_inc(sem["pe1"], 1)
            dve.wait_ge(sem["zero"], 1)
            n = 0
            for var in range(2):
                for j in range(2):
                    for k2 in range(2):
                        part = slice(k2 * DH, (k2 + 1) * DH)
                        for s in range(NB):
                            nc.vector.tensor_copy(T.q[part, var, s, j, k2, :, :],
                                                  QP[part, var, 4 * j:4 * j + 4, SEQ + s * NT:SEQ + (s + 1) * NT]).then_inc(sem["q"], 1)
                            n += 1
            dve.wait_ge(sem["q"], n)
            dve.wait_ge(sem["pe2"], 1)
            nc.vector.tensor_copy(pe_hid[:, :], bank[:, 256:258]).then_inc(sem["pre"], 1)
            dve.wait_ge(sem["pre"], 1)


def sample_b_stage(S, T, KC_S, VC_S, oT, weights, pages0, W_out):
    nc, A = S.nc, S.dram
    NPAIR = NB // 2
    SELW = PAST + NS
    WINW = WIN + NS
    NU = 12
    order = [u for n2 in range(2) for u in [(n2, 0, j, half) for j in range(2) for half in range(2)] + [(n2, 1, j, 0) for j in range(2)]]
    n_imp = NSEL_S - 3
    with ExitStack() as ctx:
        def sb(name, shape, dt=F32):
            return ctx.enter_context(nc.sbuf_tensor("sb_" + name, shape, dt))
        sel = sb("sel_pages", [P, 2, NPAGES, 512])
        win = sb("win_rows", [P, 2, 4, 512])
        kT = sb("keys_turned", [P, 2, 512])
        pc = sb("p_cmp", [P, 64])
        pcn = sb("p_cmp_plain", [P, 64])
        psel = sb("p_sel", [P, SELW])
        pwin = sb("p_win", [P, WINW])
        mx, low, den, rec, wt = (sb(n, [P, 3]) for n in ("max", "low", "den", "rec", "wt"))
        pcT = sb("p_cmp_turned", [64, 2, P])
        cov = sb("covered", [P, NSEL_S])
        small = sb("small", [P, 4, n_imp])
        least_imp = sb("least", [P, 2])
        bmask = sb("block_mask", [P, 16])
        out_rows = sb("out_rows", [P, P])
        pT = sb("p_turned", [P, 12, P])
        pTn = sb("p_new_turned", [NS, 2, P])
        s_sel, s_win = [S.sem("sb_sel0"), S.sem("sb_sel1")], [S.sem("sb_win0"), S.sem("sb_win1")]
        m = {n: S.sem("sb_" + n) for n in ("tr", "mul", "small", "cmpT", "cmpTc", "cov", "covc", "imp", "impc", "ecmp", "esel",
                                           "ewin", "lcmp", "lsel", "lwin", "ptr", "ptc", "pv", "o", "link", "pcmp", "psel", "pwin", "msk", "oc", "ot")}
        s_ev = [S.sem("sb_copied_by_vector"), S.sem("sb_copied_by_scalar")]
        B = S.banks

        def landed(pe, it, s_pg):
            pe.wait_ge(s_pg[it % 2], 16 * NPAGES * (it // 2 + 1))
        pages = [pages0, sb("cmp_pages", [P, 4, 2, 512])]
        s_pg = [S.sem("cs_pages0"), S.sem("cs_pages1")]
        C = Compress(S, "cs_", [4] * NB, weights, pages, s_pg, landed, KC_S, VC_S, (B[5], B[6], B[7]), ctx)
        HEAD = 7

        def interleave(phases, step):
            for y in range(HEAD):
                step(y)
            y = HEAD
            for pair in range(NPAIR):
                for i, phase in enumerate(phases):
                    phase(pair)
                    if 1 <= i <= 4 and y < C.last:
                        step(y)
                        y += 1
        ident = S.const("ident")
        new_mask = S.const("new_mask").rearrange("p (a c) -> p a c", a=NPAIR)

        with S.block() as block:
            @block.sync
            def _(sp):
                def page_rows(n, pg):
                    page = sp.value_load(S.page_table[0:1, n * NPAGES + pg:n * NPAGES + pg + 1], min_val=0, max_val=S.n_pool - 1)
                    return A["cache_nsa_paged"][0, bass.DynSlice(page, 1)]

                def load_cmp(n):
                    if n >= 2:
                        sp.wait_ge(C.m["tr"], 8 * (n - 1))
                    load_cmp_pages(S, sp, n, pages[n % 2], s_pg[n % 2])

                def load_sel(n):
                    if n >= 2:
                        sp.wait_ge(m["pv"], n // 2)
                    for pg in range(NPAGES):
                        src = page_rows(n, pg).rearrange("o r s h d -> (o r) (s h d)")
                        sp.dma_start(sel[:, n % 2, pg, :], src[:, 512:1024]).then_inc(s_sel[n % 2], 16)
                    sp.dma_start(win[:, n % 2, :, :], A["cache_nsa_win"][0, n].rearrange("(p a) s h d -> p a (s h d)", a=4)).then_inc(s_win[n % 2], 16)
                load_cmp(0)
                load_cmp(1)
                load_sel(0)
                load_sel(1)
                load_cmp(2)
                load_cmp(3)
                for pair in range(NPAIR):
                    for n in (2 * pair + 4, 2 * pair + 5):
                        if n < NB:
                            load_cmp(n)
                    for n in (2 * pair + 2, 2 * pair + 3):
                        if n < NB:
                            load_sel(n)
                sp.wait_ge(C.m["w2"], 2 * NB)
                w = A["b_w_out"][0].rearrange("(j k g d) e -> j k d g e", j=2, k=2, g=GQA)
                for j in range(2):
                    for k2 in range(2):
                        sp.dma_start(W_out[k2 * DH:(k2 + 1) * DH, 4 * j:4 * j + 4, :], w[j, k2]).then_inc(S.lasting_sem("ob_w"), 16)

            @block.tensor
            def _(pe):
                def turn(x):
                    pair, u = divmod(x, NU)
                    n2, which, j, half = order[u]
                    if u == 0:
                        pe.wait_ge(s_sel[0], 128 * (pair + 1))
                    if u == 6:
                        pe.wait_ge(s_sel[1], 128 * (pair + 1))
                    if u in (4, 10):
                        pe.wait_ge(s_win[u // 6], 16 * (pair + 1))
                    if x >= 2:
                        pe.wait_ge(s_ev[x % 2], x // 2)
                    if u == 0 and pair:
                        pe.wait_ge(m["o"], 4 * pair)
                    if u == 1:
                        for e in range(2):
                            pe.wait_ge(C.s_ev[e], 4 * min(HEAD + 4 * pair, 2 * NB))
                    for c in range(4):
                        src = win[:, n2, c, :] if which else sel[:, n2, 4 * half + c, :]
                        ins = nc.tensor.transpose(B[4 + x % 2][:, c * P:(c + 1) * P], src[:, j * P:(j + 1) * P], ident)
                    ins.then_inc(m["tr"], 1)

                def multiply(x):
                    pair, u = divmod(x, NU)
                    n2, which, j, half = order[u]
                    n = 2 * pair + n2
                    if u == 0 and pair:
                        pe.wait_ge(m["msk"], pair)
                    pe.wait_ge(s_ev[x % 2], x // 2 + 1)
                    rows = slice(64 * n2 + 32 * j, 64 * n2 + 32 * j + 32)
                    q = T.q[:, 1, n, j, :, :, :].rearrange("p k g t -> p (k g t)")
                    bank = B[2] if which else B[half]
                    nc.tensor.matmul(bank[rows, :], q, kT[:, x % 2, :], start=True, stop=True, skip_group_check=True).then_inc(m["mul"], 1)

                def small_scores(pair):
                    for n2 in range(2):
                        for j in range(2):
                            n = 2 * pair + n2
                            rows = slice(64 * n2 + 32 * j, 64 * n2 + 32 * j + 32)
                            q = T.q[:, 1, n, j, :, :, :].rearrange("p k g t -> p (k g t)")
                            qc = T.q[:, 0, n, j, :, :, :].rearrange("p k g t -> p (k g t)")
                            for which in range(2):
                                nc.tensor.matmul(B[3][rows, which * NS:(which + 1) * NS], q, T.kT[:, which, j, :], start=True,
                                                 stop=True, skip_group_check=True)
                            ins = nc.tensor.matmul(B[3][rows, 64:64 + NCMP_S], qc, KC_S[:, n, j, 0:NCMP_S], start=True, stop=True,
                                                   skip_group_check=True)
                    ins.then_inc(m["small"], 1)
                def scores(pair):
                    if pair:
                        pe.wait_ge(m["msk"], pair)
                    pe.wait_ge(C.m["kc"], 2 * pair + 2)
                    small_scores(pair)
                    for u in range(NU + 1):
                        if u < NU:
                            turn(NU * pair + u)
                        if u:
                            multiply(NU * pair + u - 1)
                        if u == 4:
                            pe.wait_ge(m["pcmp"], 2 * pair + 2)
                            nc.tensor.transpose(B[3][0:NCMP_S, 128:256], pcn[:, 0:NCMP_S], ident)
                            nc.tensor.transpose(B[3][0:NCMP_S, 256:384], pc[:, 0:NCMP_S], ident).then_inc(m["cmpT"], 1)
                        if u == 6:
                            pe.wait_ge(m["cmpTc"], pair + 1)
                            nc.tensor.matmul(B[3][:, 384:384 + NSEL_S], pcT[0:NCMP_S, 0, :], S.const("cover")[0:NCMP_S, :],
                                             start=True, stop=True).then_inc(m["cov"], 1)
                        if u == 8:
                            pe.wait_ge(m["covc"], pair + 1)
                            nc.tensor.matmul(B[3][:, 416:416 + NSEL_S], S.const("group_sum"), cov[:, :], start=True,
                                             stop=True).then_inc(m["imp"], 1)

                def turns(pair):
                    pe.wait_ge(m["psel"], pair + 1)
                    for c in range(8):
                        nc.tensor.transpose(B[c // 4][:, (c % 4) * P:(c % 4 + 1) * P], psel[:, c * P:(c + 1) * P], ident)
                    pe.wait_ge(m["pwin"], pair + 1)
                    nc.tensor.transpose(B[3][0:NS, 128:256], psel[:, PAST:], ident)
                    nc.tensor.transpose(B[3][0:NS, 256:384], pwin[:, WIN:], ident)
                    for c in range(4):
                        ins = nc.tensor.transpose(B[2][:, c * P:(c + 1) * P], pwin[:, c * P:(c + 1) * P], ident)
                    ins.then_inc(m["ptr"], 1)

                def output(pair):
                    pe.wait_ge(m["ptc"], 4 * (pair + 1))
                    pe.wait_ge(C.m["vc"], 2 * pair + 2)
                    for e in range(2):
                        pe.wait_ge(s_ev[e], NU // 2 * (pair + 1))
                    for n2 in range(2):
                        n = 2 * pair + n2
                        for j in range(2):
                            cols = slice(64 * n2 + 32 * j, 64 * n2 + 32 * j + 32)
                            vcol = slice(j * P, (j + 1) * P)
                            prods = [(VC_S[0:NCMP_S, n, vcol], pcT[0:NCMP_S, 1, cols])]
                            prods += [(sel[:, n2, c, 256 + j * P:256 + (j + 1) * P], pT[:, c, cols]) for c in range(8)]
                            prods += [(win[:, n2, c, 256 + j * P:256 + (j + 1) * P], pT[:, 8 + c, cols]) for c in range(4)]
                            prods += [(T.v[:, which, vcol], pTn[:, which, cols]) for which in range(2)]
                            for i, (v, p) in enumerate(prods):
                                ins = nc.tensor.matmul(B[4][cols, 0:P], p, v, start=(i == 0), stop=(i == len(prods) - 1),
                                                       skip_group_check=True)
                    ins.then_inc(m["pv"], 1)

                def merge(pair):
                    pe.wait_ge(m["oc"], pair + 1)
                    nc.tensor.transpose(B[4][:, P:2 * P], out_rows[:, :], ident).then_inc(m["ot"], 1)
                interleave((scores, lambda pair: None, lambda pair: None, turns, output, merge), lambda y: C.pe_step(pe, y))

            def evacuate(engine, x):
                engine.wait_ge(m["tr"], x + 1)
                if x >= 2:
                    engine.wait_ge(m["mul"], x - 1)
                if x % 2 == 0:
                    nc.vector.tensor_copy(kT[:, 0, :], B[4][:, :]).then_inc(s_ev[0], 1)
                else:
                    nc.scalar.activation(kT[:, 1, :], B[5][:, :], ACT.Copy).then_inc(s_ev[1], 1)

            @block.scalar
            def _(act):
                def scores(pair):
                    act.wait_ge(m["lcmp"], pair + 1)
                    if pair:
                        act.wait_ge(m["ptr"], pair)
                    nc.scalar.activation(pc[:, 0:NCMP_S], B[3][:, 64:64 + NCMP_S], ACT.Exp, bias=low[:, 0:1], scale=SCALE,
                                         accum_out=den[:, 0:1]).then_inc(m["ecmp"], 1)
                    for u in range(1, NU, 2):
                        evacuate(act, NU * pair + u)

                def least(pair):
                    act.wait_ge(m["lsel"], pair + 1)
                    nc.scalar.activation(psel[:, :], psel[:, :], ACT.Exp, bias=low[:, 1:2], scale=SCALE,
                                         accum_out=den[:, 1:2]).then_inc(m["esel"], 1)
                    act.wait_ge(m["lwin"], pair + 1)
                    nc.scalar.activation(pwin[:, :], pwin[:, :], ACT.Exp, bias=low[:, 2:3], scale=SCALE,
                                         accum_out=den[:, 2:3]).then_inc(m["ewin"], 1)

                def turns(pair):
                    act.wait_ge(m["ptr"], pair + 1)
                    if pair:
                        act.wait_ge(m["pv"], pair)
                    nc.scalar.activation(pT[:, 4:8, :], B[1][:, :].rearrange("p (c r) -> p c r", c=4), ACT.Copy).then_inc(m["ptc"], 1)
                    nc.scalar.activation(pT[:, 8:12, :], B[2][:, :].rearrange("p (c r) -> p c r", c=4), ACT.Copy).then_inc(m["ptc"], 1)
                interleave((scores, least, lambda pair: None, turns, lambda pair: None), lambda y: C.act_step(act, y))

            @block.gpsimd
            def _(pool):
                C.pool_program(pool)

            @block.vector
            def _(dve):
                link = linker(dve, m["link"])
                link(nc.vector.memset(bmask[:, :], 0.0))

                def lowest(src, i, sem):
                    link(nc.vector.tensor_reduce(mx[:, i:i + 1], src, AX, ALU.max))
                    nc.vector.tensor_scalar(low[:, i:i + 1], mx[:, i:i + 1], -SCALE, None, ALU.mult).then_inc(sem, 1)

                def weigh(pair, i):
                    link(nc.vector.reciprocal(rec[:, i:i + 1], den[:, i:i + 1]))
                    link(nc.vector.tensor_tensor(wt[:, i:i + 1], rec[:, i:i + 1], T.gates[:, pair, i:i + 1], ALU.mult))
                def scores(pair):
                    dve.wait_ge(m["small"], pair + 1)
                    lowest(B[3][:, 64:64 + NCMP_S], 0, m["lcmp"])
                    dve.wait_ge(m["ecmp"], pair + 1)
                    weigh(pair, 0)
                    if pair:
                        dve.wait_ge(m["pv"], pair)
                    nc.vector.tensor_scalar(pcn[:, 0:NCMP_S], pc[:, 0:NCMP_S], rec[:, 0:1], None, ALU.mult).then_inc(m["pcmp"], 1)
                    nc.vector.tensor_scalar(pc[:, 0:NCMP_S], pc[:, 0:NCMP_S], wt[:, 0:1], None, ALU.mult).then_inc(m["pcmp"], 1)
                    for u in range(0, NU, 2):
                        evacuate(dve, NU * pair + u)
                        if u == 4:
                            dve.wait_ge(m["cmpT"], pair + 1)
                            nc.vector.tensor_copy(pcT[0:NCMP_S, :, :], B[3][0:NCMP_S, 128:384].rearrange("p (a r) -> p a r", a=2)
                                                  ).then_inc(m["cmpTc"], 1)
                        if u == 6:
                            dve.wait_ge(m["cov"], pair + 1)
                            nc.vector.tensor_copy(cov[:, :], B[3][:, 384:384 + NSEL_S]).then_inc(m["covc"], 1)
                        if u == 8:
                            dve.wait_ge(m["imp"], pair + 1)
                            ids = S.const("block_id")
                            link(nc.vector.tensor_copy(small[:, 0, :], B[3][:, 417:417 + n_imp]))
                            link(nc.vector.tensor_reduce(least_imp[:, 0:1], small[:, 0, :], AX, ALU.min))
                            link(nc.vector.scalar_tensor_tensor(out=small[:, 1, :], in0=small[:, 0, :], scalar=least_imp[:, 0:1],
                                                                in1=ids, op0=ALU.is_equal, op1=ALU.mult))
                            link(nc.vector.tensor_reduce(least_imp[:, 1:2], small[:, 1, :], AX, ALU.max))
                            link(nc.vector.tensor_scalar(bmask[:, 1:1 + n_imp], ids, least_imp[:, 1:2], NEG, ALU.is_equal, ALU.mult))

                def least(pair):
                    dve.wait_ge(m["mul"], NU * (pair + 1))
                    for half in range(2):
                        link(nc.vector.tensor_tensor(psel[:, half * 512:(half + 1) * 512].rearrange("p (b k) -> p b k", k=SELB),
                                                     B[half][:, :].rearrange("p (b k) -> p b k", k=SELB),
                                                     bmask[:, 8 * half:8 * half + 8].unsqueeze(2).broadcast_to((P, 8, SELB)), ALU.add))
                    link(nc.vector.tensor_tensor(psel[:, PAST:], B[3][:, 0:NS], new_mask[:, pair, :], ALU.add))
                    lowest(psel[:, :], 1, m["lsel"])
                    link(nc.vector.tensor_tensor(pwin[:, 0:WIN], B[2][:, :], S.const("win_mask"), ALU.add))
                    link(nc.vector.tensor_tensor(pwin[:, WIN:], B[3][:, NS:2 * NS], new_mask[:, pair, :], ALU.add))
                    lowest(pwin[:, :], 2, m["lwin"])

                def weights(pair):
                    dve.wait_ge(m["lwin"], pair + 1)
                    dve.wait_ge(m["esel"], pair + 1)
                    weigh(pair, 1)
                    nc.vector.tensor_scalar(psel[:, :], psel[:, :], wt[:, 1:2], None, ALU.mult).then_inc(m["psel"], 1)
                    dve.wait_ge(m["ewin"], pair + 1)
                    weigh(pair, 2)
                    nc.vector.tensor_scalar(pwin[:, :], pwin[:, :], wt[:, 2:3], None, ALU.mult).then_inc(m["pwin"], 1)

                def turns(pair):
                    dve.wait_ge(m["ptr"], pair + 1)
                    if pair:
                        dve.wait_ge(m["pv"], pair)
                    nc.vector.tensor_copy(pT[:, 0:4, :], B[0][:, :].rearrange("p (c r) -> p c r", c=4)).then_inc(m["ptc"], 1)
                    nc.vector.tensor_copy(pTn[:, :, :], B[3][0:NS, 128:384].rearrange("p (a r) -> p a r", a=2)).then_inc(m["ptc"], 1)
                    dve.wait_ge(m["ptc"], 4 * (pair + 1))
                    nc.vector.memset(least_imp[:, 0:1], 0.0).then_inc(m["msk"], 1)

                def output(pair):
                    dve.wait_ge(m["msk"], pair + 1)
                    dve.wait_ge(m["pv"], pair + 1)
                    nc.vector.tensor_copy(out_rows[:, :], B[4][:, 0:P]).then_inc(m["oc"], 1)

                def merge(pair):
                    dve.wait_ge(m["ot"], pair + 1)
                    src = B[4][:, P:2 * P].rearrange("p (n j k g t) -> p n j k g t", n=2, j=2, k=2, g=GQA)
                    for j in range(2):
                        for k2 in range(2):
                            part = slice(k2 * DH, (k2 + 1) * DH)
                            cols = slice(SEQ + 2 * pair * NT, SEQ + 2 * (pair + 1) * NT)
                            out = oT[part, 4 * j:4 * j + 4, cols].rearrange("p g (n t) -> p n g t", n=2)
                            z = T.zT[part, :].rearrange("p (j g r) -> p j g r", j=2, g=GQA)[:, j, :, 2 * pair * NT:2 * (pair + 1) * NT]
                            nc.vector.tensor_tensor(out, src[part, :, j, k2, :, :], z.rearrange("p g (n t) -> p n g t", n=2),
                                                    ALU.mult).then_inc(m["o"], 1)
                interleave((scores, least, weights, turns, output, merge), lambda y: C.dve_step(dve, y))


def compress_prompt_stage(S, KC_P, VC_P, weights, pages):
    s_pg = [S.lasting_sem("cp_pages0")]

    def landed(pe, it, s_pg):
        pe.wait_ge(s_pg[0], 16 * (SEQ // PAGE))
    with ExitStack() as ctx:
        C = Compress(S, "cp_", [2], weights, [pages], s_pg, landed, KC_P, VC_P, (S.banks[0], S.banks[1], S.banks[2]), ctx)
        with S.block() as block:
            @block.tensor
            def _(pe):
                for y in range(C.last):
                    C.pe_step(pe, y)

            @block.scalar
            def _(act):
                for y in range(C.last):
                    C.act_step(act, y)

            @block.gpsimd
            def _(pool):
                C.pool_program(pool)

            @block.vector
            def _(dve):
                for y in range(C.last):
                    C.dve_step(dve, y)


def layer_b(S):
    nc, A = S.nc, S.dram
    with ExitStack() as ctx:
        def sb(name, shape, c=ctx):
            return c.enter_context(nc.sbuf_tensor("lb_" + name, shape, F32))
        oT = sb("oT", [P, KC, TOK])
        region = sb("region", [P, 2 * KC * 512])
        W_in = region[:, :].rearrange("p (c k e) -> p c k e", c=2, k=KC)
        w1 = region[:, 0:KC * 512].rearrange("p (v r m e) -> p v r m e", v=2, r=2, m=8)
        pages0 = region[:, KC * 512:].rearrange("p (b a e) -> p b a e", b=4, a=2)
        pT = region[:, KC * 512:].rearrange("p (i c g q) -> p i c g q", i=2, c=TILES, g=GQA)
        W_out = region[:, :].rearrange("p (k e) -> p k e", k=KC)
        weights = (w1, sb("w2", [HID, 2, DH]), sb("pe_rows", [2 * CSTRIDE, P]), sb("peT", [P, 2 * CSTRIDE]),
                   sb("pe_hidden", [HID, 2]), sb("k_gains", [P, 2, DH]), sb("k_gain", [P, 1]))
        T = Unit()
        T.q = sb("s_q", [P, 2, NB, 2, 2, GQA, NT])
        T.kT = sb("s_kT", [P, 2, 2, NS])
        T.v = sb("s_v", [NS, 2, 256])
        T.zT = sb("s_zT", [P, 2 * GQA * NS])
        T.gates = sb("s_gates", [P, NB // 2, 3])
        with ExitStack() as inner:
            KT = sb("kT", [P, 2, 2, TOK], inner)
            ROWS = sb("rows", [P, TILES + 1, 1024], inner)
            WINR = sb("win", [P, TILES + 1, 512], inner)
            Z = sb("z", [P, TILES + 1, D], inner)
            GATES = sb("gates", [P, TILES + 1, 3 * HB], inner)
            QP = sb("qp", [P, 2, 8, TOK], inner)

            def first_weights(sp):
                w = A["b_w_in"][0].rearrange("(k p) e -> p k e", p=P)
                for c in range(2):
                    sp.dma_start(W_in[:, c, :, :], w[:, :, c * 512:(c + 1) * 512]).then_inc(S.lasting_sem(f"pb_w{c}"), 16)
            norm_stage(S, "nb_", lambda e, t: None, A["b_norm"], oT, first_weights)
            project_b_stage(S, oT, W_in, QP, KT, ROWS, WINR, Z, GATES, weights)
            prepare_sample_b_stage(S, QP, KT, ROWS, WINR, Z, GATES, T, weights, pages0)
            KC_P = sb("kc_p", [P, 1, 2, 64], inner)
            VC_P = sb("vc_p", [64, 1, 256], inner)
            compress_prompt_stage(S, KC_P, VC_P, weights, pages0)
            attend_b_stage(S, QP, KT, ROWS, WINR, KC_P, VC_P, GATES, Z, oT, pT)
        KC_S = sb("kc_s", [P, NB, 2, 64])
        VC_S = sb("vc_s", [64, NB, 256])
        sample_b_stage(S, T, KC_S, VC_S, oT, weights, pages0, W_out)
        output_stage(S, "ob_", oT, W_out, 64, KC,
                     lambda t: A["y_p"][0, t * P:(t + 1) * P, :] if t < TILES else A["y_s"].rearrange("n t d -> (n t) d"))


def finish_stage(S):
    with S.nc.Block() as block:
        @block.sync
        def _(sp):
            for sem, value in S.outs + [(S.s_copy, S.n_copy)]:
                if value:
                    sp.wait_ge(sem, value)


def program(nc, dram, where, n_const):
    with ExitStack() as ctx:
        S = Stage(nc, dram, where, ctx)
        S.consts = ctx.enter_context(nc.sbuf_tensor("consts", [P, n_const], F32))
        S.x = ctx.enter_context(nc.sbuf_tensor("x", [P, TILES + 1, D], F32))
        S.page_table = ctx.enter_context(nc.sbuf_tensor("page_table", [1, NB * NPAGES], I32))
        S.n_pool = dram["cache_nsa_paged"].shape[1]
        S.banks = [ctx.enter_context(nc.psum_tensor(f"bank{i}", [P, 512], F32)) for i in range(8)]
        load_stage(S)
        layer_a(S)
        layer_b(S)
        finish_stage(S)


_INS = ["x_prompt", "x_sample", "cache_dil_0", "cache_dil_1", "cache_dil_2", "cache_nsa_paged", "cache_nsa_win", "page_table",
        "a_norm", "a_w_in", "a_q_norm", "a_k_norm", "a_w_out", "b_norm", "b_w_in", "b_q_norm", "b_k_norm", "b_cmp_pe",
        "b_cmp_w1", "b_cmp_w2", "b_w_out"]
_OUTS = [("y_p", (1, SEQ, D)), ("y_s", (NB, NT, D)),
         ("new_dil_0_p", (1, 1, 128, 2, HA, DH)), ("new_dil_1_p", (1, 1, 512, 2, HA, DH)), ("new_dil_2_p", (1, 1, 512, 2, HA, DH)),
         ("new_rows_p", (1, 1, SEQ, 4, KVH, DH)), ("new_win_p", (1, 1, SEQ, 2, KVH, DH)),
         ("new_dil_0_s", (1, NB, 128, 2, HA, DH)), ("new_dil_1_s", (1, NB, 512, 2, HA, DH)),
         ("new_dil_2_s", (1, NB, PAST + NT, 2, HA, DH)),
         ("new_rows_s", (1, NB, NT, 4, KVH, DH)), ("new_win_s", (1, NB, WIN, 2, KVH, DH))]


def kernel(**inputs):
    import numpy as _np
    import concourse.bacc as _bacc
    from concourse import mybir as _mybir
    from concourse.bass_utils import run_bass_kernel_spmd as _run

    nc = _bacc.Bacc("TRN2", target_bir_lowering=False, num_devices=1)
    arrays, dram = {}, {}
    table, where = constants()
    for name in _INS + ["consts"]:
        a = table if name == "consts" else _np.ascontiguousarray(inputs[name])
        arrays[f"in_{name}"] = a
        dram[name] = nc.dram_tensor(f"in_{name}", a.shape, _mybir.dt.from_np(a.dtype), kind="ExternalInput").ap()
    for name, shape in _OUTS:
        dram[name] = nc.dram_tensor(f"out_{name}", shape, _mybir.dt.float32, kind="ExternalOutput").ap()
    dram["scratch_gates"] = nc.dram_tensor("scratch_gates", (NS, 3 * HB), _mybir.dt.float32, kind="Internal").ap()
    program(nc, dram, where, where["a_mask"][0])
    r = _run(nc, [arrays], core_ids=[0])
    return tuple(r.results[0][f"out_{name}"] for name, _ in _OUTS)
```
